# Optimizing a Trainium2 kernel written in Bass

```python
import jax, jax.numpy as jnp
from jax import lax
import numpy as np

D_MODEL = 1024
BATCH = 1
SEQ = 1024
DEPTH = 1

CHUNK = 64
D_MIX = D_MODEL
M_HEADS = 4
M_HEAD_DIM = (D_MIX // 2) // M_HEADS
M_WIDTH = M_HEADS * M_HEAD_DIM
CONV_K = 4
A_HEADS = 8
A_KV_HEADS = 2
A_GROUP = A_HEADS // A_KV_HEADS
A_HEAD_DIM = (D_MIX - M_WIDTH) // A_HEADS
A_WIDTH = A_HEADS * A_HEAD_DIM
A_KV_WIDTH = A_KV_HEADS * A_HEAD_DIM
WINDOW = 128
WINDOW_CHUNKS = WINDOW // CHUNK
ROPE_THETA = 500000.0
ROPE_DIM = A_HEAD_DIM // 4
D_FF = 2816
EPS = 1e-6
IN_SIZES = [2 * M_WIDTH, M_WIDTH, M_WIDTH, M_HEADS, M_HEADS, A_WIDTH, A_KV_WIDTH, A_KV_WIDTH]
IN_DIM = sum(IN_SIZES)
IN_SPLITS = [int(s) for s in np.cumsum(IN_SIZES)[:-1]]

kernel_name = "hymba_mlstm_swa_sink_macaron"

def rms_norm(x, w):
    xf = x.astype(jnp.float32)
    y = xf * lax.rsqrt(jnp.mean(xf * xf, axis=-1, keepdims=True) + EPS)
    return (y * w.astype(jnp.float32)).astype(x.dtype)

def head_layer_norm(h, w):
    mu = jnp.mean(h, axis=-1, keepdims=True)
    hc = h - mu
    var = jnp.mean(hc * hc, axis=-1, keepdims=True)
    return hc * lax.rsqrt(var + EPS) * w.astype(jnp.float32)

def swiglu(x, w_gate, w_up, w_down):
    return (jax.nn.silu(x @ w_gate) * (x @ w_up)) @ w_down

def causal_depthwise_conv(u, w, bias):
    k = w.shape[0]
    s = u.shape[1]
    up = jnp.pad(u, ((0, 0), (k - 1, 0), (0, 0)))
    out = up[:, 0:s] * w[0]
    for j in range(1, k):
        out = out + up[:, j:j + s] * w[j]
    return out + bias

def partial_rope(t, pos):
    half = ROPE_DIM // 2
    inv_freq = ROPE_THETA ** (-jnp.arange(half, dtype=jnp.float32) / half)
    ang = pos.astype(jnp.float32)[..., None] * inv_freq
    cos = jnp.cos(ang)[:, :, None, :]
    sin = jnp.sin(ang)[:, :, None, :]
    tr = t[..., :ROPE_DIM].astype(jnp.float32)
    x1, x2 = tr[..., :half], tr[..., half:]
    rot = jnp.concatenate([x1 * cos - x2 * sin, x2 * cos + x1 * sin], axis=-1).astype(t.dtype)
    return jnp.concatenate([rot, t[..., ROPE_DIM:]], axis=-1)

def banded_chunks(t):
    nc = t.shape[1]
    tp = jnp.pad(t, ((0, 0), (WINDOW_CHUNKS - 1, 0), (0, 0), (0, 0), (0, 0)))
    return jnp.concatenate([tp[:, j:j + nc] for j in range(WINDOW_CHUNKS)], axis=2)

def swa_sink_attention(q, k, v, sinks):
    b, s = q.shape[0], q.shape[1]
    nc = s // CHUNK
    qb = q.reshape(b, nc, CHUNK, A_KV_HEADS, A_GROUP, A_HEAD_DIM)
    kb = banded_chunks(k.reshape(b, nc, CHUNK, A_KV_HEADS, A_HEAD_DIM))
    vb = banded_chunks(v.reshape(b, nc, CHUNK, A_KV_HEADS, A_HEAD_DIM))
    logits = jnp.einsum('bcqkgd,bcskd->bckgqs', qb, kb).astype(jnp.float32) * (A_HEAD_DIM ** -0.5)
    src_chunk = (jnp.arange(nc)[:, None] - (WINDOW_CHUNKS - 1)
                 + jnp.arange(WINDOW_CHUNKS * CHUNK)[None, :] // CHUNK)
    valid = src_chunk >= 0
    logits = jnp.where(valid[None, :, None, None, None, :], logits, -jnp.inf)
    sink = sinks.astype(jnp.float32).reshape(A_KV_HEADS, A_GROUP)[None, None, :, :, None, None]
    sink = jnp.broadcast_to(sink, logits.shape[:-1] + (1,))
    probs = jax.nn.softmax(jnp.concatenate([logits, sink], axis=-1), axis=-1)[..., :-1]
    out = jnp.einsum('bckgqs,bcskd->bcqkgd', probs.astype(v.dtype), vb)
    return out.reshape(b, s, A_WIDTH)

def mlstm_chunkwise(q, k, v, i_pre, f_pre):
    f32 = jnp.float32
    b, s, h, d = q.shape
    nc, ln = s // CHUNK, CHUNK

    def to_chunks(t):
        return t.astype(f32).reshape(b, nc, ln, h, -1).transpose(0, 3, 1, 2, 4)

    qc = to_chunks(q)
    kc = to_chunks(k) * (d ** -0.5)
    vc = to_chunks(v)
    li = i_pre.astype(f32).reshape(b, nc, ln, h).transpose(0, 3, 1, 2)
    lf = jax.nn.log_sigmoid(f_pre.astype(f32)).reshape(b, nc, ln, h).transpose(0, 3, 1, 2)
    cum_f = jnp.cumsum(lf, axis=-1)
    cum_f_last = cum_f[..., -1]
    causal = jnp.tril(jnp.ones((ln, ln), dtype=bool))
    dlog = jnp.where(causal, cum_f[..., :, None] - cum_f[..., None, :] + li[..., None, :], -jnp.inf)

    a = cum_f_last[..., None] - cum_f + li
    a_max = jnp.max(a, axis=-1)
    w_a = jnp.exp(a - a_max[..., None])
    c_chunk = jnp.einsum('bhcs,bhcsk,bhcsv->bhckv', w_a, kc, vc)
    n_chunk = jnp.einsum('bhcs,bhcsk->bhck', w_a, kc)

    def step(carry, inp):
        c_st, n_st, m_st = carry
        f_tot, amax_c, cc, nn = inp
        m_new = jnp.maximum(f_tot + m_st, amax_c)
        dec = jnp.exp(f_tot + m_st - m_new)
        add = jnp.exp(amax_c - m_new)
        c_new = dec[..., None, None] * c_st + add[..., None, None] * cc
        n_new = dec[..., None] * n_st + add[..., None] * nn
        return (c_new, n_new, m_new), (c_st, n_st, m_st)

    init = (jnp.zeros((b, h, d, d), f32), jnp.zeros((b, h, d), f32), jnp.zeros((b, h), f32))
    xs = (jnp.moveaxis(cum_f_last, 2, 0), jnp.moveaxis(a_max, 2, 0),
          jnp.moveaxis(c_chunk, 2, 0), jnp.moveaxis(n_chunk, 2, 0))
    _, (c_prev, n_prev, m_prev) = lax.scan(step, init, xs)
    c_prev = jnp.moveaxis(c_prev, 0, 2)
    n_prev = jnp.moveaxis(n_prev, 0, 2)
    m_prev = jnp.moveaxis(m_prev, 0, 2)

    g = cum_f + m_prev[..., None]
    m_t = jnp.maximum(jnp.max(dlog, axis=-1), g)
    sc = jnp.einsum('bhcld,bhcsd->bhcls', qc, kc) * jnp.exp(dlog - m_t[..., None])
    w_g = jnp.exp(g - m_t)
    num = (jnp.einsum('bhcls,bhcsv->bhclv', sc, vc)
           + w_g[..., None] * jnp.einsum('bhcld,bhcdv->bhclv', qc, c_prev))
    den = jnp.sum(sc, axis=-1) + w_g * jnp.einsum('bhcld,bhcd->bhcl', qc, n_prev)
    out = num / jnp.maximum(jnp.abs(den), jnp.exp(-m_t))[..., None]
    return out.transpose(0, 2, 3, 1, 4).reshape(b, s, h, d)

def token_mixer(u, positions, w_in, conv_w, conv_b, b_igate, b_fgate, mlstm_norm_w, sinks, w_out):
    bsz, s, _ = u.shape
    proj = u @ w_in
    m_qk, m_v, m_o, m_i, m_f, a_q, a_k, a_v = jnp.split(proj, IN_SPLITS, axis=-1)
    m_qk = jax.nn.silu(causal_depthwise_conv(m_qk, conv_w, conv_b))
    m_q, m_k = jnp.split(m_qk, 2, axis=-1)
    hm = mlstm_chunkwise(m_q.reshape(bsz, s, M_HEADS, M_HEAD_DIM),
                         m_k.reshape(bsz, s, M_HEADS, M_HEAD_DIM),
                         m_v.reshape(bsz, s, M_HEADS, M_HEAD_DIM),
                         m_i + b_igate, m_f + b_fgate)
    hm = head_layer_norm(hm, mlstm_norm_w).reshape(bsz, s, M_WIDTH)
    hm = (jax.nn.sigmoid(m_o.astype(jnp.float32)) * hm).astype(u.dtype)
    qa = partial_rope(a_q.reshape(bsz, s, A_HEADS, A_HEAD_DIM), positions)
    ka = partial_rope(a_k.reshape(bsz, s, A_KV_HEADS, A_HEAD_DIM), positions)
    va = a_v.reshape(bsz, s, A_KV_HEADS, A_HEAD_DIM)
    ha = swa_sink_attention(qa, ka, va, sinks)
    return jnp.concatenate([hm, ha], axis=-1) @ w_out

def setup_inputs(seed: int = 0) -> dict:
    key = jax.random.key(seed)
    ks = jax.random.split(key, 32)
    f32 = jnp.float32

    def nrm(k, shape, scale):
        return jax.random.normal(k, shape, f32) * scale

    def gain(k, shape):
        return 1.0 + 0.05 * jax.random.normal(k, shape, f32)

    x = jax.random.normal(ks[0], (BATCH, SEQ, D_MODEL), f32)
    offset = jax.random.randint(ks[1], (BATCH, 1), 0, 4096, dtype=jnp.int32)
    positions = (jnp.arange(SEQ, dtype=jnp.int32)[None, :] + offset).astype(jnp.int32)
    L = DEPTH
    return {
        "x": x,
        "positions": positions,
        "ff1_pre_w": gain(ks[2], (L, D_MODEL)),
        "ff1_w_gate": nrm(ks[3], (L, D_MODEL, D_FF), D_MODEL ** -0.5),
        "ff1_w_up": nrm(ks[4], (L, D_MODEL, D_FF), D_MODEL ** -0.5),
        "ff1_w_down": nrm(ks[5], (L, D_FF, D_MODEL), D_FF ** -0.5),
        "ff1_post_w": gain(ks[6], (L, D_MODEL)),
        "mix_pre_w": gain(ks[7], (L, D_MODEL)),
        "w_in": nrm(ks[8], (L, D_MODEL, IN_DIM), D_MODEL ** -0.5),
        "conv_w": nrm(ks[9], (L, CONV_K, 2 * M_WIDTH), CONV_K ** -0.5),
        "conv_b": nrm(ks[10], (L, 2 * M_WIDTH), 0.02),
        "b_igate": nrm(ks[11], (L, M_HEADS), 0.1),
        "b_fgate": jnp.linspace(3.0, 6.0, M_HEADS, dtype=f32)[None, :] + nrm(ks[12], (L, M_HEADS), 0.1),
        "mlstm_norm_w": gain(ks[13], (L, M_HEADS, M_HEAD_DIM)),
        "sinks": nrm(ks[14], (L, A_HEADS), 0.5),
        "w_out": nrm(ks[15], (L, D_MIX, D_MODEL), D_MIX ** -0.5),
        "mix_post_w": gain(ks[16], (L, D_MODEL)),
        "ff2_pre_w": gain(ks[17], (L, D_MODEL)),
        "ff2_w_gate": nrm(ks[18], (L, D_MODEL, D_FF), D_MODEL ** -0.5),
        "ff2_w_up": nrm(ks[19], (L, D_MODEL, D_FF), D_MODEL ** -0.5),
        "ff2_w_down": nrm(ks[20], (L, D_FF, D_MODEL), D_FF ** -0.5),
        "ff2_post_w": gain(ks[21], (L, D_MODEL)),
    }

def reference(x, positions, ff1_pre_w, ff1_w_gate, ff1_w_up, ff1_w_down, ff1_post_w,
              mix_pre_w, w_in, conv_w, conv_b, b_igate, b_fgate, mlstm_norm_w, sinks, w_out,
              mix_post_w, ff2_pre_w, ff2_w_gate, ff2_w_up, ff2_w_down, ff2_post_w):
    h = x
    for l in range(DEPTH):
        y = swiglu(rms_norm(h, ff1_pre_w[l]), ff1_w_gate[l], ff1_w_up[l], ff1_w_down[l])
        h = h + 0.5 * rms_norm(y, ff1_post_w[l])
        y = token_mixer(rms_norm(h, mix_pre_w[l]), positions, w_in[l], conv_w[l], conv_b[l],
                        b_igate[l], b_fgate[l], mlstm_norm_w[l], sinks[l], w_out[l])
        h = h + rms_norm(y, mix_post_w[l])
        y = swiglu(rms_norm(h, ff2_pre_w[l]), ff2_w_gate[l], ff2_w_up[l], ff2_w_down[l])
        h = h + 0.5 * rms_norm(y, ff2_post_w[l])
    return h


_drawn_inputs = setup_inputs


def setup_inputs(seed=0):
    import zlib

    import numpy as np

    out = dict(_drawn_inputs(seed))
    spreads = {}
    factors = {'conv_b': 5.249, 'b_igate': 8.0, 'sinks': 8.0, 'ff2_post_w': 3.461}
    for name, (base, spread) in spreads.items():
        noise = np.random.default_rng([zlib.crc32(name.encode()), seed]).standard_normal(out[name].shape)
        drawn = base * np.exp(spread * noise) if base else spread * noise
        out[name] = __import__('jax').numpy.asarray(drawn.astype(out[name].dtype))
    for name, factor in factors.items():
        out[name] = (out[name] * factor).astype(out[name].dtype)
    return out
```

```python
from contextlib import ExitStack

import concourse.bass as bass
import numpy as np
from concourse import mybir

P = 128
F32 = mybir.dt.float32
FR = mybir.dt.float32r
BF = mybir.dt.bfloat16
I32 = mybir.dt.int32
ALU = mybir.AluOpType
ACT = mybir.ActivationFunctionType
AX = mybir.AxisListType.X
BANK = 512
KB = 1024
EPS = 1e-6


class Memory:

    def __init__(self, nc, ctx):
        self.nc, self.ctx = nc, ctx
        self.base = (nc.sbuf_base + 31) // 32 * 32

    def at(self, name, shape, dtype, offset):
        return self.nc.alloc_sbuf_tensor_at(name, shape, dtype, offset=self.base + offset)

    def sem(self, name):
        return self.ctx.enter_context(self.nc.semaphore(name))


class Chain:

    def __init__(self, mem, name):
        self.sem, self.count = mem.sem(name), 0

    def then(self, engine, instruction):
        instruction.then_inc(self.sem, 1)
        self.count += 1
        engine.wait_ge(self.sem, self.count)


def inverse_root(dve, chain, out, total, scale, bias, guess, half, value):
    step = lambda instruction: chain.then(dve, instruction)
    step(dve.tensor_scalar(value, total, scale, bias, ALU.mult, ALU.add))
    step(dve.tensor_scalar(guess, value.bitcast(I32), 1, None, ALU.arith_shift_right))
    step(dve.tensor_scalar(guess, guess, -1.0, float(0x5F3759DF), ALU.mult, ALU.add))
    y = guess.bitcast(F32)
    for last in (False, False, True):
        step(dve.tensor_tensor(half, y, y, ALU.mult))
        step(dve.tensor_tensor(half, half, value, ALU.mult))
        step(dve.tensor_scalar(half, half, -0.5, 1.5, ALU.mult, ALU.add))
        step(dve.tensor_tensor(out if last else y, y, half, ALU.mult))


class Norm:

    def __init__(self, mem, name, sums, xs, junk, gain, banks):
        self.xs, self.junk, self.gain, self.banks = xs, junk, gain, banks
        self.ssq, self.rstd, self.guess, self.half, self.value = sums
        self.summed = mem.sem(f"{name}_squares_summed")
        self.xs_ready = mem.sem(f"{name}_xs_ready")
        self.turned = mem.sem(f"{name}_turned")
        self.high = mem.sem(f"{name}_high_written")
        self.low = mem.sem(f"{name}_low_written")
        self.chain = Chain(mem, f"{name}_dve_step")


class FeedForward:

    def __init__(self, mem, name, D, F, S):
        at = lambda n, shape, dt, kb: mem.at(f"{name}_{n}", shape, dt, int(kb * KB))
        s = lambda n: mem.sem(f"{name}_{n}")
        K, FT = D // P, F // P
        self.name = name
        self.h = at("h", [P, FT, S], F32, 64)
        self.raw = [at(f"raw_{m}", [P, K, P], F32, 152 + 4 * i) for i, m in enumerate(("gate", "up"))]
        self.part = [[at(f"part_{m}{b}", [P, 2, K, P], FR, 160 + 16 * b + 8 * i)
                      for i, m in enumerate(("gate", "up"))] for b in range(2)]
        self.silu = at("silu", [P, S], F32, 192)
        self.raw_loaded = [s("gate_loaded"), s("up_loaded")]
        self.w_high = s("gate_up_high")
        self.w_low = s("gate_up_low")
        self.gate_done, self.up_done = s("gate_done"), s("up_done")
        self.silu_done, self.h_done = s("silu_done"), s("h_done")
        self.dpart = [at(f"down_part{b}", [P, 2, BANK], FR, 152 + 4 * b) for b in range(3)]
        self.hpart = [at(f"h_part{b}", [P, 2, 3 * P], FR, 164 + 3 * b) for b in range(3)]
        self.y = at("y", [P, 3, D], F32, 173)
        self.res = at("res", [P, D], F32, 185)
        self.gain_post = at("gain_post", [P, D], F32, 189)
        self.gain_pre = at("gain_pre", [P, D], F32, 193)
        self.draw = [at(f"down_raw{b}", [P, BANK], F32, 197 + 2 * b) for b in range(3)]
        self.junk = at("junk", [P, D], BF, 203)
        self.draw_loaded = [s(f"down_loaded{b}") for b in range(3)]
        self.d_high, self.d_low = s("down_high"), s("down_low")
        self.hp_high, self.hp_low = s("h_part_high"), s("h_part_low")
        self.unit_done = s("down_unit_done")
        self.y_act, self.y_dve = s("y_left_by_act"), s("y_left_by_dve")
        self.gains_loaded = s("gains_loaded")
        self.y_summed = s("y_squares_summed")
        self.res_loaded = s("residual_loaded")
        self.y_final = s("y_final")
        self.res_free = s("residual_free")
        self.stored = s("stored")
        self.chain = Chain(mem, f"{name}_dve_step")


def part_low(dve, low, value, high):
    return dve.tensor_tensor(low, value, high.bitcast(F32), ALU.subtract)



def turn_tile(pe, nm, ps, ident, t, K):
    pe.wait_ge(nm.xs_ready, t + 1)
    nb = len(nm.banks)
    for q in range(2):
        if 2 * t + q >= nb:
            pe.wait_ge(nm.low, 2 * t + q - nb + 1)
        bank = nm.banks[(2 * t + q) % nb]
        for j in range(K // 2):
            k = q * (K // 2) + j
            mm = pe.transpose(ps[:, bank, j * P:(j + 1) * P],
                              nm.xs[t % len(nm.xs)][:, k * P:(k + 1) * P], ident[:, :])
        mm.then_inc(nm.turned, 1)


def high_tile(act, nm, ps, xn, t):
    for q in range(2):
        act.wait_ge(nm.turned, 2 * t + q + 1)
        bank = nm.banks[(2 * t + q) % len(nm.banks)]
        act.activation(xn[0][:, 4 * q:4 * q + 4, t * P:(t + 1) * P],
                       ps[:, bank, :].rearrange("p (k c) -> p k c", c=P), ACT.Copy).then_inc(nm.high, 1)


def low_tile(dve, nm, ps, xn, t):
    for q in range(2):
        dve.wait_ge(nm.high, 2 * t + q + 1)
        bank = nm.banks[(2 * t + q) % len(nm.banks)]
        at = (slice(None), slice(4 * q, 4 * q + 4), slice(t * P, (t + 1) * P))
        part_low(dve, xn[1][at], ps[:, bank, :].rearrange("p (k c) -> p k c", c=P),
                 xn[0][at]).then_inc(nm.low, 1)


def scale_tile(dve, nm, t, tile):
    if t >= len(nm.xs):
        dve.wait_ge(nm.turned, 2 * (t - len(nm.xs)) + 2)
    dve.scalar_tensor_tensor(nm.xs[t % len(nm.xs)][:, :], tile, nm.rstd[:, t:t + 1], nm.gain[:, :],
                             ALU.mult, ALU.mult).then_inc(nm.xs_ready, 1)


def norm_roots(dve, nm, a, b, D):
    dve.wait_ge(nm.summed, b)
    w = slice(0, b - a)
    inverse_root(dve, nm.chain, nm.rstd[:, a:b], nm.ssq[:, a:b], 1.0 / D, EPS,
                 nm.guess[:, w], nm.half[:, w], nm.value[:, w])


def norm_all_scalar(act, nm, ps, xn, tiles, ready):
    for t, tile in enumerate(tiles):
        ready(act, t)
        if t > 0:
            act.wait_ge(nm.summed, t)
        act.activation(nm.junk, tile, ACT.Square, accum_out=nm.ssq[:, t:t + 1]).then_inc(nm.summed, 1)
    for t in range(len(tiles)):
        high_tile(act, nm, ps, xn, t)


def norm_all_vector(dve, nm, ps, xn, tiles, gain_ready, D):
    n = len(tiles)
    for t, tile in enumerate(tiles):
        if t % 4 == 0:
            norm_roots(dve, nm, t, t + 4, D)
        if t == 0:
            gain_ready(dve)
        scale_tile(dve, nm, t, tile)
        if t >= 1:
            low_tile(dve, nm, ps, xn, t - 1)
    low_tile(dve, nm, ps, xn, n - 1)



def gate_up_sync(sp, s, weights):
    def load(f, first):
        for m, w in enumerate(weights):
            if not first:
                sp.wait_ge(s.w_low, 2 * f - 1 + m)
            sp.dma_start(s.raw[m][:, :, :], w[:, :, bass.ds(f * P, P)]).then_inc(s.raw_loaded[m], 16)

    load(0, True)
    with sp.Fori(1, s.h.shape[1]) as f:
        load(f, False)


def gate_up_high(act, s, f, b, first):
    done = (s.gate_done, s.up_done)
    for m in range(2):
        act.wait_ge(s.raw_loaded[m], 16 * f + 16)
        if not first:
            act.wait_ge(done[m], f - 1)
        act.activation(s.part[b][m][:, 0, :, :], s.raw[m][:, :, :], ACT.Copy).then_inc(s.w_high, 1)


def gate_up_low(dve, s, f, b):
    for m in range(2):
        dve.wait_ge(s.w_high, 2 * f + m + 1)
        part_low(dve, s.part[b][m][:, 1, :, :], s.raw[m][:, :, :],
                 s.part[b][m][:, 0, :, :]).then_inc(s.w_low, 1)


def gate_up_silu(act, s, ps, f, b, first):
    act.wait_ge(s.gate_done, f + 1)
    if not first:
        act.wait_ge(s.h_done, f)
    act.activation(s.silu[:, :].rearrange("p (a c) -> p a c", c=BANK), ps[:, 4 * b:4 * b + 2, :],
                   ACT.Silu).then_inc(s.silu_done, 1)


def gate_up_product(dve, s, ps, f, b):
    dve.wait_ge(s.silu_done, f + 1)
    dve.wait_ge(s.up_done, f + 1)
    S = s.h.shape[2]
    dve.tensor_tensor(s.h[:, f, :] if isinstance(f, int) else s.h[:, bass.ds(f, 1), :].rearrange("p a s -> p (a s)"),
                      s.silu[:, :], ps[:, 4 * b + 2:4 * b + 4, :].rearrange("p a c -> p (a c)"),
                      ALU.mult).then_inc(s.h_done, 1)


def gate_up_scalar(act, s, ps):
    FT = s.h.shape[1]
    gate_up_high(act, s, 0, 0, True)
    gate_up_high(act, s, 1, 1, True)
    gate_up_silu(act, s, ps, 0, 0, True)
    with act.Fori(1, FT - 1, 2) as f:
        for q in range(2):
            gate_up_high(act, s, f + (q + 1), q, False)
            gate_up_silu(act, s, ps, f + q, 1 - q, False)
    gate_up_silu(act, s, ps, FT - 1, 1, False)


def gate_up_vector(dve, s, ps):
    FT = s.h.shape[1]
    gate_up_low(dve, s, 0, 0)
    gate_up_low(dve, s, 1, 1)
    gate_up_product(dve, s, ps, 0, 0)
    with dve.Fori(1, FT - 1, 2) as f:
        for q in range(2):
            gate_up_low(dve, s, f + (q + 1), q)
            gate_up_product(dve, s, ps, f + q, 1 - q)
    gate_up_product(dve, s, ps, FT - 1, 1)


def three_passes(pe, out, a, b, start, stop):
    for q, (i, j) in enumerate(((0, 0), (0, 1), (1, 0))):
        mm = pe.matmul(out, a[i], b[j], start=start and q == 0, stop=stop and q == 2)
    return mm


def gate_up_tensor(pe, s, ps, xn):
    FT, K = s.h.shape[1], s.part[0][0].shape[2]

    def tile(f, b, first):
        for m, (done, free) in enumerate(((s.gate_done, s.silu_done), (s.up_done, s.h_done))):
            pe.wait_ge(s.w_low, 2 * f + m + 1)
            if not first:
                pe.wait_ge(free, f - 1)
            w = s.part[b][m]
            for th in range(2):
                for k in range(K):
                    mm = three_passes(pe, ps[:, 4 * b + 2 * m + th, :],
                                      [w[:, i, k, :] for i in range(2)],
                                      [x[:, k, th * BANK:(th + 1) * BANK] for x in xn],
                                      k == 0, k == K - 1)
            mm.then_inc(done, 1)

    tile(0, 0, True)
    tile(1, 1, True)
    with pe.Fori(2, FT, 2) as f:
        for q in range(2):
            tile(f + q, q, False)



GROUPS = [(0, 3), (3, 3), (6, 2)]
RING = 3


def down_sync(sp, s, w_down):
    FT = s.h.shape[1]

    def load(g, i, c):
        for n in range(2):
            const = 2 * (FT * g + c) + n
            if not (isinstance(i, int) and const < RING):
                sp.wait_ge(s.d_low, 6 * i + (const - RING + 1))
            sp.dma_start(s.draw[const % RING][:, :],
                         w_down[bass.ds((3 * i + c) * P, P), n * BANK:(n + 1) * BANK])\
              .then_inc(s.draw_loaded[const % RING], 16)

    for g in range(len(GROUPS)):
        for c in range(4):
            load(g, 0, c)
        with sp.Fori(1, FT // 3) as i:
            for c in range(1, 4):
                load(g, i, c)


def down_high(act, s, g, i, c):
    FT = s.h.shape[1]
    t0, n_tiles = GROUPS[g]
    v = FT * g + c
    f = 3 * i + c
    if v >= RING or not isinstance(i, int):
        act.wait_ge(s.unit_done, 6 * i + 2 * (v - RING) + 2)
    src = s.h[:, f, t0 * P:(t0 + n_tiles) * P] if isinstance(f, int) else \
        s.h[:, bass.ds(f, 1), t0 * P:(t0 + n_tiles) * P].rearrange("p a s -> p (a s)")
    act.activation(s.hpart[v % RING][:, 0, 0:n_tiles * P], src, ACT.Copy).then_inc(s.hp_high, 1)
    for n in range(2):
        const = 2 * v + n
        act.wait_ge(s.draw_loaded[const % RING], 16 * (2 * i) + 16 * (const // RING + 1))
        if const >= RING or not isinstance(i, int):
            act.wait_ge(s.unit_done, 6 * i + (const - RING + 1))
        act.activation(s.dpart[const % RING][:, 0, :], s.draw[const % RING][:, :], ACT.Copy)\
           .then_inc(s.d_high, 1)


def down_low(dve, s, g, i, c):
    FT = s.h.shape[1]
    t0, n_tiles = GROUPS[g]
    v = FT * g + c
    f = 3 * i + c
    dve.wait_ge(s.hp_high, 3 * i + v + 1)
    src = s.h[:, f, t0 * P:(t0 + n_tiles) * P] if isinstance(f, int) else \
        s.h[:, bass.ds(f, 1), t0 * P:(t0 + n_tiles) * P].rearrange("p a s -> p (a s)")
    hp = s.hpart[v % RING]
    part_low(dve, hp[:, 1, 0:n_tiles * P], src, hp[:, 0, 0:n_tiles * P]).then_inc(s.hp_low, 1)
    for n in range(2):
        const = 2 * v + n
        dve.wait_ge(s.d_high, 6 * i + const + 1)
        dp = s.dpart[const % RING]
        part_low(dve, dp[:, 1, :], s.draw[const % RING][:, :], dp[:, 0, :]).then_inc(s.d_low, 1)


def down_products(pe, s, ps, g, i, c):
    FT = s.h.shape[1]
    t0, n_tiles = GROUPS[g]
    v = FT * g + c
    pe.wait_ge(s.hp_low, 3 * i + v + 1)
    for n in range(2):
        const = 2 * v + n
        pe.wait_ge(s.d_low, 6 * i + const + 1)
        hp, dp = s.hpart[v % RING], s.dpart[const % RING]
        for k in range(n_tiles):
            if c == 0 and g > 0:
                pe.wait_ge((s.y_act, s.y_dve)[n], GROUPS[g - 1][0] + k + 1)
            mm = three_passes(pe, ps[:, 2 * k + n, :],
                              [hp[:, a, k * P:(k + 1) * P] for a in range(2)],
                              [dp[:, a, :] for a in range(2)],
                              c == 0, isinstance(i, int) and 3 * i + c == FT - 1)
        mm.then_inc(s.unit_done, 1)


def leave_scalar(act, s, ps, g, nm):
    t0, n = GROUPS[g]
    units = 2 * s.h.shape[1] * (g + 1)
    act.wait_ge(s.unit_done, units)
    if g > 0:
        act.wait_ge(s.stored, 16 * t0)
        if nm:
            act.wait_ge(nm.xs_ready, t0)
    for k in range(n):
        act.activation(s.y[:, k, 0:BANK], ps[:, 2 * k, :], ACT.Copy).then_inc(s.y_act, 1)
    for k in range(n):
        act.wait_ge(s.y_dve, t0 + k + 1)
        act.wait_ge(s.y_act, t0 + k + 1)
        if t0 + k > 0:
            act.wait_ge(s.y_summed, t0 + k)
        if nm and g > 0 and k == 0:
            act.wait_ge(nm.summed, t0)
        act.activation(s.junk[:, :], s.y[:, k, :], ACT.Square, accum_out=s.ssq[:, t0 + k:t0 + k + 1])\
           .then_inc(s.y_summed, 1)


def leave_vector(dve, s, ps, g, D, factor):
    t0, n = GROUPS[g]
    dve.wait_ge(s.unit_done, 2 * s.h.shape[1] * (g + 1))
    if g > 0:
        dve.wait_ge(s.stored, 16 * t0)
    for k in range(n):
        dve.tensor_copy(s.y[:, k, BANK:2 * BANK], ps[:, 2 * k + 1, :]).then_inc(s.y_dve, 1)
    dve.wait_ge(s.y_summed, t0 + n)
    inverse_root(dve, s.chain, s.rstd[:, t0:t0 + n], s.ssq[:, t0:t0 + n], factor ** -2 / D,
                 EPS * factor ** -2, s.guess[:, 0:n], s.half[:, 0:n], s.value[:, 0:n])


def residual_vector(dve, s, g, k):
    t = GROUPS[g][0] + k
    if t == 0:
        dve.wait_ge(s.gains_loaded, s.gains)
    s.chain.then(dve, dve.scalar_tensor_tensor(s.y[:, k, :], s.y[:, k, :], s.rstd[:, t:t + 1],
                                               s.gain_post[:, :], ALU.mult, ALU.mult))
    dve.wait_ge(s.res_loaded, 16 * (t + 1))
    dve.tensor_tensor(s.y[:, k, :], s.y[:, k, :], s.res[:, :], ALU.add).then_inc(s.y_final, 1)


def square_scalar(act, s, nm, g, k):
    t = GROUPS[g][0] + k
    act.wait_ge(s.y_final, t + 1)
    act.wait_ge(s.y_summed, GROUPS[g][0] + GROUPS[g][1])
    if t > 0:
        act.wait_ge(nm.summed, t)
    act.activation(s.junk[:, :], s.y[:, k, :], ACT.Square, accum_out=nm.ssq[:, t:t + 1])\
       .then_inc(nm.summed, 1)


def down_scalar(act, s, ps, nm, xn):
    FT = s.h.shape[1]
    act.wait_ge(s.up_done, FT)
    down_high(act, s, 0, 0, 0)
    for c in range(1, 4):
        down_high(act, s, 0, 0, c)
    with act.Fori(1, FT // 3) as i:
        for c in range(1, 4):
            down_high(act, s, 0, i, c)
    for g in range(len(GROUPS)):
        nxt = g + 1 < len(GROUPS)
        if nxt:
            down_high(act, s, g + 1, 0, 0)
        leave_scalar(act, s, ps, g, nm)
        t0, n = GROUPS[g]
        for slot in range(1, 8):
            if nxt:
                for c in range(1, 4):
                    down_high(act, s, g + 1, slot - 1, c)
            if nm and slot <= n:
                square_scalar(act, s, nm, g, slot - 1)
            if nm and 5 <= slot < 5 + n:
                high_tile(act, nm, ps, xn, t0 + slot - 5)


def down_vector(dve, s, ps, nm, xn, D, factor):
    FT = s.h.shape[1]
    for c in range(4):
        down_low(dve, s, 0, 0, c)
    with dve.Fori(1, FT // 3) as i:
        for c in range(1, 4):
            down_low(dve, s, 0, i, c)
    for g in range(len(GROUPS)):
        nxt = g + 1 < len(GROUPS)
        if nxt:
            down_low(dve, s, g + 1, 0, 0)
        leave_vector(dve, s, ps, g, D, factor)
        t0, n = GROUPS[g]
        for slot in range(1, 8):
            if nxt:
                for c in range(1, 4):
                    down_low(dve, s, g + 1, slot - 1, c)
            if slot <= n:
                residual_vector(dve, s, g, slot - 1)
            if nm and slot == 4:
                norm_roots(dve, nm, t0, t0 + n, D)
                scale_tile(dve, nm, t0, s.y[:, 0, :])
            if nm and 5 <= slot < 5 + n:
                low_tile(dve, nm, ps, xn, t0 + slot - 5)
                if slot - 4 < n:
                    scale_tile(dve, nm, t0 + slot - 4, s.y[:, slot - 4, :])


def down_tensor(pe, s, ps, nm, ident):
    FT = s.h.shape[1]
    pe.wait_ge(s.silu_done, FT)
    pe.wait_ge(s.h_done, FT)
    K = s.y.shape[2] // P
    for c in range(4):
        down_products(pe, s, ps, 0, 0, c)
    with pe.Fori(1, FT // 3 - 1) as i:
        for c in range(1, 4):
            down_products(pe, s, ps, 0, i, c)
    for c in range(1, 4):
        down_products(pe, s, ps, 0, FT // 3 - 1, c)
    for g in range(len(GROUPS)):
        t0, n = GROUPS[g]
        if g + 1 < len(GROUPS):
            down_products(pe, s, ps, g + 1, 0, 0)
            with pe.Fori(0, 5) as i:
                for c in range(1, 4):
                    down_products(pe, s, ps, g + 1, i, c)
        for slot in (5, 6, 7):
            if g + 1 < len(GROUPS) and slot >= 6:
                for c in range(1, 4):
                    down_products(pe, s, ps, g + 1, slot - 1, c)
            if nm and slot < 5 + n:
                turn_tile(pe, nm, ps, ident, t0 + slot - 5, K)


def down_pool(pool, s, res, out, nm):
    t = 0
    for g, (t0, n) in enumerate(GROUPS):
        for k in range(n):
            t = t0 + k
            if t > 0:
                pool.wait_ge(s.y_final, t)
            if nm and k == 0 and g > 0:
                pool.wait_ge(nm.turned, 2 * t0)
            if t == 0:
                pool.wait_ge(s.h_done, s.h.shape[1])
            pool.dma_start(s.res[:, :], res[t * P:(t + 1) * P, :]).then_inc(s.res_loaded, 16)
            pool.wait_ge(s.y_final, t + 1)
            pool.dma_start(out[t * P:(t + 1) * P, :], s.y[:, k, :]).then_inc(s.stored, 16)



HEADS_M, HEADS_A, HEADS_KV, DH_A = 4, 8, 2, 64
CONV = 4
ROPE_HALF = 8
THETA = 500000.0
NV, NO, NQ = 129, 512, 512
TOK = HEADS_M * NV + NO + NQ
OG, AQ = HEADS_M * NV, HEADS_M * NV + NO
BIG = 3.0e38
QK_SCALE = 0.25 * P ** -0.5


class Mixer:

    def __init__(self, mem, S, D):
        at = lambda n, shape, dt, kb: mem.at(f"mix_{n}", shape, dt, int(kb * KB))
        s = lambda n: mem.sem(f"mix_{n}")
        T, K = S // P, D // P
        self.T, self.K = T, K
        self.tok = at("tok", [P, T, TOK], F32, 64)
        self.ak = at("ak", [P, T, 4, DH_A], F32, 112.25)
        self.av = at("av", [P, T, 4, DH_A], F32, 120.25)
        self.qk = at("qk", [P, 2 * HEADS_M, S], F32, 173)
        self.traw = [at(f"token_raw{b}", [P, BANK], F32, 128.25 + 2 * b) for b in range(3)]
        self.tpart = [at(f"token_part{b}", [P, 2, BANK], FR, 134.25 + 4 * b) for b in range(3)]
        self.traw_loaded = [s(f"token_loaded{b}") for b in range(3)]
        self.t_high, self.t_low, self.t_unit = s("token_high"), s("token_low"), s("token_unit_done")
        self.left = [s("bank_left_by_act"), s("bank_left_by_dve")]
        self.tanh_o, self.og_done = s("tanh_o"), s("og_done")
        self.gain_norm = at("gain_norm", [P, HEADS_M * P], F32, 146.25)
        self.pos_i = at("pos_i", [P, T], I32, 164.25)
        self.pos = at("pos", [P, T], F32, 164.375)
        self.freq = at("freq", [P, ROPE_HALF], F32, 164.5)
        self.ang = at("ang", [P, T, ROPE_HALF], F32, 164.75)
        self.turns = at("turns", [P, T, ROPE_HALF], F32, 165)
        self.cos = at("cos", [P, T, ROPE_HALF], F32, 165.25)
        self.sin = at("sin", [P, T, ROPE_HALF], F32, 165.5)
        self.rt = [at(f"rope{i}", [P, T, 8, ROPE_HALF], F32, 156.25 + 2 * i) for i in range(4)]
        self.pos_loaded, self.angles, self.sines = s("pos_loaded"), s("angles"), s("sines")
        self.roped = s("roped")
        self.qbd = at("q_blocks", [P, 4, 2, P], F32, 148.25)
        self.kt = [at(f"kt{b}", [P, 2, 3, DH_A], F32, 152.25 + 1.5 * b) for b in range(2)]
        self.vsh = at("v_shifted", [P, 4, DH_A], F32, 155.25)
        self.pr = [at(f"probs{e}", [P, 4, P], F32, 156.25 + 2 * e) for e in range(2)]
        self.pt = [at(f"probs_turned{e}", [P, 4, P], F32, 160.25 + 2 * e) for e in range(2)]
        small = 207.25
        names = ("mx", "neg", "es", "rs", "rinv", "sd")
        stats = at("softmax_stats", [P, 12, 4], F32, small)
        self.st = [{n: stats[:, 6 * e + i, :] for i, n in enumerate(names)} for e in range(2)]
        self.sink = at("sink", [P, 4], F32, small + .1875)
        self.conv_w = at("conv_w", [P, CONV, 8], F32, small + .21875)
        self.conv_b = at("conv_b", [P, 8], F32, small + .34375)
        self.consts_loaded = s("constants_loaded")
        self.zeroed = s("zeroed")
        self.q_turned, self.k_turned = s("q_turned"), s("k_turned")
        self.qbd_ready, self.kt_ready = s("q_blocks_ready"), s("kt_ready")
        self.logits, self.stats, self.exps = s("logits"), s("softmax_shift"), s("exps")
        self.probs, self.pt_turned, self.pt_ready = s("probs"), s("probs_turned"), s("probs_turned_ready")
        self.vsh_ready, self.pv, self.ha_done = s("v_shifted_ready"), s("pv"), s("attention_out")
        self.qraw = at("qk_raw", [P, K, P], F32, 128.25)
        self.qpart = [at(f"qk_part{b}", [P, 2, K, P], FR, 132.25 + 8 * b) for b in range(2)]
        self.xp = at("conv_in", [P, 3 + S], F32, 164.25)
        self.q_loaded, self.q_high, self.q_low = s("qk_loaded"), s("qk_high"), s("qk_low")
        self.q_half, self.xp_ready = s("qk_half_done"), s("conv_in_ready")
        self.conv_done, self.tanh_qk, self.qk_done = s("conv_done"), s("tanh_qk"), s("qk_done")
        R = HEADS_M * T
        self.R = R
        self.gt = at("gates_token_major", [P, 2, HEADS_M, T], F32, 168.5)
        self.gbias = at("gate_bias", [P, 2, HEADS_M], F32, 168.75)
        g = [at(n, [R, P], F32, 168.8125 + .5 * i) for i, n in
             enumerate(("g_li", "g_f", "g_lf", "g_cum", "g_b", "g_cmax"))]
        self.g_li, self.g_f, self.g_lf, self.g_cum, self.g_b, self.g_cmax = g
        self.gout = at("g_out", [R, 2, P], F32, 171.8125)
        self.gsmall = at("g_small", [R, 8], F32, 172.875)
        self.gate_in, self.g_pe, self.g_sb, self.g_act = s("gate_in"), s("gate_pe"), s("gate_dve"), s("gate_act")
        self.g_stored = s("gate_rows_stored")
        self.col = at("gate_columns", [P, 3, R], F32, 206)
        self.dec = at("decay", [P, R], F32, 206.375)
        self.wraw = [at(f"out_raw{b}", [P, D], F32, 112.25 + 4 * b) for b in range(2)]
        self.wo = [at(f"out_{n}", [P, K, D], FR, 32 * i) for i, n in enumerate(("high", "low"))]
        self.bc = [at(f"gate_rows{b}", [P, 2, HEADS_M, P], F32, 120.25 + 4 * b) for b in range(2)]
        self.dm = at("decay_matrix", [P, HEADS_M, P], F32, 128.25)
        self.sc = at("scores", [P, HEADS_M, P], F32, 130.25)
        self.kw = at("k_weighted", [P, HEADS_M, P], F32, 132.25)
        self.qw = at("q_weighted", [P, HEADS_M, P], F32, 134.25)
        self.C = [at(f"state{b}", [P, HEADS_M, NV], F32, 136.25 + 2.125 * b) for b in range(2)]
        self.hm = at("hm", [P, HEADS_M, P], F32, 140.5)
        self.hs = [at(f"out_in{b}", [P, 2, K, P], FR, 142.5 + 8 * b) for b in range(2)]
        self.res = at("residual", [P, D], F32, 158.5)
        self.gain_post = at("gain_post", [P, D], F32, 162.5)
        self.junk = at("junk", [P, D], BF, 166.5)
        names = ("ad", "r", "rs", "nb", "vr", "half", "value")
        stats = at("norm_stats", [P, 8, 4], F32, small)
        self.sm = {n: stats[:, i, :] for i, n in enumerate(names)}
        self.sm["guess"] = stats[:, 7, :].bitcast(I32)
        self.bn = at("bn", [P, 4, 6], F32, small + .125)
        self.mv = at("mean_var", [P, 4, 2], F32, small + .21875)
        self.w_loaded = [s(f"out_loaded{b}") for b in range(2)]
        self.w_high, self.w_low = s("out_high"), s("out_low")
        self.bc_loaded = [s(f"gate_rows_loaded{b}") for b in range(2)]
        self.s_done, self.k_done = s("scores_done"), s("k_turned_m")
        self.dm_shift, self.dm_done, self.wg_done = s("decay_shift"), s("decay_done"), s("wg_done")
        self.sc_done, self.kw_done, self.qw_done = s("scores_weighted"), s("kw_done"), s("qw_done")
        self.n_done, self.c_done, self.state = s("num_done"), s("kv_done"), s("state_done")
        self.norm_ready, self.hm_norm, self.hm_done = s("norm_ready"), s("hm_norm"), s("hm_done")
        self.hm_turned, self.hs_high, self.hs_low = s("hm_turned"), s("out_in_high"), s("out_in_low")
        self.y_done, self.y_summed, self.y_scaled = s("y_done"), s("y_summed"), s("y_scaled")
        self.res_loaded, self.h_done, self.stored = s("residual_loaded"), s("h_done"), s("stored")
        self.post_loaded = s("post_gain_loaded")
        self.chain = Chain(mem, "mix_dve_step")


M_W = HEADS_M * P
GATES, A_Q = 4 * M_W, 4 * M_W + 2 * HEADS_M
A_K = A_Q + HEADS_A * DH_A
CHUNKS = [
    [(0, GATES, 2 * HEADS_M), (2 * HEADS_M, A_K, 2 * HEADS_KV * DH_A)],
    [(0, A_Q, HEADS_A * DH_A)],
    [(0, 2 * M_W, M_W)],
    [(0, 3 * M_W, M_W)],
]
WIDTH = [sum(w for _, _, w in c) for c in CHUNKS]


def tokens_sync(sp, m, w_in, ff):
    counts = [0] * RING
    m.traw_at = []
    for chunk, cols in enumerate(CHUNKS):
        for k in range(m.K):
            u = chunk * m.K + k
            if u >= RING:
                sp.wait_ge(m.t_low, u - RING + 1)
            for a, c, w in cols:
                sp.dma_start(m.traw[u % RING][:, a:a + w], w_in[k * P:(k + 1) * P, c:c + w])\
                  .then_inc(m.traw_loaded[u % RING], 16)


def token_loads(u, K):
    return 16 * sum(len(CHUNKS[v // K]) for v in range(u % RING, u + 1, RING))


def token_high(act, m, u):
    w = WIDTH[u // m.K]
    act.wait_ge(m.traw_loaded[u % RING], token_loads(u, m.K))
    if u >= RING:
        act.wait_ge(m.t_unit, u - RING + 1)
    act.activation(m.tpart[u % RING][:, 0, 0:w], m.traw[u % RING][:, 0:w], ACT.Copy).then_inc(m.t_high, 1)


def token_low(dve, m, u):
    w = WIDTH[u // m.K]
    dve.wait_ge(m.t_high, u + 1)
    p = m.tpart[u % RING]
    part_low(dve, p[:, 1, 0:w], m.traw[u % RING][:, 0:w], p[:, 0, 0:w]).then_inc(m.t_low, 1)


def tokens_tensor(pe, m, ps, xn):
    for chunk, w in enumerate(WIDTH):
        for k in range(m.K):
            u = chunk * m.K + k
            pe.wait_ge(m.t_low, u + 1)
            part = m.tpart[u % RING]
            for t in range(m.T):
                if k == 0 and chunk > 0:
                    pe.wait_ge(m.left[t % 2], m.T // 2 * (chunk - 1) + t // 2 + 1)
                mm = three_passes(pe, ps[:, t, 0:w], [x[:, k, t * P:(t + 1) * P] for x in xn],
                                  [part[:, i, 0:w] for i in range(2)], k == 0, k == m.K - 1)
            mm.then_inc(m.t_unit, 1)


def tokens_leave(eng, copy, m, ps, chunk, which):
    eng.wait_ge(m.t_unit, m.K * (chunk + 1))
    for t in range(which, m.T, 2):
        bank = ps[:, t, :]
        if chunk == 0:
            copy(m.gt[:, :, :, t], bank[:, 0:8].rearrange("p (g h) -> p g h", g=2))
            for j, to in enumerate((m.ak, m.av)):
                src = bank[:, 8 + P * j:8 + P * (j + 1)].rearrange("p (k f) -> p k f", k=2)
                for d in range(2):
                    ins = copy(to[:, t, d::2, :], src)
        elif chunk == 1:
            ins = copy(m.tok[:, t, AQ:AQ + NQ], bank)
        elif chunk == 2:
            ins = copy(m.tok[:, t, 0:HEADS_M * NV].rearrange("p (h e) -> p h e", e=NV)[:, :, 0:P],
                       bank.rearrange("p (h e) -> p h e", e=P))
        ins.then_inc(m.left[which], 1)


def tokens_scalar(act, m, ps):
    copy = lambda out, in_: act.activation(out, in_, ACT.Copy)
    for chunk in range(len(CHUNKS)):
        for k in range(m.K):
            token_high(act, m, chunk * m.K + k)
            if chunk > 0 and k == 1:
                tokens_leave(act, copy, m, ps, chunk - 1, 0)
            if chunk == 2 and k == 5:
                act.wait_ge(m.angles, 1)
                act.activation(m.sin[:, :, :], m.sin[:, :, :], ACT.Sin).then_inc(m.sines, 1)
                act.activation(m.cos[:, :, :], m.cos[:, :, :], ACT.Sin).then_inc(m.sines, 1)
    act.wait_ge(m.t_unit, m.K * len(CHUNKS))
    for t in range(m.T):
        act.activation(m.tok[:, t, OG:OG + NO], ps[:, t, :], ACT.Tanh, scale=0.5).then_inc(m.tanh_o, 1)


def angles_vector(dve, m):
    then = m.chain.then
    for i in range(ROPE_HALF):
        dve.memset(m.freq[:, i:i + 1], float(np.float32(np.float32(THETA) ** np.float32(-i / ROPE_HALF))))\
           .then_inc(m.chain.sem, 1)
        m.chain.count += 1
    dve.wait_ge(m.chain.sem, m.chain.count)
    dve.wait_ge(m.pos_loaded, 16)
    then(dve, dve.tensor_copy(m.pos[:, :], m.pos_i[:, :]))
    wide = [P, m.T, ROPE_HALF]
    then(dve, dve.tensor_tensor(m.ang[:, :, :], m.pos[:, :].unsqueeze(2).to_broadcast(wide),
                                m.freq[:, :].unsqueeze(1).to_broadcast(wide), ALU.mult))
    ROUND = 1.5 * 2.0 ** 23
    turn = 2 * np.pi
    c1 = 6.28125
    c2 = float(np.float32(np.round((turn - c1) * 2 ** 21) / 2 ** 21))
    c3 = float(np.float32(turn - c1 - c2))
    for out, shift in ((m.sin, 0.0), (m.cos, 0.25)):
        n, o, a = m.turns[:, :, :], out[:, :, :], m.ang[:, :, :]
        then(dve, dve.tensor_scalar(n, a, 1 / turn, shift, ALU.mult, ALU.add))
        then(dve, dve.tensor_scalar(n, n, ROUND, ROUND, ALU.add, ALU.subtract))
        for i, c in enumerate((c1, c2, c3)):
            then(dve, dve.scalar_tensor_tensor(o, n, -c, a if i == 0 else o, ALU.mult, ALU.add))
        if shift:
            then(dve, dve.tensor_scalar(o, o, turn / 4, None, ALU.add))
        last = dve.tensor_scalar(o, o, 3.1415925, -3.1415925, ALU.min, ALU.max)
        if shift:
            last.then_inc(m.angles, 1)
        else:
            then(dve, last)


def rope_vector(dve, m):
    dve.wait_ge(m.sines, 2)
    then = m.chain.then
    q = m.tok[:, :, AQ:AQ + NQ].rearrange("p t (h f) -> p t h f", f=DH_A)
    for x, H in ((q, HEADS_A), (m.ak[:, :, :, :], 4)):
        wide = [P, m.T, H, ROPE_HALF]
        cos = m.cos[:, :, :].unsqueeze(2).to_broadcast(wide)
        sin = m.sin[:, :, :].unsqueeze(2).to_broadcast(wide)
        x1, x2 = x[:, :, :, 0:ROPE_HALF], x[:, :, :, ROPE_HALF:2 * ROPE_HALF]
        a, b, c, d = (r[:, :, 0:H, :] for r in m.rt)
        for o, u, v in ((a, x1, cos), (b, x2, sin), (c, x2, cos), (d, x1, sin)):
            then(dve, dve.tensor_tensor(o, u, v, ALU.mult))
        dve.tensor_tensor(x1, a, b, ALU.subtract).then_inc(m.roped, 1)
        dve.tensor_tensor(x2, c, d, ALU.add).then_inc(m.roped, 1)
        dve.wait_ge(m.roped, 2 if H == HEADS_A else 4)


def tokens_vector(dve, m, ps):
    then = m.chain.then
    for chunk in range(len(CHUNKS)):
        for k in range(m.K):
            token_low(dve, m, chunk * m.K + k)
            if chunk > 0 and k == 1:
                tokens_leave(dve, dve.tensor_copy, m, ps, chunk - 1, 1)
            if chunk == 1 and k == 4:
                angles_vector(dve, m)
            if chunk == 2 and k == 4:
                dve.wait_ge(m.left[0], m.T)
                rope_vector(dve, m)
            if chunk == 3 and k == 4:
                dve.wait_ge(m.consts_loaded, m.consts)
                then(dve, dve.tensor_scalar(m.gain_norm[:, :], m.gain_norm[:, :], 0.5, None, ALU.mult))
                dve.wait_ge(m.left[0], m.T // 2)
                dve.wait_ge(m.left[1], m.T // 2)
                dve.tensor_tensor(m.gt[:, :, :, :], m.gt[:, :, :, :],
                                  m.gbias[:, :, :].unsqueeze(3).to_broadcast([P, 2, HEADS_M, m.T]),
                                  ALU.add).then_inc(m.gate_in, 1)
    for t in range(m.T):
        dve.wait_ge(m.tanh_o, t + 1)
        og = m.tok[:, t, OG:OG + NO]
        dve.scalar_tensor_tensor(og, og, 1.0, m.gain_norm[:, :], ALU.add, ALU.mult).then_inc(m.og_done, 1)



B_Q, B_K, B_L, B_P, B_V = 2, 3, (4, 5), 6, 7


def qk_sync(sp, m, w_in):
    w = w_in[:, 0:2 * M_W].rearrange("(k p) f -> p k f", p=P)
    sp.wait_ge(m.t_low, m.K * len(CHUNKS))
    for i in range(2 * HEADS_M):
        if i > 0:
            sp.wait_ge(m.q_low, i)
        sp.dma_start(m.qraw[:, :, :], w[:, :, i * P:(i + 1) * P]).then_inc(m.q_loaded, 16)


def qk_high(act, m, i):
    act.wait_ge(m.q_loaded, 16 * (i + 1))
    if i == 0:
        act.wait_ge(m.t_unit, m.K * len(CHUNKS))
        act.wait_ge(m.og_done, m.T)
    if i >= 2:
        act.wait_ge(m.q_half, 2 * (i - 1))
    act.activation(m.qpart[i % 2][:, 0, :, :], m.qraw[:, :, :], ACT.Copy).then_inc(m.q_high, 1)


def qk_low(dve, m, i):
    dve.wait_ge(m.q_high, i + 1)
    p = m.qpart[i % 2]
    part_low(dve, p[:, 1, :, :], m.qraw[:, :, :], p[:, 0, :, :]).then_inc(m.q_low, 1)


def qk_half(pe, m, ps, xn, i, th):
    pe.wait_ge(m.q_low, i + 1)
    if i == 0:
        pe.wait_ge(m.tanh_o, m.T)
    else:
        pe.wait_ge(m.xp_ready, 2 * (i - 1) + th + 1)
    w = m.qpart[i % 2]
    for k in range(m.K):
        mm = three_passes(pe, ps[:, th, :], [w[:, a, k, :] for a in range(2)],
                          [x[:, k, th * BANK:(th + 1) * BANK] for x in xn], k == 0, k == m.K - 1)
    mm.then_inc(m.q_half, 1)


def conv_in_scalar(act, m, ps, i):
    for th in range(2):
        act.wait_ge(m.q_half, 2 * i + th + 1)
        if i > 0:
            act.wait_ge(m.qk_done, i)
        else:
            act.wait_ge(m.roped, 4)
            act.wait_ge(m.sines, 2)
        act.activation(m.xp[:, 3 + th * BANK:3 + (th + 1) * BANK], ps[:, th, :], ACT.Copy)\
           .then_inc(m.xp_ready, 1)


def conv_vector(dve, m, i):
    then = m.chain.then
    S = m.qk.shape[2]
    dve.wait_ge(m.xp_ready, 2 * i + 2)
    out = m.qk[:, i, :]
    then(dve, dve.tensor_scalar(out, m.xp[:, 3:3 + S], m.conv_w[:, 3, i:i + 1], m.conv_b[:, i:i + 1],
                                ALU.mult, ALU.add))
    for j in (2, 1, 0):
        ins = dve.scalar_tensor_tensor(out, m.xp[:, j:j + S], m.conv_w[:, j, i:i + 1], out,
                                       ALU.mult, ALU.add)
        if j:
            then(dve, ins)
    ins.then_inc(m.conv_done, 1)


def tanh_scalar(act, m, i):
    S = m.qk.shape[2]
    act.wait_ge(m.conv_done, i + 1)
    act.activation(m.xp[:, 3:3 + S], m.qk[:, i, :], ACT.Tanh, scale=0.5).then_inc(m.tanh_qk, 1)


def silu_vector(dve, m, i):
    S = m.qk.shape[2]
    dve.wait_ge(m.tanh_qk, i + 1)
    dve.scalar_tensor_tensor(m.qk[:, i, :], m.xp[:, 3:3 + S], 1.0, m.qk[:, i, :], ALU.add, ALU.mult)\
       .then_inc(m.qk_done, 1)


def attend_turn_tensor(pe, m, ps, ident, i):
    if i == 0:
        pe.wait_ge(m.roped, 4)
        pe.wait_ge(m.tanh_o, m.T)
    else:
        pe.wait_ge(m.qbd_ready, 2 * i)
        pe.wait_ge(m.kt_ready, i)
        pe.wait_ge(m.g_act, GATE_ACT[min(i, len(GATE_ACT)) - 1])
        pe.wait_ge(m.g_sb, GATE_DVE[min(i, len(GATE_DVE)) - 1])
    for j in range(4):
        mm = pe.transpose(ps[:, B_Q, j * P:(j + 1) * P], m.tok[:, i, AQ + j * P:AQ + (j + 1) * P], ident[:, :])
    mm.then_inc(m.q_turned, 1)
    for j in range(2):
        mm = pe.transpose(ps[:, B_K, j * P:(j + 1) * P],
                          m.ak[:, i, 2 * j:2 * j + 2, :].rearrange("p d f -> p (d f)"), ident[:, :])
    mm.then_inc(m.k_turned, 1)


def attend_q_scalar(act, m, ps, i):
    act.wait_ge(m.q_turned, i + 1)
    if i == 0:
        act.wait_ge(m.zeroed, m.zeros)
    else:
        act.wait_ge(m.logits, 2 * i)
    for e in range(2):
        h = slice(64 * e, 64 * e + 64)
        act.activation(m.qbd[h, :, :, h], ps[h, B_Q, :].rearrange("p (j c q) -> p j c q", j=4, c=2),
                       ACT.Copy).then_inc(m.qbd_ready, 1)


def attend_k_vector(dve, m, ps, i):
    dve.wait_ge(m.k_turned, i + 1)
    if i == 0:
        dve.wait_ge(m.zeroed, m.zeros)
    if i >= 1:
        dve.wait_ge(m.logits, 2 * i)
    src = ps[:, B_K, 0:2 * P].rearrange("p (k c s) -> p k c s", k=2, c=2)
    dve.tensor_copy(m.kt[i % 2][:, :, 0:2, :], src)
    dve.tensor_copy(m.kt[1 - i % 2][:, :, 2, :], src[:, :, 1, :]).then_inc(m.kt_ready, 1)


def attend_logits_tensor(pe, m, ps, i, e):
    if e == 0:
        pe.wait_ge(m.qbd_ready, 2 * i + 2)
        pe.wait_ge(m.kt_ready, i + 1)
    if i > 0:
        pe.wait_ge(m.exps, 2 * (i - 1) + e + 1)
    for j in range(4):
        kt = m.kt[i % 2][:, j // 2, :, :]
        keys = kt[:, 0:2, :] if e else (kt[:, 0::2, :] if i else kt[:, 0:1, :])
        n = keys.shape[1] * DH_A
        mm = pe.matmul(ps[:, B_L[e], j * P:j * P + n], m.qbd[:, j, e, :], keys, start=True, stop=True)
    mm.then_inc(m.logits, 1)


def keys_of(i, e):
    return P if i or e else DH_A


def attend_max_vector(dve, m, ps, i, e):
    then, st, n = m.chain.then, m.st[e], keys_of(i, e)
    dve.wait_ge(m.logits, 2 * i + e + 1)
    if i > 0:
        dve.wait_ge(m.exps, 2 * (i - 1) + e + 1)
    lg = ps[:, B_L[e], :].rearrange("p (j s) -> p j s", j=4)[:, :, 0:n]
    then(dve, dve.tensor_reduce(st["mx"][:, :], lg, AX, ALU.max))
    then(dve, dve.scalar_tensor_tensor(st["mx"][:, :], st["mx"][:, :], DH_A ** -0.5, m.sink[:, :],
                                       ALU.mult, ALU.max))
    dve.tensor_scalar(st["neg"][:, :], st["mx"][:, :], -1.0, None, ALU.mult)
    dve.tensor_tensor(st["sd"][:, :], m.sink[:, :], st["mx"][:, :], ALU.subtract).then_inc(m.stats, 1)


def attend_exp_scalar(act, m, ps, i, e):
    st, n = m.st[e], keys_of(i, e)
    act.wait_ge(m.stats, 2 * i + e + 1)
    if i > 0:
        act.wait_ge(m.pt_turned, 2 * (i - 1) + e + 1)
        act.wait_ge(m.probs, 2 * (i - 1) + e + 1)
    else:
        act.wait_ge(m.zeroed, m.zeros)
        act.wait_ge(m.roped, 4)
    for j in range(4):
        act.activation(m.pr[e][:, j, 0:n], ps[:, B_L[e], j * P:j * P + n], ACT.Exp,
                       bias=st["neg"][:, j:j + 1], scale=DH_A ** -0.5, accum_out=st["rs"][:, j:j + 1])
    act.activation(st["es"][:, :], st["sd"][:, :], ACT.Exp).then_inc(m.exps, 1)


def attend_divide_vector(dve, m, i, e):
    then, st, n = m.chain.then, m.st[e], keys_of(i, e)
    dve.wait_ge(m.exps, 2 * i + e + 1)
    then(dve, dve.tensor_tensor(st["rinv"][:, :], st["rs"][:, :], st["es"][:, :], ALU.add))
    then(dve, dve.reciprocal(st["rinv"][:, :], st["rinv"][:, :]))
    if n < P:
        dve.memset(m.pr[e][:, :, n:P], 0.0)
    pr = m.pr[e][:, :, 0:n]
    dve.tensor_tensor(pr, pr, st["rinv"][:, :].unsqueeze(2).to_broadcast([P, 4, n]), ALU.mult)\
       .then_inc(m.probs, 1)


def attend_probs_tensor(pe, m, ps, ident, i, e):
    pe.wait_ge(m.probs, 2 * i + e + 1)
    if i or e:
        pe.wait_ge(m.pt_ready, 2 * i + e)
    for j in range(4):
        mm = pe.transpose(ps[:, B_P, j * P:(j + 1) * P], m.pr[e][:, j, :], ident[:, :])
    mm.then_inc(m.pt_turned, 1)


def attend_probs_scalar(act, m, ps, i, e):
    act.wait_ge(m.pt_turned, 2 * i + e + 1)
    if i:
        act.wait_ge(m.pv, 2 * (i - 1) + e + 1)
    act.activation(m.pt[e][:, :, :], ps[:, B_P, :].rearrange("p (j q) -> p j q", j=4), ACT.Copy)\
       .then_inc(m.pt_ready, 1)


def attend_values_tensor(pe, m, ps, i, e):
    pe.wait_ge(m.pt_ready, 2 * i + e + 1)
    if not e:
        pe.wait_ge(m.vsh_ready, 2 * i + 2)
    if i or e:
        pe.wait_ge(m.ha_done, 2 * (2 * i + e))
    for kv in range(2):
        v = m.av[:, i, 2 * kv:2 * kv + 2, :] if e else m.vsh[:, 2 * kv:2 * kv + 2, :]
        mm = pe.matmul(ps[:, B_V, 2 * kv * P:2 * (kv + 1) * P], v.rearrange("p d f -> p (d f)"),
                       m.pt[e][:, 2 * kv:2 * kv + 2, :], start=True, stop=True)
    mm.then_inc(m.pv, 1)


def attend_out_scalar(act, m, ps, i, e):
    act.wait_ge(m.pv, 2 * i + e + 1)
    ha = m.tok[:, i, AQ:AQ + NQ].rearrange("p (j q) -> p j q", j=4)
    bank = ps[:, B_V, :].rearrange("p (j q) -> p j q", j=4)
    for d in range(2):
        h = slice(64 * d, 64 * d + 64)
        act.activation(ha[h, :, 64 * e:64 * e + 64], bank[h, :, h], ACT.Copy).then_inc(m.ha_done, 1)


def shifted_values_pool(pool, m, i):
    if i == 0:
        pool.wait_ge(m.left[0], m.T // 2)
        pool.wait_ge(m.left[1], m.T // 2)
        pool.wait_ge(m.zeroed, m.zeros)
    else:
        pool.wait_ge(m.pv, 2 * i - 1)
        pool.wait_ge(m.vsh_ready, 2 * i)
    pool.tensor_copy(m.vsh[0:64, :, :], m.av[0:64, i, :, :]).then_inc(m.vsh_ready, 1)
    pool.wait_ge(m.vsh_ready, 2 * i + 1)
    if i == 0:
        pool.memset(m.vsh[64:128, :, :], 0.0).then_inc(m.vsh_ready, 1)
    else:
        pool.tensor_copy(m.vsh[64:128, :, :], m.av[64:128, i - 1, :, :]).then_inc(m.vsh_ready, 1)



GATE_DVE = (4, 9, 13, 14)
GATE_ACT = (2, 2, 3, 4)


def gate_tensor(pe, m, ps, ident, ones, step):
    R = m.R
    bank = ps[:, B_K, :]
    pe.wait_ge(m.kt_ready, step + 1)
    if step == 0:
        pe.wait_ge(m.gate_in, 1)
        for g in range(2):
            mm = pe.transpose(bank[0:R, g * P:(g + 1) * P], m.gt[:, g, :, :].rearrange("p h t -> p (h t)"),
                              ident[:, :])
    elif step == 1:
        pe.wait_ge(m.g_sb, 4)
        for g in range(2):
            mm = pe.matmul(bank[0:1, g * R:(g + 1) * R], m.gsmall[:, g:g + 1], ident[0:R, 0:R],
                           start=True, stop=True)
    elif step == 2:
        pe.wait_ge(m.g_sb, 9)
        pe.matmul(bank[0:R, 0:1], m.g_lf[0:1, 64:96], ident[0:1, 0:1], start=True, stop=True)
        pe.matmul(bank[0:R, 1:2], m.g_lf[0:1, 96:128], ident[0:1, 0:1], start=True, stop=True)
        mm = pe.matmul(bank[:, 64:64 + R], ones[0:1, :], m.g_f[0:1, 0:R], start=True, stop=True)
    else:
        pe.wait_ge(m.g_sb, 13)
        for j, x in enumerate((m.g_b, m.g_li, m.g_f)):
            mm = pe.transpose(bank[:, j * R:(j + 1) * R], x[:, :], ident[0:R, 0:R])
    mm.then_inc(m.g_pe, 1)


def gate_vector(dve, m, ps, step):
    R, T, then = m.R, m.T, m.chain.then
    bank = ps[:, B_K, :]
    last = lambda ins: ins.then_inc(m.g_sb, 1)
    if step == 0:
        dve.wait_ge(m.g_pe, 1)
        last(dve.tensor_copy(m.g_li[:, :], bank[0:R, 0:P]))
        then(dve, dve.tensor_copy(m.g_f[:, :], bank[0:R, P:2 * P]))
        last(dve.scalar_tensor_tensor(m.g_lf[:, :], m.g_f[:, :], -1.0, m.g_f[:, :], ALU.mult, ALU.max))
        then(dve, dve.memset(m.gout[:, 0, :], 1.0))
        dve.wait_ge(m.g_act, 2)
        then(dve, dve.scalar_tensor_tensor(m.g_lf[:, :], m.g_f[:, :], 0.0, m.g_lf[:, :], ALU.min, ALU.subtract))
        then(dve, dve.tensor_tensor_scan(m.g_cum[:, :], m.gout[:, 0, :], m.g_lf[:, :], 0.0, ALU.mult, ALU.add))
        then(dve, dve.tensor_tensor(m.g_b[:, :], m.g_li[:, :], m.g_cum[:, :], ALU.subtract))
        then(dve, dve.tensor_tensor_scan(m.g_cmax[:, :], m.g_b[:, :], m.g_b[:, :], -BIG, ALU.max, ALU.max))
        last(dve.tensor_copy(m.gsmall[:, 0:1], m.g_cum[:, P - 1:P]))
        last(dve.tensor_tensor(m.gsmall[:, 1:2], m.g_cum[:, P - 1:P], m.g_cmax[:, P - 1:P], ALU.add))
    elif step == 1:
        dve.wait_ge(m.g_pe, 2)
        row = m.g_lf[0:1, :]
        then(dve, dve.tensor_copy(row[:, 0:2 * R], bank[0:1, 0:2 * R]))
        then(dve, dve.memset(row[:, 64:96], 0.0))
        for h in range(HEADS_M):
            a = slice(h * T, (h + 1) * T)
            last(dve.tensor_tensor_scan(row[:, 96 + h * T:96 + (h + 1) * T], row[:, h * T:(h + 1) * T],
                                        row[:, R + h * T:R + (h + 1) * T], 0.0, ALU.add, ALU.max))
        dve.wait_ge(m.g_sb, 8)
        rows = lambda a: row[:, a:a + R].rearrange("p (h t) -> p h t", h=HEADS_M)
        then(dve, dve.tensor_copy(rows(64)[:, :, 1:T], rows(96)[:, :, 0:T - 1]))
        then(dve, dve.tensor_tensor(m.g_f[0:1, 0:R], row[:, 0:R], row[:, 64:96], ALU.add))
        last(dve.tensor_tensor(m.g_f[0:1, 0:R], m.g_f[0:1, 0:R], row[:, 96:128], ALU.subtract))
    elif step == 2:
        dve.wait_ge(m.g_pe, 3)
        then(dve, dve.tensor_copy(m.gsmall[:, 2:4], bank[0:R, 0:2]))
        before, after = m.gsmall[:, 2:3], m.gsmall[:, 3:4]
        then(dve, dve.tensor_scalar(m.gout[:, 0, :], m.g_cmax[:, :], before, -1.0, ALU.max, ALU.mult))
        last(dve.tensor_scalar(m.gout[:, 1, :], m.gout[:, 0, :], before, None, ALU.add))
        last(dve.tensor_tensor(m.g_f[:, :], m.gout[:, 0, :], m.g_cum[:, :], ALU.subtract))
        then(dve, dve.tensor_tensor(m.gsmall[:, 4:5], m.gsmall[:, 0:1], after, ALU.subtract))
        last(dve.tensor_scalar(m.g_li[:, :], m.g_b[:, :], m.gsmall[:, 4:5], None, ALU.add))
        last(dve.memset(m.gsmall[:, 5:6], 0.0))
    else:
        dve.wait_ge(m.g_act, 4)
        last(dve.tensor_scalar(m.col[:, 1, :], m.col[:, 1, :], QK_SCALE, None, ALU.mult))


def gate_scalar(act, m, ps, step):
    R, bank = m.R, ps[:, B_K, :]
    if step == 0:
        act.wait_ge(m.g_sb, 2)
        act.activation(m.g_lf[:, :], m.g_lf[:, :], ACT.Exp, scale=-1.0).then_inc(m.g_act, 1)
        act.wait_ge(m.g_act, 1)
        act.activation(m.g_lf[:, :], m.g_lf[:, :], ACT.Ln, bias=1.0).then_inc(m.g_act, 1)
    elif step == 2:
        act.wait_ge(m.g_sb, 13)
        act.activation(m.dec[:, :], bank[:, 64:64 + R], ACT.Exp).then_inc(m.g_act, 1)
    elif step == 3:
        act.wait_ge(m.g_pe, 4)
        act.activation(m.col[:, 0, :], bank[:, 0:R], ACT.Copy)
        act.activation(m.col[:, 1:3, :], bank[:, R:3 * R].rearrange("p (a r) -> p a r", a=2), ACT.Exp)\
           .then_inc(m.g_act, 1)


def heads_tensor(pe, m, ps, xn, ident, ones):
    for i in range(m.T):
        attend_turn_tensor(pe, m, ps, ident, i)
        if i:
            attend_values_tensor(pe, m, ps, i - 1, 0)
            attend_probs_tensor(pe, m, ps, ident, i - 1, 1)
        qk_half(pe, m, ps, xn, i, 0)
        attend_logits_tensor(pe, m, ps, i, 0)
        attend_logits_tensor(pe, m, ps, i, 1)
        if i:
            attend_values_tensor(pe, m, ps, i - 1, 1)
        qk_half(pe, m, ps, xn, i, 1)
        attend_probs_tensor(pe, m, ps, ident, i, 0)
        if i < 4:
            gate_tensor(pe, m, ps, ident, ones, i)
    attend_values_tensor(pe, m, ps, m.T - 1, 0)
    attend_probs_tensor(pe, m, ps, ident, m.T - 1, 1)
    attend_values_tensor(pe, m, ps, m.T - 1, 1)


def heads_scalar(act, m, ps):
    T = m.T
    qk_high(act, m, 0)
    for i in range(T):
        attend_q_scalar(act, m, ps, i)
        if i + 1 < T:
            qk_high(act, m, i + 1)
        if i:
            attend_out_scalar(act, m, ps, i - 1, 0)
            attend_probs_scalar(act, m, ps, i - 1, 1)
        attend_exp_scalar(act, m, ps, i, 0)
        attend_exp_scalar(act, m, ps, i, 1)
        if i:
            attend_out_scalar(act, m, ps, i - 1, 1)
        conv_in_scalar(act, m, ps, i)
        attend_probs_scalar(act, m, ps, i, 0)
        tanh_scalar(act, m, i)
        if i < 4:
            gate_scalar(act, m, ps, i)
    attend_out_scalar(act, m, ps, T - 1, 0)
    attend_probs_scalar(act, m, ps, T - 1, 1)
    attend_out_scalar(act, m, ps, T - 1, 1)


def heads_vector(dve, m, ps):
    T = m.T
    qk_low(dve, m, 0)
    for i in range(T):
        attend_k_vector(dve, m, ps, i)
        if i + 1 < T:
            qk_low(dve, m, i + 1)
        attend_max_vector(dve, m, ps, i, 0)
        attend_max_vector(dve, m, ps, i, 1)
        attend_divide_vector(dve, m, i, 0)
        attend_divide_vector(dve, m, i, 1)
        conv_vector(dve, m, i)
        silu_vector(dve, m, i)
        if i < 4:
            gate_vector(dve, m, ps, i)



B_S, B_T, B_N, B_C, B_Y = 0, 1, 2, 4, 6


def head_banks(ps, first):
    return ps[:, first:first + 2, 0:2 * NV].rearrange("p b (h e) -> p b h e", e=NV)


def out_weights_sync(sp, m, w_out, gate_rows):
    sp.wait_ge(m.pv, 2 * m.T)
    sp.wait_ge(m.ha_done, 4 * m.T)

    def rows(c):
        if c == 0:
            sp.wait_ge(m.g_stored, 16)
        if c >= 2:
            sp.wait_ge(m.qw_done, c - 1)
            sp.wait_ge(m.dm_done, c - 1)
            sp.wait_ge(m.dm_shift, c - 1)
        src = gate_rows.rearrange("(h c) a l -> c a h l", h=HEADS_M)[c]
        for a in range(2):
            sp.dma_start(m.bc[c % 2][:, a, :, :], src[a].unsqueeze(0).to_broadcast([P, HEADS_M, P]))\
              .then_inc(m.bc_loaded[c % 2], 16)

    rows(0)
    rows(1)
    for k in range(m.K):
        if k >= 2:
            sp.wait_ge(m.w_low, k - 1)
        sp.dma_start(m.wraw[k % 2][:, :], w_out[k * P:(k + 1) * P, :]).then_inc(m.w_loaded[k % 2], 16)
    for c in range(2, m.T):
        rows(c)


def out_weights_scalar(act, m, k):
    if k == 0:
        act.wait_ge(m.q_half, 2 * m.T)
    act.wait_ge(m.w_loaded[k % 2], 16 * (k // 2 + 1))
    act.activation(m.wo[0][:, k, :], m.wraw[k % 2][:, :], ACT.Copy).then_inc(m.w_high, 1)


def out_weights_vector(dve, m, k):
    dve.wait_ge(m.w_high, k + 1)
    part_low(dve, m.wo[1][:, k, :], m.wraw[k % 2][:, :], m.wo[0][:, k, :]).then_inc(m.w_low, 1)


def tile(m, h, c):
    return m.qk[:, h, c * P:(c + 1) * P]


def chunk_scores_tensor(pe, m, ps, ident, c):
    if c == 0:
        pe.wait_ge(m.qk_done, 2 * HEADS_M)
        pe.wait_ge(m.xp_ready, 2 * m.T)
    else:
        pe.wait_ge(m.kw_done, c)
    for h in range(HEADS_M):
        mm = pe.transpose(ps[:, B_T, h * P:(h + 1) * P], tile(m, HEADS_M + h, c), ident[:, :])
    mm.then_inc(m.k_done, 1)
    if c > 0:
        pe.wait_ge(m.sc_done, c)
    for h in range(HEADS_M):
        mm = pe.matmul(ps[:, B_S, h * P:(h + 1) * P], tile(m, HEADS_M + h, c), tile(m, h, c),
                       start=True, stop=True)
    mm.then_inc(m.s_done, 1)


def chunk_decay_vector(dve, m, causal, c):
    dve.wait_ge(m.bc_loaded[c % 2], 32 * (c // 2 + 1))
    if c == 0:
        dve.wait_ge(m.g_act, 4)
    else:
        dve.wait_ge(m.sc_done, c)
    for h in range(HEADS_M):
        r = h * m.T + c
        ins = dve.scalar_tensor_tensor(m.dm[:, h, :], m.bc[c % 2][:, 0, h, :], m.col[:, 0, r:r + 1],
                                       causal[:, :], ALU.add, ALU.min)
    ins.then_inc(m.dm_shift, 1)


def chunk_exps_scalar(act, m, ps, c):
    act.wait_ge(m.bc_loaded[c % 2], 32 * (c // 2 + 1))
    act.activation(m.bc[c % 2][:, 1, :, :], m.bc[c % 2][:, 1, :, :], ACT.Exp).then_inc(m.wg_done, 1)
    act.wait_ge(m.dm_shift, c + 1)
    act.activation(m.dm[:, :, :], m.dm[:, :, :], ACT.Exp).then_inc(m.dm_done, 1)
    act.wait_ge(m.k_done, c + 1)
    if c == 0:
        act.wait_ge(m.g_sb, 14)
    else:
        act.wait_ge(m.c_done, c)
    for h in range(HEADS_M):
        r = h * m.T + c
        ins = act.activation(m.kw[:, h, :], ps[:, B_T, h * P:(h + 1) * P], ACT.Copy, scale=m.col[:, 1, r:r + 1])
    ins.then_inc(m.kw_done, 1)


def chunk_weight_vector(dve, m, ps, c):
    dve.wait_ge(m.s_done, c + 1)
    dve.wait_ge(m.dm_done, c + 1)
    if c > 0:
        dve.wait_ge(m.n_done, c)
    dve.scalar_tensor_tensor(m.sc[:, :, :], ps[:, B_S, :].rearrange("p (h l) -> p h l", h=HEADS_M), QK_SCALE,
                             m.dm[:, :, :], ALU.mult, ALU.mult).then_inc(m.sc_done, 1)
    dve.wait_ge(m.wg_done, c + 1)
    dve.tensor_tensor(m.qw[:, :, :], m.qk[:, 0:HEADS_M, c * P:(c + 1) * P], m.bc[c % 2][:, 1, :, :], ALU.mult)\
       .then_inc(m.qw_done, 1)


def chunk_products_tensor(pe, m, ps, c):
    v = lambda h: m.tok[:, c, h * NV:(h + 1) * NV]
    pe.wait_ge(m.sc_done, c + 1)
    pe.wait_ge(m.qw_done, c + 1)
    if c == 0:
        pe.wait_ge(m.left[0], 3 * m.T // 2)
        pe.wait_ge(m.left[1], 3 * m.T // 2)
        pe.wait_ge(m.zeroed, m.zeros)
        pe.wait_ge(m.ha_done, 4 * m.T)
        pe.wait_ge(m.pt_ready, 2 * m.T)
        pe.wait_ge(m.exps, 2 * m.T)
    else:
        pe.wait_ge(m.state, c)
        pe.wait_ge(m.hm_norm, c)
    N, C = head_banks(ps, B_N), head_banks(ps, B_C)
    for h in range(HEADS_M):
        out = N[:, h // 2, h % 2, :]
        mm = pe.matmul(out, m.sc[:, h, :], v(h), start=True, stop=(c == 0))
        if c > 0:
            mm = pe.matmul(out, m.qw[:, h, :], m.C[(c - 1) % 2][:, h, :], start=False, stop=True)
    mm.then_inc(m.n_done, 1)
    pe.wait_ge(m.kw_done, c + 1)
    if c > 0:
        pe.wait_ge(m.hs_low, 2 * c)
    for h in range(HEADS_M):
        mm = pe.matmul(C[:, h // 2, h % 2, :], m.kw[:, h, :], v(h), start=True, stop=True)
    mm.then_inc(m.c_done, 1)


def chunk_state_vector(dve, m, ps, c):
    dve.wait_ge(m.c_done, c + 1)
    C = head_banks(ps, B_C)
    if c == 0:
        dve.wait_ge(m.g_act, 3)
        ins = dve.tensor_copy(m.C[0][:, :, :].rearrange("p (b h) e -> p b h e", b=2), C)
    else:
        for h in range(HEADS_M):
            r = h * m.T + c
            ins = dve.scalar_tensor_tensor(m.C[c % 2][:, h, :], m.C[(c - 1) % 2][:, h, :], m.dec[:, r:r + 1],
                                           C[:, h // 2, h % 2, :], ALU.mult, ALU.add)
    ins.then_inc(m.state, 1)


def chunk_stats_vector(dve, m, ps, c):
    then, sm = m.chain.then, m.sm
    N = head_banks(ps, B_N)
    dve.wait_ge(m.n_done, c + 1)
    pair = lambda x: x[:, :].rearrange("p (b h) -> p b h", b=2)
    if c > 0:
        dve.wait_ge(m.hm_norm, c)
    then(dve, dve.tensor_scalar(pair(sm["ad"]), N[:, :, :, P], -1.0, None, ALU.mult))
    then(dve, dve.tensor_tensor(pair(sm["ad"]), pair(sm["ad"]), N[:, :, :, P], ALU.max))
    emt = m.col[:, 2, :].rearrange("p (h t) -> p h t", h=HEADS_M)[:, :, c]
    then(dve, dve.tensor_tensor(sm["ad"][:, :], sm["ad"][:, :], emt, ALU.max))
    then(dve, dve.reciprocal(sm["r"][:, :], sm["ad"][:, :]))
    for h in range(HEADS_M):
        dve.bn_stats(m.bn[:, h, :], N[:, h // 2, h % 2, 0:P]).then_inc(m.chain.sem, 1)
        m.chain.count += 1
    dve.wait_ge(m.chain.sem, m.chain.count)
    for h in range(HEADS_M):
        dve.bn_aggr(m.mv[:, h, :], m.bn[:, h, :]).then_inc(m.chain.sem, 1)
        m.chain.count += 1
    dve.wait_ge(m.chain.sem, m.chain.count)
    then(dve, dve.tensor_tensor(sm["vr"][:, :], m.mv[:, :, 1], sm["r"][:, :], ALU.mult))
    then(dve, dve.tensor_tensor(sm["vr"][:, :], sm["vr"][:, :], sm["r"][:, :], ALU.mult))
    inverse_root(dve, m.chain, sm["rs"][:, :], sm["vr"][:, :], 1.0, EPS, sm["guess"][:, :],
                 sm["half"][:, :], sm["value"][:, :])
    then(dve, dve.tensor_tensor(sm["rs"][:, :], sm["rs"][:, :], sm["r"][:, :], ALU.mult))
    dve.scalar_tensor_tensor(sm["nb"][:, :], m.mv[:, :, 0], -1.0, sm["rs"][:, :], ALU.mult, ALU.mult)\
       .then_inc(m.norm_ready, 1)


def chunk_norm_scalar(act, m, ps, c):
    act.wait_ge(m.norm_ready, c + 1)
    if c > 0:
        act.wait_ge(m.hm_turned, c)
    N = head_banks(ps, B_N)
    for h in range(HEADS_M):
        ins = act.activation(m.hm[:, h, :], N[:, h // 2, h % 2, 0:P], ACT.Identity,
                             bias=m.sm["nb"][:, h:h + 1], scale=m.sm["rs"][:, h:h + 1])
    ins.then_inc(m.hm_norm, 1)


def chunk_gate_vector(dve, m, c):
    dve.wait_ge(m.hm_norm, c + 1)
    hm = m.hm[:, :, :].rearrange("p h v -> p (h v)")
    dve.tensor_tensor(hm, hm, m.tok[:, c, OG:OG + NO], ALU.mult).then_inc(m.hm_done, 1)


def chunk_turn_tensor(pe, m, ps, ident, c):
    pe.wait_ge(m.hm_done, c + 1)
    pe.wait_ge(m.state, c + 1)
    for h in range(HEADS_M):
        mm = pe.transpose(ps[:, B_C, h * P:(h + 1) * P], m.hm[:, h, :], ident[:, :])
    mm.then_inc(m.hm_turned, 1)


def out_in(m, ps, c):
    return (ps[:, B_C, :].rearrange("p (h l) -> p h l", h=HEADS_M),
            m.tok[:, c, AQ:AQ + NQ].rearrange("p (j q) -> p j q", j=4))


def out_high_scalar(act, m, ps, c):
    if c >= 2:
        act.wait_ge(m.y_done, c - 1)
    act.wait_ge(m.hm_turned, c + 1)
    for q, src in enumerate(out_in(m, ps, c)):
        act.activation(m.hs[c % 2][:, 0, 4 * q:4 * q + 4, :], src, ACT.Copy).then_inc(m.hs_high, 1)


def out_low_vector(dve, m, ps, c):
    for q, src in enumerate(out_in(m, ps, c)):
        dve.wait_ge(m.hs_high, 2 * c + q + 1)
        part_low(dve, m.hs[c % 2][:, 1, 4 * q:4 * q + 4, :], src, m.hs[c % 2][:, 0, 4 * q:4 * q + 4, :])\
           .then_inc(m.hs_low, 1)


def out_tensor(pe, m, ps, c):
    pe.wait_ge(m.hs_low, 2 * c + 2)
    if c == 0:
        pe.wait_ge(m.w_low, m.K)
    else:
        pe.wait_ge(m.y_scaled, c)
    hs = m.hs[c % 2]
    for n in range(2):
        for k in range(m.K):
            mm = three_passes(pe, ps[:, B_Y + n, :], [hs[:, a, k, :] for a in range(2)],
                              [w[:, k, n * BANK:(n + 1) * BANK] for w in m.wo], k == 0, k == m.K - 1)
    mm.then_inc(m.y_done, 1)


def out_sum_scalar(act, m, ps, c):
    act.wait_ge(m.y_done, c + 1)
    if c > 0:
        act.wait_ge(m.y_summed, c)
    act.activation(m.junk[:, :].rearrange("p (b c) -> p b c", c=BANK), ps[:, B_Y:B_Y + 2, :], ACT.Square,
                   accum_out=m.ssq[:, c:c + 1]).then_inc(m.y_summed, 1)


def out_scale_vector(dve, m, ps, c, D):
    dve.wait_ge(m.y_summed, c + 1)
    inverse_root(dve, m.chain, m.rstd[:, c:c + 1], m.ssq[:, c:c + 1], 1.0 / D, EPS, m.guess[:, 0:1],
                 m.half[:, 0:1], m.value[:, 0:1])
    if c == 0:
        dve.wait_ge(m.post_loaded, 16)
    dve.scalar_tensor_tensor(m.tok[:, c, 0:D], ps[:, B_Y:B_Y + 2, :].rearrange("p b c -> p (b c)"),
                             m.rstd[:, c:c + 1], m.gain_post[:, :], ALU.mult, ALU.mult).then_inc(m.y_scaled, 1)


def out_residual_pool(pool, m, c, res, out, D):
    if c > 0:
        pool.wait_ge(m.h_done, c)
    pool.dma_start(m.res[:, :], res[c * P:(c + 1) * P, :]).then_inc(m.res_loaded, 16)
    pool.wait_ge(m.y_scaled, c + 1)
    pool.wait_ge(m.res_loaded, 16 * (c + 1))
    h = m.tok[:, c, 0:D]
    pool.tensor_tensor(h, h, m.res[:, :], ALU.add).then_inc(m.h_done, 1)
    pool.wait_ge(m.h_done, c + 1)
    pool.dma_start(out[c * P:(c + 1) * P, :], h).then_inc(m.stored, 16)


def chunks_tensor(pe, m, ps, ident):
    chunk_scores_tensor(pe, m, ps, ident, 0)
    for c in range(m.T):
        chunk_products_tensor(pe, m, ps, c)
        if c + 1 < m.T:
            chunk_scores_tensor(pe, m, ps, ident, c + 1)
        if c:
            out_tensor(pe, m, ps, c - 1)
        chunk_turn_tensor(pe, m, ps, ident, c)
    out_tensor(pe, m, ps, m.T - 1)


def chunks_scalar(act, m, ps):
    chunk_exps_scalar(act, m, ps, 0)
    for c in range(m.T):
        chunk_norm_scalar(act, m, ps, c)
        if c + 1 < m.T:
            chunk_exps_scalar(act, m, ps, c + 1)
        if c == 0:
            for k in range(m.K):
                out_weights_scalar(act, m, k)
        else:
            out_sum_scalar(act, m, ps, c - 1)
        out_high_scalar(act, m, ps, c)
    out_sum_scalar(act, m, ps, m.T - 1)


def chunks_vector(dve, m, ps, causal, D):
    chunk_decay_vector(dve, m, causal, 0)
    chunk_weight_vector(dve, m, ps, 0)
    for c in range(m.T):
        chunk_stats_vector(dve, m, ps, c)
        chunk_state_vector(dve, m, ps, c)
        chunk_gate_vector(dve, m, c)
        if c + 1 < m.T:
            chunk_decay_vector(dve, m, causal, c + 1)
            chunk_weight_vector(dve, m, ps, c + 1)
        if c == 0:
            for k in range(m.K):
                out_weights_vector(dve, m, k)
        else:
            out_scale_vector(dve, m, ps, c - 1, D)
        out_low_vector(dve, m, ps, c)
    out_scale_vector(dve, m, ps, m.T - 1, D)



def bass_hymba_layer(nc, x, positions, ff1_pre_w, ff1_w_gate, ff1_w_up, ff1_w_down, ff1_post_w,
                     mix_pre_w, w_in, conv_w, conv_b, b_igate, b_fgate, mlstm_norm_w, sinks, w_out,
                     mix_post_w, ff2_pre_w, ff2_w_gate, ff2_w_up, ff2_w_down, ff2_post_w, out):
    _, S, D = x.shape
    F = ff1_w_gate.shape[2]
    T, K = S // P, D // P
    x, out = x[0], out[0]
    row = lambda w: w.to_broadcast([P, w.shape[1]])
    by_rows = lambda w: w[0].rearrange("(k p) f -> p k f", p=P)

    with ExitStack() as ctx:
        mem = Memory(nc, ctx)
        ps = ctx.enter_context(nc.psum_tensor("ps", [P, 8, BANK], F32))
        h1 = nc.dram_tensor("after_ff1", [S, D], F32, kind="Internal").ap()
        h2 = nc.dram_tensor("after_mixer", [S, D], F32, kind="Internal").ap()
        gate_rows = nc.dram_tensor("gate_rows", [HEADS_M * T, 2, P], F32, kind="Internal").ap()

        ident = mem.at("ident", [P, P], F32, 205 * KB)
        causal = mem.at("causal", [P, P], F32, 205 * KB + 512)
        xn = [mem.at("xn_high", [P, K, S], FR, 0), mem.at("xn_low", [P, K, S], FR, 32 * KB)]
        small = 206 * KB + 512
        root = [mem.at("root_guess", [P, T], I32, small), mem.at("root_half", [P, T], F32, small + 32),
                mem.at("root_value", [P, T], F32, small + 64)]
        sums = [[mem.at(f"ssq{i}", [P, T], F32, small + 96 + 64 * i),
                 mem.at(f"rstd{i}", [P, T], F32, small + 128 + 64 * i)] + root for i in range(6)]

        xt = mem.at("x_tiles", [P, T, D], F32, 64 * KB)
        xs1 = [mem.at(f"norm1_xs{i}", [P, D], F32, (96 + 4 * i) * KB) for i in range(2)]
        gain1 = mem.at("norm1_gain", [P, D], F32, 104 * KB)
        junk1 = mem.at("norm1_junk", [P, D], F32, 108 * KB)
        n1 = Norm(mem, "norm1", sums[0], xs1, junk1[:, :], gain1, [0, 1, 2, 3])
        x_loaded = [mem.sem(f"x_loaded{t}") for t in range(T)]
        gain1_loaded = mem.sem("norm1_gain_loaded")
        set_up = mem.sem("constants_set")

        f1 = FeedForward(mem, "ff1", D, F, S)
        f1.ssq, f1.rstd, f1.guess, f1.half, f1.value = sums[1]
        f1.gains = 32
        nm = Norm(mem, "norm_mix", sums[2], [f1.res], None, f1.gain_pre, [6, 7])

        m = Mixer(mem, S, D)
        m.ssq, m.rstd, m.guess, m.half, m.value = sums[3]
        m.zeros, m.consts = 2, 16 * (CONV + 1 + 2 + 3)

        xs2 = [mem.at(f"norm2_xs{i}", [P, D], F32, int((112.25 + 4 * i) * KB)) for i in range(2)]
        junk2 = mem.at("norm2_junk", [P, D], F32, int(120.25 * KB))
        gain2 = mem.at("norm2_gain", [P, D], F32, int(168.75 * KB))
        n2 = Norm(mem, "norm2", sums[4], xs2, junk2[:, :], gain2, [0, 1, 2, 3])
        gain2_loaded = mem.sem("norm2_gain_loaded")
        f2 = FeedForward(mem, "ff2", D, F, S)
        f2.ssq, f2.rstd, f2.guess, f2.half, f2.value = sums[5]
        f2.gains = 16

        x_tiles = [xt[:, t, :] for t in range(T)]
        h_tiles = [m.tok[:, t, 0:D] for t in range(T)]
        block = ctx.enter_context(nc.Block())

        @block.sync
        def _(sp):
            gate_up_sync(sp, f1, [by_rows(ff1_w_gate), by_rows(ff1_w_up)])
            down_sync(sp, f1, ff1_w_down[0])
            sp.wait_ge(f1.unit_done, 2 * len(GROUPS) * (F // P))
            tokens_sync(sp, m, w_in[0], f1)
            qk_sync(sp, m, w_in[0])
            out_weights_sync(sp, m, w_out[0], gate_rows)
            sp.wait_ge(m.y_done, T)
            sp.wait_ge(m.y_scaled, T)
            sp.wait_ge(m.h_done, T)
            gate_up_sync(sp, f2, [by_rows(ff2_w_gate), by_rows(ff2_w_up)])
            down_sync(sp, f2, ff2_w_down[0])

        @block.gpsimd
        def _(pool):
            pool.dma_start(gain1[:, :], row(ff1_pre_w)).then_inc(gain1_loaded, 16)
            pool.memset(ident[:, :], 0.0).then_inc(set_up, 1)
            pool.memset(causal[:, :], 0.0).then_inc(set_up, 1)
            pool.wait_ge(set_up, 2)
            pool.affine_select(out=ident[:, :], in_=ident[:, :], compare_op=ALU.not_equal, fill=1.0,
                               base=0, pattern=[[-1, P]], channel_multiplier=1).then_inc(set_up, 1)
            pool.affine_select(out=causal[:, :], in_=causal[:, :], compare_op=ALU.is_ge, fill=-BIG,
                               base=0, pattern=[[1, P]], channel_multiplier=-1).then_inc(set_up, 1)
            with nc.allow_non_contiguous_dma(reason="a few KB of per-feature constants"):
                for j in range(CONV):
                    pool.dma_start(m.conv_w[:, j, :], conv_w[0, j].rearrange("(f p) -> p f", p=P))\
                        .then_inc(m.consts_loaded, 16)
                pool.dma_start(m.conv_b[:, :], conv_b[0].rearrange("(f p) -> p f", p=P))\
                    .then_inc(m.consts_loaded, 16)
                for e in range(2):
                    pool.dma_start(m.sink[64 * e:64 * e + 64, :],
                                   sinks.rearrange("a (j e) -> a e j", e=2)[:, e, :].to_broadcast([64, 4]))\
                        .then_inc(m.consts_loaded, 16)
            pool.wait_ge(f1.h_done, F // P)
            pool.dma_start(f1.gain_post[:, :], row(ff1_post_w)).then_inc(f1.gains_loaded, 16)
            pool.dma_start(f1.gain_pre[:, :], row(mix_pre_w)).then_inc(f1.gains_loaded, 16)
            down_pool(pool, f1, x, h1, nm)

            pool.wait_ge(f1.unit_done, 2 * len(GROUPS) * (F // P))
            pool.dma_start(m.gain_norm[:, :], row(mlstm_norm_w.rearrange("a h d -> a (h d)")))\
                .then_inc(m.consts_loaded, 16)
            with nc.allow_non_contiguous_dma(reason="positions and gate biases"):
                pool.dma_start(m.pos_i[:, :], positions[0].rearrange("(t p) -> p t", p=P))\
                    .then_inc(m.pos_loaded, 16)
                for g, b in enumerate((b_igate, b_fgate)):
                    pool.dma_start(m.gbias[:, g, :], row(b)).then_inc(m.consts_loaded, 16)
            pool.memset(m.tok[:, :, 0:HEADS_M * NV].rearrange("p t (h e) -> p t h e", e=NV)[:, :, :, P], 1.0)\
                .then_inc(m.zeroed, 1)
            pool.memset(m.qbd[:, :, :, :], 0.0).then_inc(m.zeroed, 1)
            for i in range(T):
                shifted_values_pool(pool, m, i)
            pool.wait_ge(m.g_sb, GATE_DVE[-1])
            pool.dma_start(gate_rows, m.gout[:, :, :]).then_inc(m.g_stored, 16)
            pool.wait_ge(m.xp_ready, 2 * T)
            pool.wait_ge(m.qk_done, T)
            pool.wait_ge(m.pt_ready, 2 * T)
            pool.wait_ge(m.pv, 2 * T)
            pool.dma_start(m.gain_post[:, :], row(mix_post_w)).then_inc(m.post_loaded, 16)
            pool.wait_ge(m.g_stored, 16)
            pool.wait_ge(m.g_act, GATE_ACT[-1])
            pool.dma_start(gain2[:, :], row(ff2_pre_w)).then_inc(gain2_loaded, 16)
            pool.wait_ge(f1.stored, 16 * T)
            for c in range(T):
                out_residual_pool(pool, m, c, h1, h2, D)

            pool.wait_ge(m.stored, 16 * T)
            pool.wait_ge(f2.h_done, F // P)
            pool.dma_start(f2.gain_post[:, :], row(ff2_post_w)).then_inc(f2.gains_loaded, 16)
            down_pool(pool, f2, h2, out, None)
            pool.wait_ge(f2.stored, 16 * T)

        @block.scalar
        def _(act):
            for t in range(T):
                act.dma_start(xt[:, t, :], x[t * P:(t + 1) * P, :]).then_inc(x_loaded[t], 16)
            norm_all_scalar(act, n1, ps, xn, x_tiles, lambda e, t: e.wait_ge(x_loaded[t], 16))
            gate_up_scalar(act, f1, ps)
            down_scalar(act, f1, ps, nm, xn)
            tokens_scalar(act, m, ps)
            heads_scalar(act, m, ps)
            chunks_scalar(act, m, ps)
            act.wait_ge(m.y_done, T)
            norm_all_scalar(act, n2, ps, xn, h_tiles, lambda e, t: e.wait_ge(m.h_done, t + 1))
            gate_up_scalar(act, f2, ps)
            down_scalar(act, f2, ps, None, xn)

        @block.vector
        def _(dve):
            norm_all_vector(dve, n1, ps, xn, x_tiles, lambda e: e.wait_ge(gain1_loaded, 16), D)
            gate_up_vector(dve, f1, ps)
            down_vector(dve, f1, ps, nm, xn, D, 0.5)
            tokens_vector(dve, m, ps)
            dve.wait_ge(f1.stored, 16 * T)
            m.chain.then(dve, dve.memset(m.xp[:, 0:3], 0.0))
            heads_vector(dve, m, ps)
            dve.wait_ge(set_up, 4)
            chunks_vector(dve, m, ps, causal, D)
            norm_all_vector(dve, n2, ps, xn, h_tiles, lambda e: e.wait_ge(gain2_loaded, 16), D)
            dve.wait_ge(m.stored, 16 * T)
            gate_up_vector(dve, f2, ps)
            down_vector(dve, f2, ps, None, xn, D, 0.5)

        @block.tensor
        def _(pe):
            pe.wait_ge(set_up, 4)
            for t in range(T):
                turn_tile(pe, n1, ps, ident, t, K)
            pe.wait_ge(n1.low, 2 * T)
            gate_up_tensor(pe, f1, ps, xn)
            down_tensor(pe, f1, ps, nm, ident)
            pe.wait_ge(nm.low, 2 * T)
            pe.wait_ge(f1.y_act, T)
            pe.wait_ge(f1.y_dve, T)
            tokens_tensor(pe, m, ps, xn)
            heads_tensor(pe, m, ps, xn, ident, m.gout[:, 0, :])
            chunks_tensor(pe, m, ps, ident)
            for t in range(T):
                turn_tile(pe, n2, ps, ident, t, K)
            pe.wait_ge(n2.low, 2 * T)
            gate_up_tensor(pe, f2, ps, xn)
            down_tensor(pe, f2, ps, None, ident)


_INS = ['x', 'positions', 'ff1_pre_w', 'ff1_w_gate', 'ff1_w_up', 'ff1_w_down', 'ff1_post_w', 'mix_pre_w',
        'w_in', 'conv_w', 'conv_b', 'b_igate', 'b_fgate', 'mlstm_norm_w', 'sinks', 'w_out', 'mix_post_w',
        'ff2_pre_w', 'ff2_w_gate', 'ff2_w_up', 'ff2_w_down', 'ff2_post_w']


def kernel(**inputs):
    import numpy as _np
    import concourse.bacc as _bacc
    from concourse import mybir as _mybir
    from concourse.bass_utils import run_bass_kernel_spmd as _run

    nc = _bacc.Bacc("TRN2", target_bir_lowering=False, num_devices=1)
    arrays, args = {}, []
    for name in _INS:
        a = _np.ascontiguousarray(inputs[name])
        arrays[f"in_{name}_dram"] = a
        args.append(nc.dram_tensor(f"in_{name}_dram", a.shape, _mybir.dt.from_np(a.dtype), kind="ExternalInput").ap())
    out = nc.dram_tensor("out_dram", inputs["x"].shape, _mybir.dt.float32, kind="ExternalOutput").ap()
    bass_hymba_layer(nc, *args, out)
    r = _run(nc, [arrays], core_ids=[0])
    return r.results[0]["out_dram"]
```

```python
from contextlib import ExitStack

import concourse.bass as bass
import numpy as np
from concourse import mybir

P = 128
F32 = mybir.dt.float32
FR = mybir.dt.float32r
BF = mybir.dt.bfloat16
I32 = mybir.dt.int32
ALU = mybir.AluOpType
ACT = mybir.ActivationFunctionType
AX = mybir.AxisListType.X
BANK = 512
KB = 1024
EPS = 1e-6


class Memory:

    def __init__(self, nc, ctx):
        self.nc, self.ctx = nc, ctx
        self.base = (nc.sbuf_base + 31) // 32 * 32

    def at(self, name, shape, dtype, offset):
        return self.nc.alloc_sbuf_tensor_at(name, shape, dtype, offset=self.base + offset)

    def sem(self, name):
        return self.ctx.enter_context(self.nc.semaphore(name))


class Chain:

    def __init__(self, mem, name):
        self.sem, self.count = mem.sem(name), 0

    def then(self, engine, instruction):
        instruction.then_inc(self.sem, 1)
        self.count += 1
        engine.wait_ge(self.sem, self.count)


def inverse_root(dve, chain, out, total, scale, bias, guess, half, value):
    step = lambda instruction: chain.then(dve, instruction)
    step(dve.tensor_scalar(value, total, -0.5 * scale, -0.5 * bias, ALU.mult, ALU.add))
    step(dve.tensor_scalar(guess, value.bitcast(I32), 1, None, ALU.arith_shift_right))
    step(dve.tensor_scalar(guess, guess, -1.0, float(0x5F3759DF - 2 ** 30 - 2 ** 22), ALU.mult, ALU.add))
    y = guess.bitcast(F32)
    for last in (False, False, True):
        if out.shape[1] == 1:
            step(dve.scalar_tensor_tensor(half, y, value, y, ALU.mult, ALU.mult))
        else:
            step(dve.tensor_tensor(half, y, y, ALU.mult))
            step(dve.tensor_tensor(half, half, value, ALU.mult))
        step(dve.scalar_tensor_tensor(out if last else y, half, 1.5, y, ALU.add, ALU.mult))


class Norm:

    def __init__(self, mem, name, sums, xs, junk, gain, banks):
        self.xs, self.junk, self.gain, self.banks = xs, junk, gain, banks
        self.ssq, self.rstd, self.guess, self.half, self.value = sums
        self.summed = mem.sem(f"{name}_squares_summed")
        self.xs_ready = mem.sem(f"{name}_xs_ready")
        self.turned = mem.sem(f"{name}_turned")
        self.high = mem.sem(f"{name}_high_written")
        self.low = mem.sem(f"{name}_low_written")
        self.chain = Chain(mem, f"{name}_dve_step")


class FeedForward:

    def __init__(self, mem, name, D, F, S, xn, norm_follows):
        at = lambda n, shape, dt, kb: mem.at(f"{name}_{n}", shape, dt, int(kb * KB))
        s = lambda n: mem.sem(f"{name}_{n}")
        K, FT = D // P, F // P
        self.name = name
        self.h = at("h", [P, FT, S], F32, 64)
        self.raw = [at(f"raw_{m}", [P, K, P], F32, 152 + 4 * i) for i, m in enumerate(("gate", "up"))]
        self.part = [[at(f"part_{m}{b}", [P, 2, K, P], FR, 160 + 16 * b + 8 * i)
                      for i, m in enumerate(("gate", "up"))] for b in range(2)]
        self.silu = at("silu", [P, S], F32, 192)
        self.raw_loaded = [s("gate_loaded"), s("up_loaded")]
        self.w_high = s("gate_up_high")
        self.w_low = s("gate_up_low")
        self.gate_done, self.up_done = s("gate_done"), s("up_done")
        self.silu_done, self.h_done = s("silu_done"), s("h_done")
        own = at("down_part", [P, 2, D // 256, 256], FR, 152)
        tail = slice(S - 256, S)
        self.dpart = [[own[:, a, :, :] for a in range(2)]] + \
            [[x[:, 4 * b:4 * b + 4, tail] for x in xn] for b in range(2)]
        self.hpart = [at(f"h_part{b}", [P, 2, 3 * P], FR, 160 + 3 * b) for b in range(3)]
        self.y = at("y", [P, 3, D], F32, 169)
        self.gain_post = at("gain_post", [P, D], F32, 185)
        gain_pre = at("gain_pre", [P, D], F32, 189)
        self.res = [at("res", [P, D], F32, 181)]
        if norm_follows:
            self.gain_pre = gain_pre
        else:
            self.res.append(gain_pre)
        self.draw = [at(f"down_raw{b}", [P, D], F32, kb) for b, kb in enumerate((197, 201, 193))]
        self.draw_loaded = [s(f"down_loaded{b}") for b in range(3)]
        self.d_high, self.d_low = s("down_high"), s("down_low")
        self.hp_high, self.hp_low = s("h_part_high"), s("h_part_low")
        self.unit_done, self.tile_done = s("down_unit_done"), s("down_tile_done")
        self.y_act, self.y_dve = s("y_left_by_act"), s("y_left_by_dve")
        self.gains_loaded = s("gains_loaded")
        self.y_summed = s("y_squares_summed")
        self.res_loaded = [s(f"residual_loaded{i}") for i in range(len(self.res))]
        self.y_final = s("y_final")
        self.stored = s("stored")
        self.chain = Chain(mem, f"{name}_dve_step")


def part_low(dve, low, value, high):
    return dve.tensor_tensor(low, value, high.bitcast(F32), ALU.subtract)



def turn_tile(pe, nm, ps, ident, t, K):
    pe.wait_ge(nm.xs_ready, t + 1)
    for q in range(2):
        bank = nm.banks[2 * t + q]
        before = [j for j in range(2 * t + q) if nm.banks[j] == bank]
        if before:
            pe.wait_ge(nm.low, before[-1] + 1)
        for j in range(K // 2):
            k = q * (K // 2) + j
            mm = pe.transpose(ps[:, bank, j * P:(j + 1) * P], nm.xs[t][:, k * P:(k + 1) * P], ident[:, :])
        mm.then_inc(nm.turned, 1)


def high_tile(act, nm, ps, xn, t):
    for q in range(2):
        act.wait_ge(nm.turned, 2 * t + q + 1)
        bank = nm.banks[2 * t + q]
        act.activation(xn[0][:, 4 * q:4 * q + 4, t * P:(t + 1) * P],
                       ps[:, bank, :].rearrange("p (k c) -> p k c", c=P), ACT.Copy).then_inc(nm.high, 1)


def low_tile(dve, nm, ps, xn, t):
    for q in range(2):
        dve.wait_ge(nm.high, 2 * t + q + 1)
        bank = nm.banks[2 * t + q]
        at = (slice(None), slice(4 * q, 4 * q + 4), slice(t * P, (t + 1) * P))
        part_low(dve, xn[1][at], ps[:, bank, :].rearrange("p (k c) -> p k c", c=P),
                 xn[0][at]).then_inc(nm.low, 1)


def scale_tile(dve, nm, t, tile):
    before = [j for j in range(t) if nm.xs[j] is nm.xs[t]]
    if before:
        dve.wait_ge(nm.turned, 2 * before[-1] + 2)
    halves = lambda x: x.rearrange("p (a c) -> p a c", a=nm.gain.shape[1])
    dve.scalar_tensor_tensor(halves(nm.xs[t]), halves(tile), nm.rstd[:, t:t + 1], nm.gain,
                             ALU.mult, ALU.mult).then_inc(nm.xs_ready, 1)


def norm_roots(dve, nm, a, b, D):
    dve.wait_ge(nm.summed, b)
    w = slice(0, b - a)
    inverse_root(dve, nm.chain, nm.rstd[:, a:b], nm.ssq[:, a:b], 1.0 / D, EPS,
                 nm.guess[:, w], nm.half[:, w], nm.value[:, w])


def norm_square(act, nm, t, tile):
    if t > 0:
        act.wait_ge(nm.summed, t)
    act.activation(nm.junk, tile, ACT.Square, accum_out=nm.ssq[:, t:t + 1]).then_inc(nm.summed, 1)



def square_tiles(act, nm, tiles, ready, *which):
    for t in which:
        ready(act, t)
        norm_square(act, nm, t, tiles[t])


def start_scalar(act, nm, ps, xn, tiles, ready, s, up_free=None, high_from=0, squared=0):
    def square(*ts):
        square_tiles(act, nm, tiles, ready, *(t for t in ts if t >= squared))

    def high(*ts):
        for t in ts:
            if t >= high_from:
                high_tile(act, nm, ps, xn, t)

    square(0, 1, 2, 3)
    high(0)
    gate_up_high(act, s, 0, 0, True, 0)
    high(1, 2)
    square(4)
    high(3)
    if up_free:
        up_free(act)
    gate_up_high(act, s, 0, 0, True, 1)
    square(5, 6, 7)
    high(4, 5, 6, 7)


def start_vector(dve, nm, ps, xn, tiles, gain_ready, D, s, scalable=None, between=None):
    def scale(*ts):
        for t in ts:
            if t % 2 == 0:
                norm_roots(dve, nm, t, t + 2, D)
            if t == 0:
                gain_ready(dve)
            if scalable:
                scalable(dve, t)
            scale_tile(dve, nm, t, tiles[t])

    def low(t):
        low_tile(dve, nm, ps, xn, t)

    for first in (0, 4):
        scale(first, first + 1)
        for t in (first, first + 1):
            low(t)
            scale(t + 2)
        low(first + 2)
        if first == 0:
            gate_up_low(dve, s, 0, 0, 0)
        low(first + 3)
        if first == 0:
            if between:
                between()
            gate_up_low(dve, s, 0, 0, 1)


def start_tensor(pe, nm, ps, ident, s, xn, T, K, turned=0):
    half = T // 2
    for t in range(turned, half):
        turn_tile(pe, nm, ps, ident, t, K)
    for th in range(2):
        for m in range(2):
            pe.wait_ge(nm.low, T * (th + 1))
            pe.wait_ge(s.w_low, m + 1)
            mm = gate_up_products(pe, s, ps, xn, 0, m, th)
            if th == 1:
                mm.then_inc((s.gate_done, s.up_done)[m], 1)
            else:
                for t in range(half + half // 2 * m, half + half // 2 * (m + 1)):
                    turn_tile(pe, nm, ps, ident, t, K)



def gate_up_sync(sp, s, weights, first):
    def load(f, fresh):
        for m, w in enumerate(weights):
            if not fresh:
                sp.wait_ge(s.w_low, 2 * f - 1 + m)
            sp.dma_start(s.raw[m][:, :, :], w[:, :, bass.ds(f * P, P)]).then_inc(s.raw_loaded[m], 16)

    if first:
        load(0, True)
    else:
        with sp.Fori(1, s.h.shape[1]) as f:
            load(f, False)


def gate_up_high(act, s, f, b, first, only=None):
    done = (s.gate_done, s.up_done)
    for m in range(2) if only is None else (only,):
        act.wait_ge(s.raw_loaded[m], 16 * f + 16)
        if not first:
            act.wait_ge(done[m], f - 1)
        act.activation(s.part[b][m][:, 0, :, :], s.raw[m][:, :, :], ACT.Copy).then_inc(s.w_high, 1)


def gate_up_low(dve, s, f, b, only=None):
    for m in range(2) if only is None else (only,):
        dve.wait_ge(s.w_high, 2 * f + m + 1)
        part_low(dve, s.part[b][m][:, 1, :, :], s.raw[m][:, :, :],
                 s.part[b][m][:, 0, :, :]).then_inc(s.w_low, 1)


def gate_up_silu(act, s, ps, f, b, first):
    act.wait_ge(s.gate_done, f + 1)
    if not first:
        act.wait_ge(s.h_done, f)
    act.activation(s.silu[:, :].rearrange("p (a c) -> p a c", c=BANK), ps[:, 4 * b:4 * b + 2, :],
                   ACT.Silu).then_inc(s.silu_done, 1)


def gate_up_product(dve, s, ps, f, b):
    dve.wait_ge(s.silu_done, f + 1)
    dve.wait_ge(s.up_done, f + 1)
    S = s.h.shape[2]
    dve.tensor_tensor(s.h[:, f, :] if isinstance(f, int) else s.h[:, bass.ds(f, 1), :].rearrange("p a s -> p (a s)"),
                      s.silu[:, :], ps[:, 4 * b + 2:4 * b + 4, :].rearrange("p a c -> p (a c)"),
                      ALU.mult).then_inc(s.h_done, 1)


def gate_up_scalar(act, s, ps):
    FT = s.h.shape[1]
    gate_up_high(act, s, 1, 1, True)
    gate_up_silu(act, s, ps, 0, 0, True)
    with act.Fori(1, FT - 1, 2) as f:
        for q in range(2):
            gate_up_high(act, s, f + (q + 1), q, False)
            gate_up_silu(act, s, ps, f + q, 1 - q, False)
    gate_up_silu(act, s, ps, FT - 1, 1, False)


def gate_up_vector(dve, s, ps):
    FT = s.h.shape[1]
    gate_up_low(dve, s, 1, 1)
    gate_up_product(dve, s, ps, 0, 0)
    with dve.Fori(1, FT - 1, 2) as f:
        for q in range(2):
            gate_up_low(dve, s, f + (q + 1), q)
            gate_up_product(dve, s, ps, f + q, 1 - q)
    gate_up_product(dve, s, ps, FT - 1, 1)


def three_passes(pe, out, a, b, start, stop):
    for q, (i, j) in enumerate(((0, 0), (0, 1), (1, 0))):
        mm = pe.matmul(out, a[i], b[j], start=start and q == 0, stop=stop and q == 2)
    return mm


def gate_up_products(pe, s, ps, xn, b, m, th):
    K, w = s.part[0][0].shape[2], s.part[b][m]
    for k in range(K):
        mm = three_passes(pe, ps[:, 4 * b + 2 * m + th, :], [w[:, i, k, :] for i in range(2)],
                          [x[:, k, th * BANK:(th + 1) * BANK] for x in xn], k == 0, k == K - 1)
    return mm


def gate_up_tensor(pe, s, ps, xn):
    def tile(f, b, first):
        for m, (done, free) in enumerate(((s.gate_done, s.silu_done), (s.up_done, s.h_done))):
            pe.wait_ge(s.w_low, 2 * f + m + 1)
            if not first:
                pe.wait_ge(free, f - 1)
            for th in range(2):
                mm = gate_up_products(pe, s, ps, xn, b, m, th)
            mm.then_inc(done, 1)

    tile(1, 1, True)
    with pe.Fori(2, s.h.shape[1], 2) as f:
        for q in range(2):
            tile(f + q, q, False)



GROUPS = [(0, 2), (2, 3), (5, 3)]
RING = 3


def down_sync(sp, s, w_down):
    FT = s.h.shape[1]

    def load(g, i, c):
        v = FT * g + c
        if not (isinstance(i, int) and v < RING):
            sp.wait_ge(s.d_low, 3 * i + (v - RING + 1))
        elif v == RING - 1:
            sp.wait_ge(s.h_done, FT)
        sp.dma_start(s.draw[v % RING][:, :], w_down[bass.ds((3 * i + c) * P, P), :])\
          .then_inc(s.draw_loaded[v % RING], 16)

    for g in range(len(GROUPS)):
        for c in range(4):
            load(g, 0, c)
        with sp.Fori(1, FT // 3) as i:
            for c in range(1, 4):
                load(g, i, c)


def h_tile(s, g, i, c):
    t0, n = GROUPS[g]
    f = 3 * i + c
    if isinstance(f, int):
        return s.h[:, f, t0 * P:(t0 + n) * P]
    return s.h[:, bass.ds(f, 1), t0 * P:(t0 + n) * P].rearrange("p a s -> p (a s)")


def down_high(act, s, g, i, c):
    v, n = s.h.shape[1] * g + c, GROUPS[g][1]
    if v >= RING or not isinstance(i, int):
        act.wait_ge(s.unit_done, 3 * i + (v - RING + 1))
    act.activation(s.hpart[v % RING][:, 0, 0:n * P], h_tile(s, g, i, c), ACT.Copy).then_inc(s.hp_high, 1)
    act.wait_ge(s.draw_loaded[v % RING], 16 * i + 16 * (v // RING + 1))
    high = s.dpart[v % RING][0]
    act.activation(high, s.draw[v % RING][:, :].rearrange("p (a c) -> p a c", c=high.shape[2]),
                   ACT.Copy).then_inc(s.d_high, 1)


def down_low(dve, s, g, i, c):
    v, n = s.h.shape[1] * g + c, GROUPS[g][1]
    hp, (high, low) = s.hpart[v % RING], s.dpart[v % RING]
    dve.wait_ge(s.hp_high, 3 * i + v + 1)
    part_low(dve, hp[:, 1, 0:n * P], h_tile(s, g, i, c), hp[:, 0, 0:n * P]).then_inc(s.hp_low, 1)
    dve.wait_ge(s.d_high, 3 * i + v + 1)
    part_low(dve, low, s.draw[v % RING][:, :].rearrange("p (a c) -> p a c", c=high.shape[2]),
             high).then_inc(s.d_low, 1)


def products(pe, s, ps, g, i, c, k):
    v = s.h.shape[1] * g + c
    hp, dp = s.hpart[v % RING], s.dpart[v % RING]
    half = dp[0].shape[1] // 2
    for n in range(2):
        if c == 0 and g > 0 and k < GROUPS[g - 1][1]:
            pe.wait_ge((s.y_act, s.y_dve)[n], GROUPS[g - 1][0] + k + 1)
        elif c == 0 and g > 0 and k == 2 and n == 0:
            pe.wait_ge(s.silu_done, s.h.shape[1])
        mm = three_passes(pe, ps[:, 2 * k + n, :].rearrange("p (a c) -> p a c", a=half),
                          [hp[:, a, k * P:(k + 1) * P] for a in range(2)],
                          [w[:, n * half:(n + 1) * half, :] for w in dp],
                          c == 0, isinstance(i, int) and 3 * i + c == s.h.shape[1] - 1)
    return mm


def down_products(pe, s, ps, g, i, c):
    v = s.h.shape[1] * g + c
    pe.wait_ge(s.hp_low, 3 * i + v + 1)
    pe.wait_ge(s.d_low, 3 * i + v + 1)
    last = isinstance(i, int) and 3 * i + c == s.h.shape[1] - 1
    for k in range(GROUPS[g][1]):
        mm = products(pe, s, ps, g, i, c, k)
        if last and k < GROUPS[g][1] - 1:
            mm.then_inc(s.tile_done, 1)
    mm.then_inc(s.unit_done, 1)


def down_last_units(pe, s, ps):
    g, FT = len(GROUPS) - 1, s.h.shape[1]
    n = GROUPS[g][1]
    for k in range(n):
        for f in range(FT - RING, FT):
            pe.wait_ge(s.hp_low, FT * g + f + 1)
            pe.wait_ge(s.d_low, FT * g + f + 1)
            mm = products(pe, s, ps, g, 0, f, k)
            if k == n - 1:
                mm.then_inc(s.unit_done, 1)
        if k < n - 1:
            mm.then_inc(s.tile_done, 1)


def wait_tile(eng, s, g, k):
    if k < GROUPS[g][1] - 1:
        eng.wait_ge(s.tile_done, sum(n - 1 for _, n in GROUPS[:g]) + k + 1)
    else:
        eng.wait_ge(s.unit_done, s.h.shape[1] * (g + 1))


def y_free(eng, s, nm, g):
    if g > 0:
        eng.wait_ge(s.stored, 16 * GROUPS[g][0])
        if nm:
            eng.wait_ge(nm.turned, 2 * GROUPS[g][0])


def leave_scalar(act, s, ps, g, k):
    wait_tile(act, s, g, k)
    act.activation(s.y[:, k, 0:BANK], ps[:, 2 * k, :], ACT.Copy).then_inc(s.y_act, 1)


def leave_vector(dve, s, ps, g, k):
    wait_tile(dve, s, g, k)
    dve.tensor_copy(s.y[:, k, BANK:2 * BANK], ps[:, 2 * k + 1, :]).then_inc(s.y_dve, 1)


def in_banks(ps):
    return ps[:, 6:8, :].rearrange("p b c -> p (b c)")


def y_square_scalar(act, s, g, k, nm, junk, summed_next=0):
    t = GROUPS[g][0] + k
    if t == 0:
        act.wait_ge(s.h_done, s.h.shape[1])
    act.wait_ge(s.y_dve, t + 1)
    act.wait_ge(s.y_act, t + 1)
    if t > 0:
        act.wait_ge(s.y_summed, t)
    if nm and k == 0 and g > 0:
        act.wait_ge(nm.summed, t)
        act.wait_ge(nm.low, 2 * t)
    if nm and summed_next:
        act.wait_ge(nm.summed, summed_next)
    act.activation(junk, s.y[:, k, :], ACT.Square,
                   accum_out=s.ssq[:, t:t + 1]).then_inc(s.y_summed, 1)


def y_roots(dve, s, a, b, D, factor):
    dve.wait_ge(s.y_summed, b)
    w = slice(0, b - a)
    inverse_root(dve, s.chain, s.rstd[:, a:b], s.ssq[:, a:b], factor ** -2 / D,
                 EPS * factor ** -2, s.guess[:, w], s.half[:, w], s.value[:, w])


def residual_vector(dve, s, g, k, y=None):
    t = GROUPS[g][0] + k
    if t == 0:
        dve.wait_ge(s.gains_loaded, s.gains)
    s.chain.then(dve, dve.scalar_tensor_tensor(s.y[:, k, :], s.y[:, k, :] if y is None else y,
                                               s.rstd[:, t:t + 1], s.gain_post[:, :], ALU.mult, ALU.mult))
    dve.wait_ge(s.res_loaded[t % len(s.res)], 16 * (t // len(s.res) + 1))
    dve.tensor_tensor(s.y[:, k, :], s.y[:, k, :], s.res[t % len(s.res)][:, :], ALU.add)\
       .then_inc(s.y_final, 1)


def square_scalar(act, s, nm, g, k, summed, junk):
    t = GROUPS[g][0] + k
    act.wait_ge(s.y_final, t + 1)
    act.wait_ge(s.y_summed, max(summed, t + 1))
    if t > 0:
        act.wait_ge(nm.summed, t)
    act.activation(junk, s.y[:, k, :], ACT.Square,
                   accum_out=nm.ssq[:, t:t + 1]).then_inc(nm.summed, 1)


Y_SQUARE, Y_ROOTS, RESIDUAL, SQUARE, ROOTS, SCALE, TURN, PARTS = (
    (2, 3, 4), 5, (5, 7, 9), (6, 8, 10), 11, (11, 14, 17), (12, 15, 18), (14, 17, 20))


def scale_y(dve, s, nm, t, k):
    dve.wait_ge(s.stored, 16 * (t + 1))
    scale_tile(dve, nm, t, s.y[:, k, :])


def steps_scalar(act, s, ps, nm, xn, g, f):
    t0, n = GROUPS[g]
    for k in range(n):
        if f == Y_SQUARE[k]:
            y_square_scalar(act, s, g, k, nm, in_banks(ps))
        if nm and f == SQUARE[k]:
            square_scalar(act, s, nm, g, k, t0 + n, in_banks(ps))
        if nm and f == PARTS[k]:
            high_tile(act, nm, ps, xn, t0 + k)


def steps_vector(dve, s, ps, nm, xn, g, f, D, factor):
    t0, n = GROUPS[g]
    if f == Y_ROOTS:
        y_roots(dve, s, t0, t0 + n, D, factor)
    if nm and f == ROOTS:
        norm_roots(dve, nm, t0, t0 + n, D)
    for k in range(n):
        if f == RESIDUAL[k]:
            residual_vector(dve, s, g, k)
        if nm and f == PARTS[k]:
            low_tile(dve, nm, ps, xn, t0 + k)
        if nm and f == SCALE[k]:
            scale_y(dve, s, nm, t0 + k, k)


def steps_tensor(pe, s, ps, nm, ident, g, f):
    for k in range(GROUPS[g][1]):
        if nm and f == TURN[k]:
            turn_tile(pe, nm, ps, ident, GROUPS[g][0] + k, s.y.shape[2] // P)



def tail_scalar(act, s, ps, nm, xn, u):
    g = len(GROUPS) - 1
    t0, n = GROUPS[g]
    junk = s.draw[0][:, :]
    if u == RING:
        act.wait_ge(s.d_low, len(GROUPS) * s.h.shape[1])
        y_free(act, s, nm, g)
        for k in range(n):
            leave_scalar(act, s, ps, g, k)
            y_square_scalar(act, s, g, k, nm, junk, t0 + k - 1 if k > 1 else 0)
            if k > 0:
                square_scalar(act, s, nm, g, k - 1, t0 + k + 1, junk)
    if u == RING + 3:
        square_scalar(act, s, nm, g, n - 1, t0 + n, junk)
    if RING + 4 <= u < RING + 4 + n:
        high_tile(act, nm, ps, xn, t0 + u - RING - 4)


def tail_vector(dve, s, ps, nm, xn, u, D, factor):
    g = len(GROUPS) - 1
    t0, n = GROUPS[g]
    if u == RING:
        y_free(dve, s, nm, g)
        for k in range(n):
            leave_vector(dve, s, ps, g, k)
            if k > 1:
                residual_vector(dve, s, g, k - 1)
            y_roots(dve, s, t0 + k, t0 + k + 1, D, factor)
            if k == 0:
                residual_vector(dve, s, g, k)
    if u == RING + 2:
        norm_roots(dve, nm, t0, t0 + n - 1, D)
        residual_vector(dve, s, g, n - 1)
        for k in range(n - 1):
            scale_y(dve, s, nm, t0 + k, k)
    if u == RING + 3:
        norm_roots(dve, nm, t0 + n - 1, t0 + n, D)
        scale_y(dve, s, nm, t0 + n - 1, n - 1)
    if RING + 4 <= u < RING + 4 + n:
        low_tile(dve, nm, ps, xn, t0 + u - RING - 4)


def tail_tensor(pe, s, ps, nm, ident, u):
    t0, n = GROUPS[-1]
    k = u - (RING + 2)
    if 0 <= k < n:
        turn_tile(pe, nm, ps, ident, t0 + k, s.y.shape[2] // P)


def down_scalar(act, s, ps, nm, xn):
    FT = s.h.shape[1]
    act.wait_ge(s.w_low, 2 * FT)
    act.wait_ge(s.up_done, FT - 1)
    down_high(act, s, 0, 0, 0)
    act.wait_ge(s.up_done, FT)
    for c in range(1, 4):
        down_high(act, s, 0, 0, c)
    with act.Fori(1, FT // 3) as i:
        for c in range(1, 4):
            down_high(act, s, 0, i, c)
    for g in range(1, len(GROUPS)):
        for f in range(2):
            down_high(act, s, g, 0, f)
        y_free(act, s, nm, g - 1)
        for k in range(GROUPS[g - 1][1]):
            leave_scalar(act, s, ps, g - 1, k)
        for f in range(2, FT):
            down_high(act, s, g, 0, f)
            steps_scalar(act, s, ps, nm, xn, g - 1, f)
    if nm is None:
        last_scalar(act, s, ps)


def down_vector(dve, s, ps, nm, xn, D, factor):
    FT = s.h.shape[1]
    for c in range(4):
        down_low(dve, s, 0, 0, c)
    with dve.Fori(1, FT // 3) as i:
        for c in range(1, 4):
            down_low(dve, s, 0, i, c)
    for g in range(1, len(GROUPS)):
        for f in range(2):
            down_low(dve, s, g, 0, f)
        y_free(dve, s, nm, g - 1)
        for k in range(GROUPS[g - 1][1]):
            leave_vector(dve, s, ps, g - 1, k)
        for f in range(2, FT):
            down_low(dve, s, g, 0, f)
            steps_vector(dve, s, ps, nm, xn, g - 1, f, D, factor)
    if nm is None:
        last_vector(dve, s, ps, D, factor)


def down_tensor(pe, s, ps, nm, ident):
    FT = s.h.shape[1]
    pe.wait_ge(s.h_done, FT - 1)
    for c in range(4):
        down_products(pe, s, ps, 0, 0, c)
    with pe.Fori(1, FT // 3 - 1) as i:
        for c in range(1, 4):
            down_products(pe, s, ps, 0, i, c)
    for c in range(1, 4):
        down_products(pe, s, ps, 0, FT // 3 - 1, c)
    for g in range(1, len(GROUPS)):
        for c in range(4):
            down_products(pe, s, ps, g, 0, c)
        first = (TURN[0] - 1) // 3 if nm else FT // 3 - 1
        with pe.Fori(1, first) as i:
            for c in range(1, 4):
                down_products(pe, s, ps, g, i, c)
        last = g == len(GROUPS) - 1
        for f in range(3 * first + 1, FT - RING if last else FT):
            down_products(pe, s, ps, g, 0, f)
            steps_tensor(pe, s, ps, nm, ident, g - 1, f)
        if last:
            down_last_units(pe, s, ps)


def last_scalar(act, s, ps):
    g = len(GROUPS) - 1
    t0, n = GROUPS[g]
    for k in range(n):
        wait_tile(act, s, g, k)
        act.wait_ge(s.y_summed, t0 + k)
        act.activation(ps[:, 6:8, :], ps[:, 2 * k:2 * k + 2, :], ACT.Square,
                       accum_out=s.ssq[:, t0 + k:t0 + k + 1]).then_inc(s.y_summed, 1)


def last_vector(dve, s, ps, D, factor):
    g = len(GROUPS) - 1
    t0, n = GROUPS[g]
    dve.wait_ge(s.stored, 16 * t0)
    for k in range(n):
        wait_tile(dve, s, g, k)
        y_roots(dve, s, t0 + k, t0 + k + 1, D, factor)
        residual_vector(dve, s, g, k, ps[:, 2 * k:2 * k + 2, :].rearrange("p b c -> p (b c)"))


def down_pool(pool, s, res, out, nm):
    tiles, ahead = out.shape[0] // P, len(s.res)

    def load(t):
        if t >= ahead:
            pool.wait_ge(s.y_final, t - ahead + 1)
        pool.dma_start(s.res[t % ahead][:, :], res[t * P:(t + 1) * P, :])\
            .then_inc(s.res_loaded[t % ahead], 16)

    for t in range(ahead - 1):
        load(t)
    for g, (t0, n) in enumerate(GROUPS):
        for k in range(n):
            t = t0 + k
            if t + ahead - 1 < tiles:
                load(t + ahead - 1)
            pool.wait_ge(s.y_final, t + 1)
            pool.dma_start(out[t * P:(t + 1) * P, :], s.y[:, k, :]).then_inc(s.stored, 16)



HEADS_M, HEADS_A, HEADS_KV, DH_A = 4, 8, 2, 64
CONV = 4
ROPE_HALF = 8
THETA = 500000.0
NV, NO, NQ = 129, 512, 512
TOK = HEADS_M * NV + NO + NQ
OG, AQ = HEADS_M * NV, HEADS_M * NV + NO
BIG = 3.0e38
QK_SCALE = 0.25 * P ** -0.5


class Mixer:

    def __init__(self, mem, S, D):
        at = lambda n, shape, dt, kb: mem.at(f"mix_{n}", shape, dt, int(kb * KB))
        s = lambda n: mem.sem(f"mix_{n}")
        T, K = S // P, D // P
        self.T, self.K = T, K
        self.tok = at("tok", [P, T, TOK], F32, 64)
        self.ak = at("ak", [P, T, 4, DH_A], F32, 132.25)
        self.av = at("av", [P, T, 4, DH_A], F32, 140.25)
        self.qk = at("qk", [P, 2 * HEADS_M, S], F32, 173)
        self.traw = [at(f"token_raw{b}", [P, BANK], F32, 112.25 + 2 * b) for b in range(3)]
        self.tpart = [at(f"token_part{b}", [P, 2, BANK], FR, 118.25 + 4 * b) for b in range(3)]
        self.traw_loaded = [s(f"token_loaded{b}") for b in range(3)]
        self.t_high, self.t_low, self.t_unit = s("token_high"), s("token_low"), s("token_unit_done")
        self.left = [s("bank_left_by_act"), s("bank_left_by_dve")]
        self.tanh_o, self.og_done = s("tanh_o"), s("og_done")
        self.gain_norm = at("gain_norm", [P, HEADS_M * P], F32, 130.25)
        self.pos_i = at("pos_i", [P, T], I32, 164.25)
        self.pos = at("pos", [P, T], F32, 164.375)
        self.freq = at("freq", [P, ROPE_HALF], F32, 164.5)
        self.ang = at("ang", [P, T, ROPE_HALF], F32, 164.75)
        self.turns = at("turns", [P, T, ROPE_HALF], F32, 165)
        self.cos = at("cos", [P, T, ROPE_HALF], F32, 165.25)
        self.sin = at("sin", [P, T, ROPE_HALF], F32, 165.5)
        self.rt = [at(f"rope{i}", [P, T, 8, ROPE_HALF], F32, 156.25 + 2 * i) for i in range(4)]
        self.pos_loaded, self.angles, self.sines = s("pos_loaded"), s("angles"), s("sines")
        self.roped = s("roped")
        self.qbd = at("q_blocks", [P, 4, 2, P], F32, 148.25)
        self.kt = [at(f"kt{b}", [P, 2, 3, DH_A], F32, 152.25 + 1.5 * b) for b in range(2)]
        self.vsh = at("v_shifted", [P, 4, DH_A], F32, 155.25)
        self.pr = [at(f"probs{e}", [P, 4, P], F32, 156.25 + 2 * e) for e in range(2)]
        self.pt = [at(f"probs_turned{e}", [P, 4, P], F32, 160.25 + 2 * e) for e in range(2)]
        small = 207.25
        names = ("mx", "neg", "es", "rs", "rinv", "sd")
        stats = at("softmax_stats", [P, 12, 4], F32, small)
        self.st = [{n: stats[:, 6 * e + i, :] for i, n in enumerate(names)} for e in range(2)]
        self.sink = at("sink", [P, 4], F32, small + .1875)
        self.conv_w = at("conv_w", [P, CONV, 8], F32, small + .21875)
        self.conv_b = at("conv_b", [P, 8], F32, small + .34375)
        self.consts_loaded = s("constants_loaded")
        self.zeroed = s("zeroed")
        self.q_turned, self.k_turned = s("q_turned"), s("k_turned")
        self.qbd_ready, self.kt_ready = s("q_blocks_ready"), s("kt_ready")
        self.logits, self.stats, self.exps = s("logits"), s("softmax_shift"), s("exps")
        self.probs, self.pt_turned, self.pt_ready = s("probs"), s("probs_turned"), s("probs_turned_ready")
        self.vsh_ready, self.pv, self.ha_done = s("v_shifted_ready"), s("pv"), s("attention_out")
        self.qraw = at("qk_raw", [P, K, P], F32, 112.25)
        self.qpart = [at(f"qk_part{b}", [P, 2, K, P], FR, 116.25 + 8 * b) for b in range(2)]
        self.xp = at("conv_in", [P, 3 + S], F32, 164.25)
        self.q_loaded, self.q_high, self.q_low = s("qk_loaded"), s("qk_high"), s("qk_low")
        self.q_half, self.xp_ready = s("qk_half_done"), s("conv_in_ready")
        self.conv_done, self.tanh_qk, self.qk_done = s("conv_done"), s("tanh_qk"), s("qk_done")
        R = HEADS_M * T
        self.R = R
        self.gt = at("gates_token_major", [P, 2, HEADS_M, T], F32, 168.5)
        self.gbias = at("gate_bias", [P, 2, HEADS_M], F32, 168.75)
        g = [at(n, [R, P], F32, 168.8125 + .5 * i) for i, n in
             enumerate(("g_li", "g_f", "g_lf", "g_cum", "g_b", "g_cmax"))]
        self.g_li, self.g_f, self.g_lf, self.g_cum, self.g_b, self.g_cmax = g
        self.gout = at("g_out", [R, 2, P], F32, 171.8125)
        self.gsmall = at("g_small", [R, 8], F32, 172.875)
        self.gate_in, self.g_pe, self.g_sb, self.g_act = s("gate_in"), s("gate_pe"), s("gate_dve"), s("gate_act")
        self.g_stored = s("gate_rows_stored")
        self.col = at("gate_columns", [P, 3, R], F32, 206)
        self.dec = at("decay", [P, R], F32, 206.375)
        self.wo = [at(f"out_{n}", [P, K, D], FR, 32 * i) for i, n in enumerate(("high", "low"))]
        self.wraw = at("out_raw", [P, K, D], F32, 32)
        self.bc = [at(f"gate_rows{b}", [P, 2, HEADS_M, P], F32, 116.25 - 4 * b) for b in range(2)]
        self.dm = at("decay_matrix", [P, HEADS_M, P], F32, 120.25)
        self.sc = at("scores", [P, HEADS_M, P], F32, 122.25)
        self.kw = at("k_weighted", [P, HEADS_M, P], F32, 124.25)
        self.qw = at("q_weighted", [P, HEADS_M, P], F32, 126.25)
        self.hm = at("hm", [P, HEADS_M, P], F32, 128.25)
        self.junk = at("junk", [P, D], BF, 128.25)
        self.C = [at(f"state{b}", [P, HEADS_M, NV], F32, 130.25 + 2.125 * b) for b in range(2)]
        self.hs = [at(f"out_in{b}", [P, 2, K, P], FR, 134.5 + 8 * b) for b in range(2)]
        self.res = at("residual", [P, D], F32, 168.75)
        self.gain_post, self.gain_next = (self.tok[:, t:t + 2, AQ:AQ + NQ] for t in (0, 2))
        names = ("ad", "r", "rs", "nb", "vr", "half", "value")
        stats = at("norm_stats", [P, 8, 5], F32, small)
        self.sm = {n: stats[:, i, :] for i, n in enumerate(names)}
        self.sm["guess"] = stats[:, 7, :].bitcast(I32)
        self.bn = at("bn", [P, 4, 6], F32, small + .15625)
        self.mv = at("mean_var", [P, 4, 2], F32, small + .25)
        self.w_loaded = [s(f"out_loaded{b}") for b in range(4)]
        self.w_high, self.w_low = s("out_high"), s("out_low")
        self.bc_loaded = [s(f"gate_rows_loaded{b}") for b in range(2)]
        self.s_done, self.k_done = s("scores_done"), s("k_turned_m")
        self.dm_shift, self.dm_done, self.wg_done = s("decay_shift"), s("decay_done"), s("wg_done")
        self.sc_done, self.kw_done, self.qw_done = s("scores_weighted"), s("kw_done"), s("qw_done")
        self.n_done, self.c_done, self.state = s("num_done"), s("kv_done"), s("state_done")
        self.norm_ready, self.hm_norm, self.hm_done = s("norm_ready"), s("hm_norm"), s("hm_done")
        self.hm_turned, self.hs_high, self.hs_low = s("hm_turned"), s("out_in_high"), s("out_in_low")
        self.y_half, self.y_done, self.y_left = s("y_half_done"), s("y_done"), s("y_left")
        self.y_summed, self.y_scaled = s("y_summed"), s("y_scaled")
        self.res_loaded, self.h_done, self.stored = s("residual_loaded"), s("h_done"), s("stored")
        self.post_loaded = s("post_gain_loaded")
        self.chain = Chain(mem, "mix_dve_step")


M_W = HEADS_M * P
GATES, A_Q = 4 * M_W, 4 * M_W + 2 * HEADS_M
A_K = A_Q + HEADS_A * DH_A
CHUNKS = [
    [(0, GATES, 2 * HEADS_M), (2 * HEADS_M, A_K, 2 * HEADS_KV * DH_A)],
    [(0, A_Q, HEADS_A * DH_A)],
    [(0, 2 * M_W, M_W)],
    [(0, 3 * M_W, M_W)],
]
WIDTH = [sum(w for _, _, w in c) for c in CHUNKS]


EARLY = GROUPS[-1][0]


def token_units(m):
    return [(0, k, range(EARLY)) for k in range(m.K)] + [(0, k, range(EARLY, m.T)) for k in range(m.K)] + \
        [(chunk, k, range(m.T)) for chunk in range(1, len(CHUNKS)) for k in range(m.K)]


def tokens_sync(sp, m, w_in):
    for u, (chunk, k, _) in enumerate(token_units(m)):
        if u >= RING:
            sp.wait_ge(m.t_low, u - RING + 1)
        for a, c, w in CHUNKS[chunk]:
            sp.dma_start(m.traw[u % RING][:, a:a + w], w_in[k * P:(k + 1) * P, c:c + w])\
              .then_inc(m.traw_loaded[u % RING], 16)


def token_loads(m, u):
    return 16 * sum(len(CHUNKS[token_units(m)[v][0]]) for v in range(u % RING, u + 1, RING))


def units_through(m, chunk):
    return m.K * (chunk + 2)


def token_high(act, m, u, w):
    act.wait_ge(m.traw_loaded[u % RING], token_loads(m, u))
    if u >= RING:
        act.wait_ge(m.t_unit, u - RING + 1)
    act.activation(m.tpart[u % RING][:, 0, 0:w], m.traw[u % RING][:, 0:w], ACT.Copy).then_inc(m.t_high, 1)


def token_low(dve, m, u, w):
    dve.wait_ge(m.t_high, u + 1)
    p = m.tpart[u % RING]
    part_low(dve, p[:, 1, 0:w], m.traw[u % RING][:, 0:w], p[:, 0, 0:w]).then_inc(m.t_low, 1)


def tokens_tensor(pe, m, ps, xn, ff, nm, ident):
    for u, (chunk, k, tiles) in enumerate(token_units(m)):
        w = WIDTH[chunk]
        pe.wait_ge(m.t_low, u + 1)
        part = m.tpart[u % RING]
        if k == 0 and chunk == 0:
            pe.wait_ge(nm.low, 2 * tiles[-1] + 2)
        for t in tiles:
            if k == 0:
                if chunk > 0:
                    pe.wait_ge(m.left[t % 2], m.T // 2 * (chunk - 1) + t // 2 + 1)
                elif t < 2 * GROUPS[-1][1]:
                    pe.wait_ge((ff.y_act, ff.y_dve)[t % 2], EARLY + t // 2 + 1)
            mm = three_passes(pe, ps[:, t, 0:w], [x[:, k, t * P:(t + 1) * P] for x in xn],
                              [part[:, i, 0:w] for i in range(2)], k == 0, k == m.K - 1)
        mm.then_inc(m.t_unit, 1)
        tail_tensor(pe, ff, ps, nm, ident, u)


def tokens_leave(eng, copy, m, ps, chunk, which, units, tiles):
    eng.wait_ge(m.t_unit, units)
    for t in tiles[(which - tiles[0]) % 2::2]:
        bank = ps[:, t, :]
        if chunk == 0:
            copy(m.gt[:, :, :, t], bank[:, 0:8].rearrange("p (g h) -> p g h", g=2))
            for j, to in enumerate((m.ak, m.av)):
                src = bank[:, 8 + P * j:8 + P * (j + 1)].rearrange("p (k f) -> p k f", k=2)
                for d in range(2):
                    ins = copy(to[:, t, d::2, :], src)
        elif chunk == 1:
            ins = copy(m.tok[:, t, AQ:AQ + NQ], bank)
        elif chunk == 2:
            ins = copy(m.tok[:, t, 0:HEADS_M * NV].rearrange("p (h e) -> p h e", e=NV)[:, :, 0:P],
                       bank.rearrange("p (h e) -> p h e", e=P))
        ins.then_inc(m.left[which], 1)


def leave_after(m, u):
    chunk, k, tiles = token_units(m)[u]
    if k != 1 or u < m.K:
        return None
    if chunk == 0:
        return 0, m.K, range(EARLY)
    return chunk - 1, units_through(m, chunk - 1), range(EARLY if chunk == 1 else 0, m.T)


def tokens_scalar(act, m, ps, xn, ff, nm):
    copy = lambda out, in_: act.activation(out, in_, ACT.Copy)
    for u, (chunk, k, _) in enumerate(token_units(m)):
        if u == 0:
            act.wait_ge(ff.unit_done, len(GROUPS) * ff.h.shape[1] - RING)
        tail_scalar(act, ff, ps, nm, xn, u)
        token_high(act, m, u, WIDTH[chunk])
        leave = leave_after(m, u)
        if leave:
            tokens_leave(act, copy, m, ps, leave[0], 0, *leave[1:])
        if chunk == 2 and k == 5:
            act.wait_ge(m.angles, 1)
            act.activation(m.sin[:, :, :], m.sin[:, :, :], ACT.Sin).then_inc(m.sines, 1)
            act.activation(m.cos[:, :, :], m.cos[:, :, :], ACT.Sin).then_inc(m.sines, 1)
    act.wait_ge(m.t_unit, units_through(m, len(CHUNKS) - 1))
    for t in range(m.T):
        act.activation(m.tok[:, t, OG:OG + NO], ps[:, t, :], ACT.Tanh, scale=0.5).then_inc(m.tanh_o, 1)


def angles_vector(dve, m):
    then = m.chain.then
    for i in range(ROPE_HALF):
        dve.memset(m.freq[:, i:i + 1], float(np.float32(np.float32(THETA) ** np.float32(-i / ROPE_HALF))))\
           .then_inc(m.chain.sem, 1)
        m.chain.count += 1
    dve.wait_ge(m.chain.sem, m.chain.count)
    dve.wait_ge(m.pos_loaded, 16)
    then(dve, dve.tensor_copy(m.pos[:, :], m.pos_i[:, :]))
    wide = [P, m.T, ROPE_HALF]
    then(dve, dve.tensor_tensor(m.ang[:, :, :], m.pos[:, :].unsqueeze(2).to_broadcast(wide),
                                m.freq[:, :].unsqueeze(1).to_broadcast(wide), ALU.mult))
    ROUND = 1.5 * 2.0 ** 23
    turn = 2 * np.pi
    c1 = 6.28125
    c2 = float(np.float32(np.round((turn - c1) * 2 ** 21) / 2 ** 21))
    c3 = float(np.float32(turn - c1 - c2))
    for out, shift in ((m.sin, 0.0), (m.cos, 0.25)):
        n, o, a = m.turns[:, :, :], out[:, :, :], m.ang[:, :, :]
        then(dve, dve.tensor_scalar(n, a, 1 / turn, shift, ALU.mult, ALU.add))
        then(dve, dve.tensor_scalar(n, n, ROUND, ROUND, ALU.add, ALU.subtract))
        for i, c in enumerate((c1, c2, c3)):
            then(dve, dve.scalar_tensor_tensor(o, n, -c, a if i == 0 else o, ALU.mult, ALU.add))
        if shift:
            then(dve, dve.tensor_scalar(o, o, turn / 4, None, ALU.add))
        last = dve.tensor_scalar(o, o, 3.1415925, -3.1415925, ALU.min, ALU.max)
        if shift:
            last.then_inc(m.angles, 1)
        else:
            then(dve, last)


def rope_vector(dve, m):
    dve.wait_ge(m.sines, 2)
    then = m.chain.then
    q = m.tok[:, :, AQ:AQ + NQ].rearrange("p t (h f) -> p t h f", f=DH_A)
    for x, H in ((q, HEADS_A), (m.ak[:, :, :, :], 4)):
        wide = [P, m.T, H, ROPE_HALF]
        cos = m.cos[:, :, :].unsqueeze(2).to_broadcast(wide)
        sin = m.sin[:, :, :].unsqueeze(2).to_broadcast(wide)
        x1, x2 = x[:, :, :, 0:ROPE_HALF], x[:, :, :, ROPE_HALF:2 * ROPE_HALF]
        a, b, c, d = (r[:, :, 0:H, :] for r in m.rt)
        for o, u, v in ((a, x1, cos), (b, x2, sin), (c, x2, cos), (d, x1, sin)):
            then(dve, dve.tensor_tensor(o, u, v, ALU.mult))
        dve.tensor_tensor(x1, a, b, ALU.subtract).then_inc(m.roped, 1)
        dve.tensor_tensor(x2, c, d, ALU.add).then_inc(m.roped, 1)
        dve.wait_ge(m.roped, 2 if H == HEADS_A else 4)


def tokens_vector(dve, m, ps, xn, ff, nm, D):
    then = m.chain.then
    for u, (chunk, k, _) in enumerate(token_units(m)):
        tail_vector(dve, ff, ps, nm, xn, u, D, 0.5)
        token_low(dve, m, u, WIDTH[chunk])
        leave = leave_after(m, u)
        if leave:
            tokens_leave(dve, dve.tensor_copy, m, ps, leave[0], 1, *leave[1:])
        if chunk == 1 and k == 4:
            angles_vector(dve, m)
        if chunk == 2 and k == 4:
            dve.wait_ge(m.left[0], m.T)
            rope_vector(dve, m)
        if chunk == 3 and k == 4:
            dve.wait_ge(m.consts_loaded, m.consts)
            then(dve, dve.tensor_scalar(m.gain_norm[:, :], m.gain_norm[:, :], 0.5, None, ALU.mult))
            dve.wait_ge(m.left[0], m.T // 2)
            dve.wait_ge(m.left[1], m.T // 2)
            dve.tensor_tensor(m.gt[:, :, :, :], m.gt[:, :, :, :],
                              m.gbias[:, :, :].unsqueeze(3).to_broadcast([P, 2, HEADS_M, m.T]),
                              ALU.add).then_inc(m.gate_in, 1)
    for t in range(m.T):
        dve.wait_ge(m.tanh_o, t + 1)
        og = m.tok[:, t, OG:OG + NO]
        dve.scalar_tensor_tensor(og, og, 1.0, m.gain_norm[:, :], ALU.add, ALU.mult).then_inc(m.og_done, 1)



B_Q, B_K, B_L, B_P, B_V = 2, 3, (4, 5), 6, 7


def qk_sync(sp, m, w_in):
    w = w_in[:, 0:2 * M_W].rearrange("(k p) f -> p k f", p=P)
    sp.wait_ge(m.t_low, units_through(m, len(CHUNKS) - 1))
    for i in range(2 * HEADS_M):
        if i > 0:
            sp.wait_ge(m.q_low, i)
        sp.dma_start(m.qraw[:, :, :], w[:, :, i * P:(i + 1) * P]).then_inc(m.q_loaded, 16)


def qk_high(act, m, i):
    act.wait_ge(m.q_loaded, 16 * (i + 1))
    if i == 0:
        act.wait_ge(m.t_unit, units_through(m, len(CHUNKS) - 1))
        act.wait_ge(m.og_done, m.T)
    if i >= 2:
        act.wait_ge(m.q_half, 2 * (i - 1))
    act.activation(m.qpart[i % 2][:, 0, :, :], m.qraw[:, :, :], ACT.Copy).then_inc(m.q_high, 1)


def qk_low(dve, m, i):
    dve.wait_ge(m.q_high, i + 1)
    p = m.qpart[i % 2]
    part_low(dve, p[:, 1, :, :], m.qraw[:, :, :], p[:, 0, :, :]).then_inc(m.q_low, 1)


def qk_half(pe, m, ps, xn, i, th):
    pe.wait_ge(m.q_low, i + 1)
    if i == 0:
        pe.wait_ge(m.tanh_o, m.T)
    else:
        pe.wait_ge(m.xp_ready, 2 * (i - 1) + th + 1)
    w = m.qpart[i % 2]
    for k in range(m.K):
        mm = three_passes(pe, ps[:, th, :], [w[:, a, k, :] for a in range(2)],
                          [x[:, k, th * BANK:(th + 1) * BANK] for x in xn], k == 0, k == m.K - 1)
    mm.then_inc(m.q_half, 1)


def conv_in_scalar(act, m, ps, i, th):
    act.wait_ge(m.q_half, 2 * i + th + 1)
    if i > 0:
        act.wait_ge(m.qk_done, i)
    else:
        act.wait_ge(m.roped, 4)
        act.wait_ge(m.sines, 2)
    act.activation(m.xp[:, 3 + th * BANK:3 + (th + 1) * BANK], ps[:, th, :], ACT.Copy)\
       .then_inc(m.xp_ready, 1)


def conv_vector(dve, m, i):
    then = m.chain.then
    S = m.qk.shape[2]
    dve.wait_ge(m.xp_ready, 2 * i + 2)
    out = m.qk[:, i, :]
    then(dve, dve.tensor_scalar(out, m.xp[:, 3:3 + S], m.conv_w[:, 3, i:i + 1], m.conv_b[:, i:i + 1],
                                ALU.mult, ALU.add))
    for j in (2, 1, 0):
        ins = dve.scalar_tensor_tensor(out, m.xp[:, j:j + S], m.conv_w[:, j, i:i + 1], out,
                                       ALU.mult, ALU.add)
        if j:
            then(dve, ins)
    ins.then_inc(m.conv_done, 1)


def tanh_scalar(act, m, i):
    S = m.qk.shape[2]
    act.wait_ge(m.conv_done, i + 1)
    act.activation(m.xp[:, 3:3 + S], m.qk[:, i, :], ACT.Tanh, scale=0.5).then_inc(m.tanh_qk, 1)


def silu_vector(dve, m, i):
    S = m.qk.shape[2]
    dve.wait_ge(m.tanh_qk, i + 1)
    dve.scalar_tensor_tensor(m.qk[:, i, :], m.xp[:, 3:3 + S], 1.0, m.qk[:, i, :], ALU.add, ALU.mult)\
       .then_inc(m.qk_done, 1)


def attend_turn_tensor(pe, m, ps, ident, i):
    if i == 0:
        pe.wait_ge(m.roped, 4)
        pe.wait_ge(m.tanh_o, m.T)
    else:
        pe.wait_ge(m.qbd_ready, 2 * i)
        pe.wait_ge(m.kt_ready, i)
        step = min(i, len(GATE_ACT)) - 1
        pe.wait_ge(m.g_act, GATE_ACT[step])
        pe.wait_ge(m.g_sb, GATE_READ[step])
    for j in range(4):
        mm = pe.transpose(ps[:, B_Q, j * P:(j + 1) * P], m.tok[:, i, AQ + j * P:AQ + (j + 1) * P], ident[:, :])
    mm.then_inc(m.q_turned, 1)
    for j in range(2):
        mm = pe.transpose(ps[:, B_K, j * P:(j + 1) * P],
                          m.ak[:, i, 2 * j:2 * j + 2, :].rearrange("p d f -> p (d f)"), ident[:, :])
    mm.then_inc(m.k_turned, 1)


def attend_q_scalar(act, m, ps, i):
    act.wait_ge(m.q_turned, i + 1)
    if i == 0:
        act.wait_ge(m.zeroed, m.zeros)
    else:
        act.wait_ge(m.logits, 2 * i)
    for e in range(2):
        h = slice(64 * e, 64 * e + 64)
        act.activation(m.qbd[h, :, :, h], ps[h, B_Q, :].rearrange("p (j c q) -> p j c q", j=4, c=2),
                       ACT.Copy).then_inc(m.qbd_ready, 1)


def attend_k_vector(dve, m, ps, i):
    dve.wait_ge(m.k_turned, i + 1)
    if i == 0:
        dve.wait_ge(m.zeroed, m.zeros)
    if i >= 1:
        dve.wait_ge(m.logits, 2 * i)
    src = ps[:, B_K, 0:2 * P].rearrange("p (k c s) -> p k c s", k=2, c=2)
    dve.tensor_copy(m.kt[i % 2][:, :, 0:2, :], src)
    dve.tensor_copy(m.kt[1 - i % 2][:, :, 2, :], src[:, :, 1, :]).then_inc(m.kt_ready, 1)


def attend_logits_tensor(pe, m, ps, i, e):
    if e == 0:
        pe.wait_ge(m.qbd_ready, 2 * i + 2)
        pe.wait_ge(m.kt_ready, i + 1)
    if i > 0:
        pe.wait_ge(m.exps, 2 * (i - 1) + e + 1)
    for j in range(4):
        kt = m.kt[i % 2][:, j // 2, :, :]
        keys = kt[:, 0:2, :] if e else (kt[:, 0::2, :] if i else kt[:, 0:1, :])
        n = keys.shape[1] * DH_A
        mm = pe.matmul(ps[:, B_L[e], j * P:j * P + n], m.qbd[:, j, e, :], keys, start=True, stop=True)
    mm.then_inc(m.logits, 1)


def keys_of(i, e):
    return P if i or e else DH_A


def attend_max_vector(dve, m, ps, i, e):
    then, st, n = m.chain.then, m.st[e], keys_of(i, e)
    dve.wait_ge(m.logits, 2 * i + e + 1)
    if i > 0:
        dve.wait_ge(m.exps, 2 * (i - 1) + e + 1)
    lg = ps[:, B_L[e], :].rearrange("p (j s) -> p j s", j=4)[:, :, 0:n]
    then(dve, dve.tensor_reduce(st["mx"][:, :], lg, AX, ALU.max))
    then(dve, dve.scalar_tensor_tensor(st["mx"][:, :], st["mx"][:, :], DH_A ** -0.5, m.sink[:, :],
                                       ALU.mult, ALU.max))
    dve.tensor_scalar(st["neg"][:, :], st["mx"][:, :], -1.0, None, ALU.mult)
    dve.tensor_tensor(st["sd"][:, :], m.sink[:, :], st["mx"][:, :], ALU.subtract).then_inc(m.stats, 1)


def attend_exp_scalar(act, m, ps, i, e):
    st, n = m.st[e], keys_of(i, e)
    act.wait_ge(m.stats, 2 * i + e + 1)
    if i > 0:
        act.wait_ge(m.pt_turned, 2 * (i - 1) + e + 1)
        act.wait_ge(m.probs, 2 * (i - 1) + e + 1)
    else:
        act.wait_ge(m.zeroed, m.zeros)
        act.wait_ge(m.roped, 4)
    for j in range(4):
        act.activation(m.pr[e][:, j, 0:n], ps[:, B_L[e], j * P:j * P + n], ACT.Exp,
                       bias=st["neg"][:, j:j + 1], scale=DH_A ** -0.5, accum_out=st["rs"][:, j:j + 1])
    act.activation(st["es"][:, :], st["sd"][:, :], ACT.Exp).then_inc(m.exps, 1)


def attend_divide_vector(dve, m, i, e):
    then, st, n = m.chain.then, m.st[e], keys_of(i, e)
    dve.wait_ge(m.exps, 2 * i + e + 1)
    then(dve, dve.tensor_tensor(st["rinv"][:, :], st["rs"][:, :], st["es"][:, :], ALU.add))
    then(dve, dve.reciprocal(st["rinv"][:, :], st["rinv"][:, :]))
    if n < P:
        dve.memset(m.pr[e][:, :, n:P], 0.0)
    pr = m.pr[e][:, :, 0:n]
    dve.tensor_tensor(pr, pr, st["rinv"][:, :].unsqueeze(2).to_broadcast([P, 4, n]), ALU.mult)\
       .then_inc(m.probs, 1)


def attend_probs_tensor(pe, m, ps, ident, i, e):
    pe.wait_ge(m.probs, 2 * i + e + 1)
    if i or e:
        pe.wait_ge(m.pt_ready, 2 * i + e)
    for j in range(4):
        mm = pe.transpose(ps[:, B_P, j * P:(j + 1) * P], m.pr[e][:, j, :], ident[:, :])
    mm.then_inc(m.pt_turned, 1)


def attend_probs_scalar(act, m, ps, i, e):
    act.wait_ge(m.pt_turned, 2 * i + e + 1)
    if i:
        act.wait_ge(m.pv, 2 * (i - 1) + e + 1)
    act.activation(m.pt[e][:, :, :], ps[:, B_P, :].rearrange("p (j q) -> p j q", j=4), ACT.Copy)\
       .then_inc(m.pt_ready, 1)


def attend_values_tensor(pe, m, ps, i, e):
    pe.wait_ge(m.pt_ready, 2 * i + e + 1)
    if not e:
        pe.wait_ge(m.vsh_ready, 2 * i + 2)
    if i or e:
        pe.wait_ge(m.ha_done, 2 * (2 * i + e))
    for kv in range(2):
        v = m.av[:, i, 2 * kv:2 * kv + 2, :] if e else m.vsh[:, 2 * kv:2 * kv + 2, :]
        mm = pe.matmul(ps[:, B_V, 2 * kv * P:2 * (kv + 1) * P], v.rearrange("p d f -> p (d f)"),
                       m.pt[e][:, 2 * kv:2 * kv + 2, :], start=True, stop=True)
    mm.then_inc(m.pv, 1)


def attend_out_scalar(act, m, ps, i, e):
    act.wait_ge(m.pv, 2 * i + e + 1)
    ha = m.tok[:, i, AQ:AQ + NQ].rearrange("p (j q) -> p j q", j=4)
    bank = ps[:, B_V, :].rearrange("p (j q) -> p j q", j=4)
    for d in range(2):
        h = slice(64 * d, 64 * d + 64)
        act.activation(ha[h, :, 64 * e:64 * e + 64], bank[h, :, h], ACT.Copy).then_inc(m.ha_done, 1)


def shifted_values_pool(pool, m, i):
    if i == 0:
        pool.wait_ge(m.left[0], m.T // 2)
        pool.wait_ge(m.left[1], m.T // 2)
        pool.wait_ge(m.zeroed, m.zeros)
    else:
        pool.wait_ge(m.pv, 2 * i - 1)
        pool.wait_ge(m.vsh_ready, 2 * i)
    pool.tensor_copy(m.vsh[0:64, :, :], m.av[0:64, i, :, :]).then_inc(m.vsh_ready, 1)
    pool.wait_ge(m.vsh_ready, 2 * i + 1)
    if i == 0:
        pool.memset(m.vsh[64:128, :, :], 0.0).then_inc(m.vsh_ready, 1)
    else:
        pool.tensor_copy(m.vsh[64:128, :, :], m.av[64:128, i - 1, :, :]).then_inc(m.vsh_ready, 1)



GATE_DVE = (4, 9, 13, 14)
GATE_ACT = (2, 2, 3, 4)
GATE_READ = (2, 5, 10, 10)


def gate_tensor(pe, m, ps, ident, ones, step):
    R = m.R
    bank = ps[:, B_K, :]
    pe.wait_ge(m.kt_ready, step + 1)
    if step == 0:
        pe.wait_ge(m.gate_in, 1)
        for g in range(2):
            mm = pe.transpose(bank[0:R, g * P:(g + 1) * P], m.gt[:, g, :, :].rearrange("p h t -> p (h t)"),
                              ident[:, :])
    elif step == 1:
        pe.wait_ge(m.g_sb, 4)
        for g in range(2):
            mm = pe.matmul(bank[0:1, g * R:(g + 1) * R], m.gsmall[:, g:g + 1], ident[0:R, 0:R],
                           start=True, stop=True)
    elif step == 2:
        pe.wait_ge(m.g_sb, 9)
        pe.matmul(bank[0:R, 0:1], m.g_lf[0:1, 64:96], ident[0:1, 0:1], start=True, stop=True)
        pe.matmul(bank[0:R, 1:2], m.g_lf[0:1, 96:128], ident[0:1, 0:1], start=True, stop=True)
        mm = pe.matmul(bank[:, 64:64 + R], ones[0:1, :], m.g_f[0:1, 0:R], start=True, stop=True)
    else:
        pe.wait_ge(m.g_sb, 13)
        for j, x in enumerate((m.g_b, m.g_li, m.g_f)):
            mm = pe.transpose(bank[:, j * R:(j + 1) * R], x[:, :], ident[0:R, 0:R])
    mm.then_inc(m.g_pe, 1)


def gate_vector(dve, m, ps, step):
    R, T, then = m.R, m.T, m.chain.then
    bank = ps[:, B_K, :]
    last = lambda ins: ins.then_inc(m.g_sb, 1)
    if step == 0:
        dve.wait_ge(m.g_pe, 1)
        last(dve.tensor_copy(m.g_li[:, :], bank[0:R, 0:P]))
        then(dve, dve.tensor_copy(m.g_f[:, :], bank[0:R, P:2 * P]))
        last(dve.scalar_tensor_tensor(m.g_lf[:, :], m.g_f[:, :], -1.0, m.g_f[:, :], ALU.mult, ALU.max))
        then(dve, dve.memset(m.gout[:, 0, :], 1.0))
        dve.wait_ge(m.g_act, 2)
        then(dve, dve.scalar_tensor_tensor(m.g_lf[:, :], m.g_f[:, :], 0.0, m.g_lf[:, :], ALU.min, ALU.subtract))
        then(dve, dve.tensor_tensor_scan(m.g_cum[:, :], m.gout[:, 0, :], m.g_lf[:, :], 0.0, ALU.mult, ALU.add))
        then(dve, dve.tensor_tensor(m.g_b[:, :], m.g_li[:, :], m.g_cum[:, :], ALU.subtract))
        then(dve, dve.tensor_tensor_scan(m.g_cmax[:, :], m.g_b[:, :], m.g_b[:, :], -BIG, ALU.max, ALU.max))
        last(dve.tensor_copy(m.gsmall[:, 0:1], m.g_cum[:, P - 1:P]))
        last(dve.tensor_tensor(m.gsmall[:, 1:2], m.g_cum[:, P - 1:P], m.g_cmax[:, P - 1:P], ALU.add))
    elif step == 1:
        dve.wait_ge(m.g_pe, 2)
        row = m.g_lf[0:1, :]
        then(dve, dve.tensor_copy(row[:, 0:2 * R], bank[0:1, 0:2 * R]))
        then(dve, dve.memset(row[:, 64:96], 0.0))
        for h in range(HEADS_M):
            a = slice(h * T, (h + 1) * T)
            last(dve.tensor_tensor_scan(row[:, 96 + h * T:96 + (h + 1) * T], row[:, h * T:(h + 1) * T],
                                        row[:, R + h * T:R + (h + 1) * T], 0.0, ALU.add, ALU.max))
        dve.wait_ge(m.g_sb, 8)
        rows = lambda a: row[:, a:a + R].rearrange("p (h t) -> p h t", h=HEADS_M)
        then(dve, dve.tensor_copy(rows(64)[:, :, 1:T], rows(96)[:, :, 0:T - 1]))
        then(dve, dve.tensor_tensor(m.g_f[0:1, 0:R], row[:, 0:R], row[:, 64:96], ALU.add))
        last(dve.tensor_tensor(m.g_f[0:1, 0:R], m.g_f[0:1, 0:R], row[:, 96:128], ALU.subtract))
    elif step == 2:
        dve.wait_ge(m.g_pe, 3)
        then(dve, dve.tensor_copy(m.gsmall[:, 2:4], bank[0:R, 0:2]))
        before, after = m.gsmall[:, 2:3], m.gsmall[:, 3:4]
        then(dve, dve.tensor_scalar(m.gout[:, 0, :], m.g_cmax[:, :], before, -1.0, ALU.max, ALU.mult))
        last(dve.tensor_scalar(m.gout[:, 1, :], m.gout[:, 0, :], before, None, ALU.add))
        last(dve.tensor_tensor(m.g_f[:, :], m.gout[:, 0, :], m.g_cum[:, :], ALU.subtract))
        then(dve, dve.tensor_tensor(m.gsmall[:, 4:5], m.gsmall[:, 0:1], after, ALU.subtract))
        last(dve.tensor_scalar(m.g_li[:, :], m.g_b[:, :], m.gsmall[:, 4:5], None, ALU.add))
        last(dve.memset(m.gsmall[:, 5:6], 0.0))
    else:
        dve.wait_ge(m.g_act, 4)
        last(dve.tensor_scalar(m.col[:, 1, :], m.col[:, 1, :], QK_SCALE, None, ALU.mult))


def gate_scalar(act, m, ps, step):
    R, bank = m.R, ps[:, B_K, :]
    if step == 0:
        act.wait_ge(m.g_sb, 2)
        act.activation(m.g_lf[:, :], m.g_lf[:, :], ACT.Exp, scale=-1.0).then_inc(m.g_act, 1)
        act.wait_ge(m.g_act, 1)
        act.activation(m.g_lf[:, :], m.g_lf[:, :], ACT.Ln, bias=1.0).then_inc(m.g_act, 1)
    elif step == 2:
        act.wait_ge(m.g_sb, GATE_READ[2])
        act.activation(m.dec[:, :], bank[:, 64:64 + R], ACT.Exp).then_inc(m.g_act, 1)
    elif step == 3:
        act.wait_ge(m.g_pe, 4)
        act.activation(m.col[:, 0, :], bank[:, 0:R], ACT.Copy)
        act.activation(m.col[:, 1:3, :], bank[:, R:3 * R].rearrange("p (a r) -> p a r", a=2), ACT.Exp)\
           .then_inc(m.g_act, 1)


def heads_tensor(pe, m, ps, xn, ident, ones):
    for i in range(m.T):
        attend_turn_tensor(pe, m, ps, ident, i)
        if i:
            attend_values_tensor(pe, m, ps, i - 1, 0)
            attend_probs_tensor(pe, m, ps, ident, i - 1, 1)
        qk_half(pe, m, ps, xn, i, 0)
        attend_logits_tensor(pe, m, ps, i, 0)
        attend_logits_tensor(pe, m, ps, i, 1)
        if i < 4:
            gate_tensor(pe, m, ps, ident, ones, i)
        if i:
            attend_values_tensor(pe, m, ps, i - 1, 1)
        qk_half(pe, m, ps, xn, i, 1)
        attend_probs_tensor(pe, m, ps, ident, i, 0)
    attend_values_tensor(pe, m, ps, m.T - 1, 0)
    attend_probs_tensor(pe, m, ps, ident, m.T - 1, 1)
    attend_values_tensor(pe, m, ps, m.T - 1, 1)


def heads_scalar(act, m, ps):
    T = m.T
    qk_high(act, m, 0)
    for i in range(T + 1):
        if i:
            conv_in_scalar(act, m, ps, i - 1, 1)
            attend_probs_scalar(act, m, ps, i - 1, 0)
        if i < T:
            attend_q_scalar(act, m, ps, i)
        if i:
            attend_out_scalar(act, m, ps, i - 1, 0)
            attend_probs_scalar(act, m, ps, i - 1, 1)
        if i + 1 < T:
            qk_high(act, m, i + 1)
        if i:
            tanh_scalar(act, m, i - 1)
        if i < T:
            conv_in_scalar(act, m, ps, i, 0)
            attend_exp_scalar(act, m, ps, i, 0)
            if i < 4:
                gate_scalar(act, m, ps, i)
            attend_exp_scalar(act, m, ps, i, 1)
        if i:
            attend_out_scalar(act, m, ps, i - 1, 1)
    out_weights_scalar(act, m, 0)


def heads_vector(dve, m, ps, causal):
    T = m.T
    qk_low(dve, m, 0)
    for i in range(T + 1):
        if i < T:
            attend_k_vector(dve, m, ps, i)
        if i:
            conv_vector(dve, m, i - 1)
        if i + 1 < T:
            qk_low(dve, m, i + 1)
        if i == T:
            chunk_decay_vector(dve, m, causal, 0)
        if i:
            silu_vector(dve, m, i - 1)
        if i < T:
            attend_max_vector(dve, m, ps, i, 0)
            attend_max_vector(dve, m, ps, i, 1)
            if i < 4:
                gate_vector(dve, m, ps, i)
            attend_divide_vector(dve, m, i, 0)
            attend_divide_vector(dve, m, i, 1)
    out_weights_vector(dve, m, 0)



B_S, B_T, B_N, B_C, B_Y = 0, 1, 2, 4, 6


def head_banks(ps, first):
    return ps[:, first:first + 2, 0:2 * NV].rearrange("p b (h e) -> p b h e", e=NV)


def out_weights_sync(sp, m, w_out, gate_rows):
    def rows(c):
        if c == 0:
            sp.wait_ge(m.g_stored, 16)
            sp.wait_ge(m.q_half, 2 * m.T - 2)
        if c == 1:
            sp.wait_ge(m.q_low, m.T)
        if c >= 2:
            sp.wait_ge(m.qw_done, c - 1)
            sp.wait_ge(m.dm_done, c - 1)
            sp.wait_ge(m.dm_shift, c - 1)
        src = gate_rows.rearrange("(h c) a l -> c a h l", h=HEADS_M)[c]
        for a in range(2):
            sp.dma_start(m.bc[c % 2][:, a, :, :], src[a].unsqueeze(0).to_broadcast([P, HEADS_M, P]))\
              .then_inc(m.bc_loaded[c % 2], 16)

    rows(0)
    rows(1)
    w = w_out.rearrange("(k p) f -> p k f", p=P)
    for n in range(2):
        sp.wait_ge(m.q_half, 2 * m.T - 1 + n)
        for j in range(2):
            at = (slice(None), slice(4 * j, 4 * j + 4), slice(n * BANK, (n + 1) * BANK))
            sp.dma_start(m.wraw[at], w[at]).then_inc(m.w_loaded[2 * n + j], 16)
    for c in range(2, m.T):
        rows(c)


def out_weights_scalar(act, m, n):
    for j in range(2):
        at = (slice(None), slice(4 * j, 4 * j + 4), slice(n * BANK, (n + 1) * BANK))
        act.wait_ge(m.w_loaded[2 * n + j], 16)
        act.activation(m.wo[0][at], m.wraw[at], ACT.Copy).then_inc(m.w_high, 1)


def out_weights_vector(dve, m, n):
    for j in range(2):
        at = (slice(None), slice(4 * j, 4 * j + 4), slice(n * BANK, (n + 1) * BANK))
        dve.wait_ge(m.w_high, 2 * n + j + 1)
        part_low(dve, m.wo[1][at], m.wraw[at], m.wo[0][at]).then_inc(m.w_low, 1)


def tile(m, h, c):
    return m.qk[:, h, c * P:(c + 1) * P]


def chunk_scores_tensor(pe, m, ps, ident, c):
    if c == 0:
        pe.wait_ge(m.qk_done, 2 * HEADS_M)
        pe.wait_ge(m.xp_ready, 2 * m.T)
    else:
        pe.wait_ge(m.kw_done, c)
    for h in range(HEADS_M):
        mm = pe.transpose(ps[:, B_T, h * P:(h + 1) * P], tile(m, HEADS_M + h, c), ident[:, :])
    mm.then_inc(m.k_done, 1)
    if c > 0:
        pe.wait_ge(m.sc_done, c)
    for h in range(HEADS_M):
        mm = pe.matmul(ps[:, B_S, h * P:(h + 1) * P], tile(m, HEADS_M + h, c), tile(m, h, c),
                       start=True, stop=True)
    mm.then_inc(m.s_done, 1)


def chunk_decay_vector(dve, m, causal, c):
    dve.wait_ge(m.bc_loaded[c % 2], 32 * (c // 2 + 1))
    if c == 0:
        dve.wait_ge(m.g_act, 4)
    else:
        dve.wait_ge(m.sc_done, c)
    for h in range(HEADS_M):
        r = h * m.T + c
        ins = dve.scalar_tensor_tensor(m.dm[:, h, :], m.bc[c % 2][:, 0, h, :], m.col[:, 0, r:r + 1],
                                       causal[:, :], ALU.add, ALU.min)
    ins.then_inc(m.dm_shift, 1)


def chunk_exps_scalar(act, m, ps, c):
    act.wait_ge(m.bc_loaded[c % 2], 32 * (c // 2 + 1))
    act.activation(m.bc[c % 2][:, 1, :, :], m.bc[c % 2][:, 1, :, :], ACT.Exp).then_inc(m.wg_done, 1)
    act.wait_ge(m.dm_shift, c + 1)
    act.activation(m.dm[:, :, :], m.dm[:, :, :], ACT.Exp).then_inc(m.dm_done, 1)
    act.wait_ge(m.k_done, c + 1)
    if c == 0:
        act.wait_ge(m.g_sb, 14)
    else:
        act.wait_ge(m.c_done, c)
    for h in range(HEADS_M):
        r = h * m.T + c
        ins = act.activation(m.kw[:, h, :], ps[:, B_T, h * P:(h + 1) * P], ACT.Copy, scale=m.col[:, 1, r:r + 1])
    ins.then_inc(m.kw_done, 1)


def chunk_weight_vector(dve, m, ps, c):
    dve.wait_ge(m.s_done, c + 1)
    dve.wait_ge(m.dm_done, c + 1)
    if c > 0:
        dve.wait_ge(m.n_done, c)
    dve.scalar_tensor_tensor(m.sc[:, :, :], ps[:, B_S, :].rearrange("p (h l) -> p h l", h=HEADS_M), QK_SCALE,
                             m.dm[:, :, :], ALU.mult, ALU.mult).then_inc(m.sc_done, 1)
    dve.wait_ge(m.wg_done, c + 1)
    dve.tensor_tensor(m.qw[:, :, :], m.qk[:, 0:HEADS_M, c * P:(c + 1) * P], m.bc[c % 2][:, 1, :, :], ALU.mult)\
       .then_inc(m.qw_done, 1)


def chunk_products_tensor(pe, m, ps, c):
    v = lambda h: m.tok[:, c, h * NV:(h + 1) * NV]
    pe.wait_ge(m.sc_done, c + 1)
    pe.wait_ge(m.qw_done, c + 1)
    if c == 0:
        pe.wait_ge(m.left[0], 3 * m.T // 2)
        pe.wait_ge(m.left[1], 3 * m.T // 2)
        pe.wait_ge(m.zeroed, m.zeros)
        pe.wait_ge(m.ha_done, 4 * m.T)
        pe.wait_ge(m.pt_ready, 2 * m.T)
        pe.wait_ge(m.exps, 2 * m.T)
    else:
        pe.wait_ge(m.state, c)
        pe.wait_ge(m.hm_norm, c)
    N, C = head_banks(ps, B_N), head_banks(ps, B_C)
    for h in range(HEADS_M):
        out = N[:, h // 2, h % 2, :]
        mm = pe.matmul(out, m.sc[:, h, :], v(h), start=True, stop=(c == 0))
        if c > 0:
            mm = pe.matmul(out, m.qw[:, h, :], m.C[(c - 1) % 2][:, h, :], start=False, stop=True)
    mm.then_inc(m.n_done, 1)
    pe.wait_ge(m.kw_done, c + 1)
    if c > 0:
        pe.wait_ge(m.hs_low, 2 * c)
    for h in range(HEADS_M):
        mm = pe.matmul(C[:, h // 2, h % 2, :], m.kw[:, h, :], v(h), start=True, stop=True)
    mm.then_inc(m.c_done, 1)


def chunk_state_vector(dve, m, ps, c):
    dve.wait_ge(m.c_done, c + 1)
    C = head_banks(ps, B_C)
    if c == 0:
        dve.wait_ge(m.g_act, 3)
        ins = dve.tensor_copy(m.C[0][:, :, :].rearrange("p (b h) e -> p b h e", b=2), C)
    else:
        for h in range(HEADS_M):
            r = h * m.T + c
            ins = dve.scalar_tensor_tensor(m.C[c % 2][:, h, :], m.C[(c - 1) % 2][:, h, :], m.dec[:, r:r + 1],
                                           C[:, h // 2, h % 2, :], ALU.mult, ALU.add)
    ins.then_inc(m.state, 1)


def chunk_stats_vector(dve, m, ps, c):
    then = m.chain.then
    N = head_banks(ps, B_N)
    dve.wait_ge(m.n_done, c + 1)
    sm = {n: x[:, 0:HEADS_M] for n, x in m.sm.items()}
    pair = lambda x: x.rearrange("p (b h) -> p b h", b=2)
    if c > 0:
        dve.wait_ge(m.hm_norm, c)
    then(dve, dve.tensor_scalar(pair(sm["ad"]), N[:, :, :, P], -1.0, None, ALU.mult))
    then(dve, dve.tensor_tensor(pair(sm["ad"]), pair(sm["ad"]), N[:, :, :, P], ALU.max))
    emt = m.col[:, 2, :].rearrange("p (h t) -> p h t", h=HEADS_M)[:, :, c]
    then(dve, dve.tensor_tensor(sm["ad"][:, :], sm["ad"][:, :], emt, ALU.max))
    then(dve, dve.reciprocal(sm["r"][:, :], sm["ad"][:, :]))
    for h in range(HEADS_M):
        dve.bn_stats(m.bn[:, h, :], N[:, h // 2, h % 2, 0:P]).then_inc(m.chain.sem, 1)
        m.chain.count += 1
    dve.wait_ge(m.chain.sem, m.chain.count)
    for h in range(HEADS_M):
        dve.bn_aggr(m.mv[:, h, :], m.bn[:, h, :]).then_inc(m.chain.sem, 1)
        m.chain.count += 1
    dve.wait_ge(m.chain.sem, m.chain.count)
    then(dve, dve.tensor_tensor(sm["vr"][:, :], m.mv[:, :, 1], sm["r"][:, :], ALU.mult))
    then(dve, dve.tensor_tensor(sm["vr"][:, :], sm["vr"][:, :], sm["r"][:, :], ALU.mult))
    n = HEADS_M + (c >= 2)
    if c >= 2:
        dve.wait_ge(m.y_summed, c - 1)
    inverse_root(dve, m.chain, m.sm["rs"][:, 0:n], m.sm["vr"][:, 0:n], 1.0, EPS, m.sm["guess"][:, 0:n],
                 m.sm["half"][:, 0:n], m.sm["value"][:, 0:n])
    then(dve, dve.tensor_tensor(sm["rs"][:, :], sm["rs"][:, :], sm["r"][:, :], ALU.mult))
    dve.scalar_tensor_tensor(sm["nb"][:, :], m.mv[:, :, 0], -1.0, sm["rs"][:, :], ALU.mult, ALU.mult)\
       .then_inc(m.norm_ready, 1)


def chunk_norm_scalar(act, m, ps, c):
    act.wait_ge(m.norm_ready, c + 1)
    if c > 0:
        act.wait_ge(m.hm_turned, c)
    if c > 1:
        act.wait_ge(m.y_summed, c - 1)
    N = head_banks(ps, B_N)
    for h in range(HEADS_M):
        ins = act.activation(m.hm[:, h, :], N[:, h // 2, h % 2, 0:P], ACT.Identity,
                             bias=m.sm["nb"][:, h:h + 1], scale=m.sm["rs"][:, h:h + 1])
    ins.then_inc(m.hm_norm, 1)


def chunk_gate_vector(dve, m, c):
    dve.wait_ge(m.hm_norm, c + 1)
    hm = m.hm[:, :, :].rearrange("p h v -> p (h v)")
    dve.tensor_tensor(hm, hm, m.tok[:, c, OG:OG + NO], ALU.mult).then_inc(m.hm_done, 1)


def chunk_turn_tensor(pe, m, ps, ident, c):
    pe.wait_ge(m.hm_done, c + 1)
    pe.wait_ge(m.state, c + 1)
    for h in range(HEADS_M):
        mm = pe.transpose(ps[:, B_C, h * P:(h + 1) * P], m.hm[:, h, :], ident[:, :])
    mm.then_inc(m.hm_turned, 1)


def out_in(m, ps, c):
    return (ps[:, B_C, :].rearrange("p (h l) -> p h l", h=HEADS_M),
            m.tok[:, c, AQ:AQ + NQ].rearrange("p (j q) -> p j q", j=4))


def out_high_scalar(act, m, ps, c):
    if c >= 2:
        act.wait_ge(m.y_done, c - 1)
    act.wait_ge(m.hm_turned, c + 1)
    for q, src in enumerate(out_in(m, ps, c)):
        act.activation(m.hs[c % 2][:, 0, 4 * q:4 * q + 4, :], src, ACT.Copy).then_inc(m.hs_high, 1)


def out_low_vector(dve, m, ps, c):
    for q, src in enumerate(out_in(m, ps, c)):
        dve.wait_ge(m.hs_high, 2 * c + q + 1)
        part_low(dve, m.hs[c % 2][:, 1, 4 * q:4 * q + 4, :], src, m.hs[c % 2][:, 0, 4 * q:4 * q + 4, :])\
           .then_inc(m.hs_low, 1)


def out_tensor(pe, m, ps, c, n):
    pe.wait_ge(m.hs_low, 2 * c + 2)
    pe.wait_ge(m.w_low, 2 * n + 2)
    if c > 0:
        pe.wait_ge(m.y_left, c)
    hs = m.hs[c % 2]
    for k in range(m.K):
        mm = three_passes(pe, ps[:, B_Y + n, :], [hs[:, a, k, :] for a in range(2)],
                          [w[:, k, n * BANK:(n + 1) * BANK] for w in m.wo], k == 0, k == m.K - 1)
    mm.then_inc((m.y_half, m.y_done)[n], 1)


def out_leave_scalar(act, m, ps, c):
    D = m.wo[0].shape[2]
    act.wait_ge(m.y_done, c + 1)
    act.wait_ge(m.hm_turned, c + 1)
    act.activation(m.tok[:, c, 0:D].rearrange("p (b c) -> p b c", c=BANK), ps[:, B_Y:B_Y + 2, :], ACT.Copy)\
       .then_inc(m.y_left, 1)
    act.wait_ge(m.y_left, c + 1)
    act.wait_ge(m.hm_turned, min(c + 2, m.T))
    if c > 0:
        act.wait_ge(m.y_summed, c)
    if c == m.T - 1:
        act.wait_ge(m.y_scaled, c)
    act.activation(m.junk[:, :], m.tok[:, c, 0:D], ACT.Square, scale=D ** -0.5,
                   accum_out=m.sm["vr"][:, 4:5]).then_inc(m.y_summed, 1)


def out_scale_vector(dve, m, c):
    if c >= m.T - 2:
        dve.wait_ge(m.y_summed, c + 1)
        inverse_root(dve, m.chain, m.sm["rs"][:, 4:5], m.sm["vr"][:, 4:5], 1.0, EPS, m.sm["guess"][:, 4:5],
                     m.sm["half"][:, 4:5], m.sm["value"][:, 4:5])
    if c == 0:
        dve.wait_ge(m.post_loaded, 16)
    y = m.tok[:, c, 0:m.wo[0].shape[2]].rearrange("p (b c) -> p b c", c=BANK)
    dve.scalar_tensor_tensor(y, y, m.sm["rs"][:, 4:5], m.gain_post, ALU.mult, ALU.mult)\
       .then_inc(m.y_scaled, 1)


def out_residual_pool(pool, m, c, res, out, D):
    if c > 0:
        pool.wait_ge(m.h_done, c)
    pool.dma_start(m.res[:, :], res[c * P:(c + 1) * P, :]).then_inc(m.res_loaded, 16)
    pool.wait_ge(m.y_scaled, c + 1)
    pool.wait_ge(m.res_loaded, 16 * (c + 1))
    h = m.tok[:, c, 0:D]
    pool.tensor_tensor(h, h, m.res[:, :], ALU.add).then_inc(m.h_done, 1)
    pool.wait_ge(m.h_done, c + 1)
    pool.dma_start(out[c * P:(c + 1) * P, :], h).then_inc(m.stored, 16)


def chunks_tensor(pe, m, ps, ident):
    chunk_scores_tensor(pe, m, ps, ident, 0)
    for c in range(m.T):
        chunk_products_tensor(pe, m, ps, c)
        if c + 1 < m.T:
            chunk_scores_tensor(pe, m, ps, ident, c + 1)
        if c:
            out_tensor(pe, m, ps, c - 1, 0)
        chunk_turn_tensor(pe, m, ps, ident, c)
        if c:
            out_tensor(pe, m, ps, c - 1, 1)
    out_tensor(pe, m, ps, m.T - 1, 0)


def chunks_scalar(act, m, ps, nm, tiles, ready):
    chunk_exps_scalar(act, m, ps, 0)
    for c in range(m.T):
        if c > 3:
            act.wait_ge(nm.summed, c - 3)
        chunk_norm_scalar(act, m, ps, c)
        if c + 1 < m.T:
            chunk_exps_scalar(act, m, ps, c + 1)
        if c == 0:
            out_weights_scalar(act, m, 1)
        out_high_scalar(act, m, ps, c)
        if c:
            out_leave_scalar(act, m, ps, c - 1)
        if c >= 3:
            square_tiles(act, nm, tiles, ready, c - 3)


def chunks_vector(dve, m, ps, causal):
    chunk_weight_vector(dve, m, ps, 0)
    for c in range(m.T):
        chunk_stats_vector(dve, m, ps, c)
        chunk_state_vector(dve, m, ps, c)
        chunk_gate_vector(dve, m, c)
        if c + 1 < m.T:
            chunk_decay_vector(dve, m, causal, c + 1)
            chunk_weight_vector(dve, m, ps, c + 1)
        if c == 0:
            out_weights_vector(dve, m, 1)
        out_low_vector(dve, m, ps, c)
        if c >= 2:
            out_scale_vector(dve, m, c - 2)
    out_scale_vector(dve, m, m.T - 2)



def bass_hymba_layer(nc, x, positions, ff1_pre_w, ff1_w_gate, ff1_w_up, ff1_w_down, ff1_post_w,
                     mix_pre_w, w_in, conv_w, conv_b, b_igate, b_fgate, mlstm_norm_w, sinks, w_out,
                     mix_post_w, ff2_pre_w, ff2_w_gate, ff2_w_up, ff2_w_down, ff2_post_w, out):
    _, S, D = x.shape
    F = ff1_w_gate.shape[2]
    T, K = S // P, D // P
    x, out = x[0], out[0]
    row = lambda w: w.to_broadcast([P, w.shape[1]])
    by_rows = lambda w: w[0].rearrange("(k p) f -> p k f", p=P)

    with ExitStack() as ctx:
        mem = Memory(nc, ctx)
        ps = ctx.enter_context(nc.psum_tensor("ps", [P, 8, BANK], F32))
        h1 = nc.dram_tensor("after_ff1", [S, D], F32, kind="Internal").ap()
        h2 = nc.dram_tensor("after_mixer", [S, D], F32, kind="Internal").ap()
        gate_rows = nc.dram_tensor("gate_rows", [HEADS_M * T, 2, P], F32, kind="Internal").ap()

        ident = mem.at("ident", [P, P], F32, 205 * KB)
        causal = mem.at("causal", [P, P], F32, 205 * KB + 512)
        xn = [mem.at("xn_high", [P, K, S], FR, 0), mem.at("xn_low", [P, K, S], FR, 32 * KB)]
        small = 206 * KB + 512
        root = [mem.at("root_guess", [P, T], I32, small), mem.at("root_half", [P, T], F32, small + 32),
                mem.at("root_value", [P, T], F32, small + 64)]
        sums = [[mem.at(f"ssq{i}", [P, T], F32, small + 96 + 64 * i),
                 mem.at(f"rstd{i}", [P, T], F32, small + 128 + 64 * i)] + root for i in range(6)]

        xt = mem.at("x_tiles", [P, T, D], F32, 64 * KB)
        xs1 = [mem.at(f"norm1_xs{i}", [P, D], F32, (96 + 4 * i) * KB) for i in range(2)]
        gain1 = mem.at("norm1_gain", [P, D], F32, 104 * KB)
        junk1 = mem.at("norm1_junk", [P, D], F32, 108 * KB)
        n1 = Norm(mem, "norm1", sums[0], [xs[:, :] for xs in xs1] * (T // 2), junk1[:, :], gain1[:, :].unsqueeze(1), [4, 5, 6, 7] * (T // 2))
        x_loaded = [mem.sem(f"x_loaded{t}") for t in range(T)]
        gain1_loaded = mem.sem("norm1_gain_loaded")
        set_up = mem.sem("constants_set")

        f1 = FeedForward(mem, "ff1", D, F, S, xn, True)
        f1.ssq, f1.rstd, f1.guess, f1.half, f1.value = sums[1]
        f1.gains = 32
        nm = Norm(mem, "norm_mix", sums[2], [f1.y[:, k, :] for _, n in GROUPS for k in range(n)], None,
                  f1.gain_pre[:, :].unsqueeze(1), [6, 7] * T)

        m = Mixer(mem, S, D)
        m.ssq, m.rstd, m.guess, m.half, m.value = sums[3]
        m.zeros, m.consts = 2, 16 * (CONV + 1 + 2 + 3)

        h_tiles = [m.tok[:, t, 0:D] for t in range(T)]
        n2 = Norm(mem, "norm2", sums[4], h_tiles, m.junk[:, :], m.gain_next,
                  [4, 5, 2, 3] * (T // 4) + [4, 5, 6, 7] * (T // 4))
        gain2_loaded = mem.sem("norm2_gain_loaded")
        f2 = FeedForward(mem, "ff2", D, F, S, xn, False)
        f2.ssq, f2.rstd, f2.guess, f2.half, f2.value = sums[5]
        f2.gains = 16

        x_tiles = [xt[:, t, :] for t in range(T)]
        block = ctx.enter_context(nc.Block())

        @block.sync
        def _(sp):
            w1, w2 = ([by_rows(g), by_rows(u)] for g, u in ((ff1_w_gate, ff1_w_up), (ff2_w_gate, ff2_w_up)))
            for half in range(2):
                for t in range(T // 2 * half, T // 2 * (half + 1)):
                    sp.dma_start(xt[:, t, :], x[t * P:(t + 1) * P, :]).then_inc(x_loaded[t], 16)
                gate_up_sync(sp, f1, w1, half == 0)
            down_sync(sp, f1, ff1_w_down[0])
            sp.wait_ge(f1.unit_done, len(GROUPS) * (F // P) - RING)
            tokens_sync(sp, m, w_in[0])
            qk_sync(sp, m, w_in[0])
            out_weights_sync(sp, m, w_out[0], gate_rows)
            sp.wait_ge(m.pt_ready, 2 * T)
            sp.wait_ge(m.pv, 2 * T)
            gate_up_sync(sp, f2, w2, True)
            gate_up_sync(sp, f2, w2, False)
            down_sync(sp, f2, ff2_w_down[0])

        @block.gpsimd
        def _(pool):
            pool.dma_start(gain1[:, :], row(ff1_pre_w)).then_inc(gain1_loaded, 16)
            pool.memset(ident[:, :], 0.0).then_inc(set_up, 1)
            pool.memset(causal[:, :], 0.0).then_inc(set_up, 1)
            pool.wait_ge(set_up, 2)
            pool.affine_select(out=ident[:, :], in_=ident[:, :], compare_op=ALU.not_equal, fill=1.0,
                               base=0, pattern=[[-1, P]], channel_multiplier=1).then_inc(set_up, 1)
            pool.affine_select(out=causal[:, :], in_=causal[:, :], compare_op=ALU.is_ge, fill=-BIG,
                               base=0, pattern=[[1, P]], channel_multiplier=-1).then_inc(set_up, 1)
            with nc.allow_non_contiguous_dma(reason="a few KB of per-feature constants"):
                for j in range(CONV):
                    pool.dma_start(m.conv_w[:, j, :], conv_w[0, j].rearrange("(f p) -> p f", p=P))\
                        .then_inc(m.consts_loaded, 16)
                pool.dma_start(m.conv_b[:, :], conv_b[0].rearrange("(f p) -> p f", p=P))\
                    .then_inc(m.consts_loaded, 16)
                for e in range(2):
                    pool.dma_start(m.sink[64 * e:64 * e + 64, :],
                                   sinks.rearrange("a (j e) -> a e j", e=2)[:, e, :].to_broadcast([64, 4]))\
                        .then_inc(m.consts_loaded, 16)
            pool.wait_ge(f1.h_done, F // P)
            pool.dma_start(f1.gain_post[:, :], row(ff1_post_w)).then_inc(f1.gains_loaded, 16)
            pool.dma_start(f1.gain_pre[:, :], row(mix_pre_w)).then_inc(f1.gains_loaded, 16)
            down_pool(pool, f1, x, h1, nm)

            pool.wait_ge(f1.unit_done, len(GROUPS) * (F // P))
            pool.dma_start(m.gain_norm[:, :], row(mlstm_norm_w.rearrange("a h d -> a (h d)")))\
                .then_inc(m.consts_loaded, 16)
            with nc.allow_non_contiguous_dma(reason="positions and gate biases"):
                pool.dma_start(m.pos_i[:, :], positions[0].rearrange("(t p) -> p t", p=P))\
                    .then_inc(m.pos_loaded, 16)
                for g, b in enumerate((b_igate, b_fgate)):
                    pool.dma_start(m.gbias[:, g, :], row(b)).then_inc(m.consts_loaded, 16)
            pool.memset(m.tok[:, :, 0:HEADS_M * NV].rearrange("p t (h e) -> p t h e", e=NV)[:, :, :, P], 1.0)\
                .then_inc(m.zeroed, 1)
            pool.memset(m.qbd[:, :, :, :], 0.0).then_inc(m.zeroed, 1)
            for i in range(T):
                shifted_values_pool(pool, m, i)
            pool.wait_ge(m.g_sb, GATE_DVE[-1])
            pool.dma_start(gate_rows, m.gout[:, :, :]).then_inc(m.g_stored, 16)
            gains = lambda w: row(w).rearrange("p (a c) -> p a c", a=2)
            pool.wait_ge(m.hs_low, 4)
            pool.dma_start(m.gain_post, gains(mix_post_w)).then_inc(m.post_loaded, 16)
            pool.wait_ge(m.g_act, GATE_ACT[-1])
            pool.wait_ge(f1.stored, 16 * T)
            for c in range(T):
                out_residual_pool(pool, m, c, h1, h2, D)
                if c == 2:
                    pool.wait_ge(m.hs_low, 8)
                    pool.dma_start(m.gain_next, gains(ff2_pre_w)).then_inc(gain2_loaded, 16)

            pool.wait_ge(m.stored, 16 * T)
            pool.wait_ge(f2.h_done, F // P)
            pool.dma_start(f2.gain_post[:, :], row(ff2_post_w)).then_inc(f2.gains_loaded, 16)
            down_pool(pool, f2, h2, out, None)
            pool.wait_ge(f2.stored, 16 * T)

        @block.scalar
        def _(act):
            start_scalar(act, n1, ps, xn, x_tiles, lambda e, t: e.wait_ge(x_loaded[t], 16), f1)
            gate_up_scalar(act, f1, ps)
            down_scalar(act, f1, ps, nm, xn)
            tokens_scalar(act, m, ps, xn, f1, nm)
            heads_scalar(act, m, ps)
            h_ready = lambda e, t: (e.wait_ge(m.h_done, t + 1), e.wait_ge(m.y_summed, min(t + 3, T)))
            chunks_scalar(act, m, ps, n2, h_tiles, h_ready)
            act.wait_ge(m.y_half, T)
            for t in range(2):
                high_tile(act, n2, ps, xn, t)
            out_leave_scalar(act, m, ps, T - 1)
            start_scalar(act, n2, ps, xn, h_tiles, h_ready, f2,
                         lambda e: e.wait_ge(m.h_done, T), 2, T - 3)
            gate_up_scalar(act, f2, ps)
            down_scalar(act, f2, ps, None, xn)

        @block.vector
        def _(dve):
            start_vector(dve, n1, ps, xn, x_tiles, lambda e: e.wait_ge(gain1_loaded, 16), D, f1)
            gate_up_vector(dve, f1, ps)
            down_vector(dve, f1, ps, nm, xn, D, 0.5)
            tokens_vector(dve, m, ps, xn, f1, nm, D)
            dve.wait_ge(f1.stored, 16 * T)
            m.chain.then(dve, dve.memset(m.xp[:, 0:3], 0.0))
            dve.wait_ge(set_up, 4)
            heads_vector(dve, m, ps, causal)
            chunks_vector(dve, m, ps, causal)
            start_vector(dve, n2, ps, xn, h_tiles, lambda e: e.wait_ge(gain2_loaded, 16), D, f2,
                         lambda e, t: e.wait_ge(m.stored, 16 * (t + 1)),
                         lambda: out_scale_vector(dve, m, T - 1))
            dve.wait_ge(m.stored, 16 * T)
            gate_up_vector(dve, f2, ps)
            down_vector(dve, f2, ps, None, xn, D, 0.5)

        @block.tensor
        def _(pe):
            pe.wait_ge(set_up, 4)
            start_tensor(pe, n1, ps, ident, f1, xn, T, K)
            gate_up_tensor(pe, f1, ps, xn)
            down_tensor(pe, f1, ps, nm, ident)
            tokens_tensor(pe, m, ps, xn, f1, nm, ident)
            heads_tensor(pe, m, ps, xn, ident, m.gout[:, 0, :])
            chunks_tensor(pe, m, ps, ident)
            for t in range(2):
                turn_tile(pe, n2, ps, ident, t, K)
            out_tensor(pe, m, ps, T - 1, 1)
            start_tensor(pe, n2, ps, ident, f2, xn, T, K, 2)
            gate_up_tensor(pe, f2, ps, xn)
            down_tensor(pe, f2, ps, None, ident)


_INS = ['x', 'positions', 'ff1_pre_w', 'ff1_w_gate', 'ff1_w_up', 'ff1_w_down', 'ff1_post_w', 'mix_pre_w',
        'w_in', 'conv_w', 'conv_b', 'b_igate', 'b_fgate', 'mlstm_norm_w', 'sinks', 'w_out', 'mix_post_w',
        'ff2_pre_w', 'ff2_w_gate', 'ff2_w_up', 'ff2_w_down', 'ff2_post_w']


def kernel(**inputs):
    import numpy as _np
    import concourse.bacc as _bacc
    from concourse import mybir as _mybir
    from concourse.bass_utils import run_bass_kernel_spmd as _run

    nc = _bacc.Bacc("TRN2", target_bir_lowering=False, num_devices=1)
    arrays, args = {}, []
    for name in _INS:
        a = _np.ascontiguousarray(inputs[name])
        arrays[f"in_{name}_dram"] = a
        args.append(nc.dram_tensor(f"in_{name}_dram", a.shape, _mybir.dt.from_np(a.dtype), kind="ExternalInput").ap())
    out = nc.dram_tensor("out_dram", inputs["x"].shape, _mybir.dt.float32, kind="ExternalOutput").ap()
    bass_hymba_layer(nc, *args, out)
    r = _run(nc, [arrays], core_ids=[0])
    return r.results[0]["out_dram"]
```

```python
from contextlib import ExitStack

import concourse.bass as bass
import numpy as np
from concourse import mybir

P = 128
F32 = mybir.dt.float32
FR = mybir.dt.float32r
BF = mybir.dt.bfloat16
I32 = mybir.dt.int32
ALU = mybir.AluOpType
ACT = mybir.ActivationFunctionType
AX = mybir.AxisListType.X
BANK = 512
KB = 1024
EPS = 1e-6


class Memory:

    def __init__(self, nc, ctx):
        self.nc, self.ctx = nc, ctx
        self.base = (nc.sbuf_base + 31) // 32 * 32
        self.chain = Chain(self, "dve_step")

    def at(self, name, shape, dtype, offset):
        return self.nc.alloc_sbuf_tensor_at(name, shape, dtype, offset=self.base + offset)

    def sem(self, name):
        return self.ctx.enter_context(self.nc.semaphore(name))


class Chain:

    def __init__(self, mem, name):
        self.sem, self.count = mem.sem(name), 0

    def then(self, engine, instruction):
        instruction.then_inc(self.sem, 1)
        self.count += 1
        engine.wait_ge(self.sem, self.count)


def inverse_roots(dve, chain, *roots):
    wide = any(root[0].shape[1] > 1 for root in roots)

    def step(operation):
        for root in roots:
            operation(*root).then_inc(chain.sem, 1)
        chain.count += len(roots)
        dve.wait_ge(chain.sem, chain.count)

    step(lambda out, total, scale, bias, s:
         dve.tensor_scalar(s[2], total, -0.5 * scale, -0.5 * bias, ALU.mult, ALU.add))
    step(lambda out, total, scale, bias, s:
         dve.tensor_scalar(s[0], s[2].bitcast(I32), 1, None, ALU.arith_shift_right))
    step(lambda out, total, scale, bias, s:
         dve.tensor_scalar(s[0], s[0], -1.0, float(0x5F3759DF - 2 ** 30 - 2 ** 22), ALU.mult, ALU.add))
    for last in (False, False, True):
        step(lambda out, total, scale, bias, s:
             dve.tensor_tensor(s[1], s[0].bitcast(F32), s[0].bitcast(F32), ALU.mult)
             if wide else
             dve.scalar_tensor_tensor(s[1], s[0].bitcast(F32), s[2], s[0].bitcast(F32), ALU.mult, ALU.mult))
        if wide:
            step(lambda out, total, scale, bias, s: dve.tensor_tensor(s[1], s[1], s[2], ALU.mult))
        step(lambda out, total, scale, bias, s:
             dve.scalar_tensor_tensor(out if last else s[0].bitcast(F32), s[1], 1.5, s[0].bitcast(F32),
                                      ALU.add, ALU.mult))


class Norm:

    def __init__(self, mem, name, sums, xs, junk, gain, banks):
        self.xs, self.junk, self.gain, self.banks = xs, junk, gain, banks
        self.ssq, self.rstd, self.scratch = sums
        self.summed = mem.sem(f"{name}_squares_summed")
        self.xs_ready = mem.sem(f"{name}_xs_ready")
        self.turned = mem.sem(f"{name}_turned")
        self.high = mem.sem(f"{name}_high_written")
        self.low = mem.sem(f"{name}_low_written")
        self.chain = mem.chain


class FeedForward:

    def __init__(self, mem, name, D, F, S, xn, norm_follows):
        at = lambda n, shape, dt, kb: mem.at(f"{name}_{n}", shape, dt, int(kb * KB))
        s = lambda n: mem.sem(f"{name}_{n}")
        K, FT = D // P, F // P
        self.name = name
        self.h = at("h", [P, FT, S], F32, 64)
        self.raw = [at(f"raw_{m}", [P, K, P], F32, 152 + 4 * i) for i, m in enumerate(("gate", "up"))]
        self.part = [[at(f"part_{m}{b}", [P, 2, K, P], FR, 160 + 16 * b + 8 * i)
                      for i, m in enumerate(("gate", "up"))] for b in range(2)]
        self.raw_loaded = [s("gate_loaded"), s("up_loaded")]
        self.w_high = s("gate_up_high")
        self.w_low = s("gate_up_low")
        self.gate_done, self.up_done = s("gate_done"), s("up_done")
        self.silu_done, self.h_done = s("silu_done"), s("h_done")
        own = at("down_part", [P, 2, D // 256, 256], FR, 152)
        tail = slice(S - 256, S)
        self.dpart = [[own[:, a, :, :] for a in range(2)]] + \
            [[x[:, 4 * b:4 * b + 4, tail] for x in xn] for b in range(2)]
        self.hpart = [at(f"h_part{b}", [P, 2, 3 * P], FR, 160 + 3 * b) for b in range(3)]
        self.y = at("y", [P, 3, D], F32, 169)
        self.gain_post = at("gain_post", [P, D], F32, 185)
        gain_pre = at("gain_pre", [P, D], F32, 189)
        self.draw = [at(f"down_raw{b}", [P, D], F32, kb) for b, kb in enumerate((193, 197, 201))]
        self.res = [at("res", [P, D], F32, 181)]
        if norm_follows:
            self.gain_pre = gain_pre
            self.res += self.draw[1:]
            self.place = [0] * (S // P - 2) + [1, 2]
        else:
            self.res.append(gain_pre)
            self.place = [t % 2 for t in range(S // P)]
        self.draw_loaded = [s(f"down_loaded{b}") for b in range(3)]
        self.d_high, self.d_low = s("down_high"), s("down_low")
        self.hp_high, self.hp_low = s("h_part_high"), s("h_part_low")
        self.unit_done, self.tile_done = s("down_unit_done"), s("down_tile_done")
        self.y_even, self.y_odd = s("y_even_banks_left"), s("y_odd_banks_left")
        self.gains_loaded = s("gains_loaded")
        self.y_summed = s("y_squares_summed")
        self.res_loaded = [s(f"residual_loaded{i}") for i in range(len(self.res))]
        self.y_final = s("y_final")
        self.stored, self.last_stored = s("stored"), None if norm_follows else s("last_stored")
        self.chain = mem.chain


def part_low(dve, low, value, high):
    return dve.tensor_tensor(low, value, high.bitcast(F32), ALU.subtract)



def turn_tile(pe, nm, ps, ident, t, K):
    pe.wait_ge(nm.xs_ready, t + 1)
    for q in range(2):
        bank = nm.banks[2 * t + q]
        before = [j for j in range(2 * t + q) if nm.banks[j] == bank]
        if before:
            pe.wait_ge(nm.low, before[-1] + 1)
        for j in range(K // 2):
            k = q * (K // 2) + j
            mm = pe.transpose(ps[:, bank, j * P:(j + 1) * P], nm.xs[t][:, k * P:(k + 1) * P], ident[:, :])
        mm.then_inc(nm.turned, 1)


def high_tile(act, nm, ps, xn, t):
    for q in range(2):
        act.wait_ge(nm.turned, 2 * t + q + 1)
        bank = nm.banks[2 * t + q]
        act.activation(xn[0][:, 4 * q:4 * q + 4, t * P:(t + 1) * P],
                       ps[:, bank, :].rearrange("p (k c) -> p k c", c=P), ACT.Copy).then_inc(nm.high, 1)


def low_tile(dve, nm, ps, xn, t):
    for q in range(2):
        dve.wait_ge(nm.high, 2 * t + q + 1)
        bank = nm.banks[2 * t + q]
        at = (slice(None), slice(4 * q, 4 * q + 4), slice(t * P, (t + 1) * P))
        part_low(dve, xn[1][at], ps[:, bank, :].rearrange("p (k c) -> p k c", c=P),
                 xn[0][at]).then_inc(nm.low, 1)


def scale_tile(dve, nm, t, tile):
    before = [j for j in range(t) if nm.xs[j] is nm.xs[t]]
    if before:
        dve.wait_ge(nm.turned, 2 * before[-1] + 2)
    halves = lambda x: x.rearrange("p (a c) -> p a c", a=nm.gain.shape[1])
    dve.scalar_tensor_tensor(halves(nm.xs[t]), halves(tile), nm.rstd[:, t:t + 1], nm.gain,
                             ALU.mult, ALU.mult).then_inc(nm.xs_ready, 1)


def norm_root(dve, nm, a, b, D):
    dve.wait_ge(nm.summed, b)
    return nm.rstd[:, a:b], nm.ssq[:, a:b], 1.0 / D, EPS, [x[:, a:b] for x in nm.scratch]


def norm_roots(dve, nm, a, b, D):
    inverse_roots(dve, nm.chain, norm_root(dve, nm, a, b, D))


def norm_square(act, nm, t, tile, junk):
    if t > 0:
        act.wait_ge(nm.summed, t)
    act.activation(junk, tile, ACT.Square, accum_out=nm.ssq[:, t:t + 1]).then_inc(nm.summed, 1)



def square_tiles(act, nm, tiles, ready, which, junk):
    for t in which:
        ready(act, t)
        norm_square(act, nm, t, tiles[t], junk)


def start_scalar(act, nm, ps, xn, tiles, ready, s):
    square = lambda *ts: square_tiles(act, nm, tiles, ready, ts, nm.junk)

    def high(*ts):
        for t in ts:
            high_tile(act, nm, ps, xn, t)

    square(0, 1, 2, 3)
    high(0)
    gate_up_high(act, s, 0, 0, True, 0)
    high(1, 2)
    square(4)
    high(3)
    gate_up_high(act, s, 0, 0, True, 1)
    square(5, 6, 7)
    high(4, 5, 6, 7)


def start_vector(dve, nm, ps, xn, tiles, gain_ready, D, s):
    def scale(*ts):
        for t in ts:
            if t % 2 == 0:
                norm_roots(dve, nm, t, t + 2, D)
            if t == 0:
                gain_ready(dve)
            scale_tile(dve, nm, t, tiles[t])

    def low(t):
        low_tile(dve, nm, ps, xn, t)

    for first in (0, 4):
        scale(first, first + 1)
        for t in (first, first + 1):
            low(t)
            scale(t + 2)
        low(first + 2)
        if first == 0:
            gate_up_low(dve, s, 0, 0, 0)
        low(first + 3)
        if first == 0:
            gate_up_low(dve, s, 0, 0, 1)


def resume_scalar(act, nm, ps, xn, tiles, ready, s, T, up_free, between):
    squares = lambda *ts: square_tiles(act, nm, tiles, ready, ts, nm.junk)
    squares(T - 4)
    gate_up_high(act, s, 0, 0, True, 0)
    for t in range(2):
        high_tile(act, nm, ps, xn, t)
    between()
    for t in range(2, T // 2):
        high_tile(act, nm, ps, xn, t)
    squares(T - 3)
    up_free(act)
    gate_up_high(act, s, 0, 0, True, 1)
    squares(T - 2, T - 1)
    for t in range(T // 2, T):
        high_tile(act, nm, ps, xn, t)


def resume_vector(dve, nm, ps, xn, tiles, D, s, T, stored, between):
    def scale(t):
        stored(dve, t)
        scale_tile(dve, nm, t, tiles[t])

    def low(t):
        low_tile(dve, nm, ps, xn, t)

    scale(3)
    low(0)
    low(1)
    gate_up_low(dve, s, 0, 0, 0)
    low(2)
    low(3)
    scale(4)
    between(norm_root(dve, nm, 5, 6, D))
    gate_up_low(dve, s, 0, 0, 1)
    scale(5)
    low(4)
    norm_roots(dve, nm, 6, 8, D)
    scale(6)
    scale_tile(dve, nm, 7, tiles[7])
    for t in range(5, T):
        low(t)


def start_tensor(pe, nm, ps, ident, s, xn, T, K, turned=0):
    half = T // 2
    for t in range(turned, half):
        turn_tile(pe, nm, ps, ident, t, K)
    for th in range(2):
        for m in range(2):
            pe.wait_ge(nm.low, T * (th + 1))
            pe.wait_ge(s.w_low, m + 1)
            mm = gate_up_products(pe, s, ps, xn, 0, m, th)
            if th == 1:
                mm.then_inc((s.gate_done, s.up_done)[m], 1)
            else:
                for t in range(half + half // 2 * m, half + half // 2 * (m + 1)):
                    turn_tile(pe, nm, ps, ident, t, K)



def gate_up_sync(sp, s, weights, first):
    def load(f, fresh):
        for m, w in enumerate(weights):
            if not fresh:
                sp.wait_ge(s.w_low, 2 * f - 1 + m)
            sp.dma_start(s.raw[m][:, :, :], w[:, :, bass.ds(f * P, P)]).then_inc(s.raw_loaded[m], 16)

    if first:
        load(0, True)
    else:
        with sp.Fori(1, s.h.shape[1]) as f:
            load(f, False)


def gate_up_high(act, s, f, b, first, only=None):
    done = (s.gate_done, s.up_done)
    for m in range(2) if only is None else (only,):
        act.wait_ge(s.raw_loaded[m], 16 * f + 16)
        if not first:
            act.wait_ge(done[m], f - 1)
        act.activation(s.part[b][m][:, 0, :, :], s.raw[m][:, :, :], ACT.Copy).then_inc(s.w_high, 1)


def gate_up_low(dve, s, f, b, only=None):
    for m in range(2) if only is None else (only,):
        dve.wait_ge(s.w_high, 2 * f + m + 1)
        part_low(dve, s.part[b][m][:, 1, :, :], s.raw[m][:, :, :],
                 s.part[b][m][:, 0, :, :]).then_inc(s.w_low, 1)


def whole_h_tile(s, f):
    return s.h[:, f, :] if isinstance(f, int) else s.h[:, bass.ds(f, 1), :].rearrange("p a s -> p (a s)")


def gate_up_silu(act, s, ps, f, b):
    act.wait_ge(s.gate_done, f + 1)
    act.activation(whole_h_tile(s, f).rearrange("p (a c) -> p a c", c=BANK), ps[:, 4 * b:4 * b + 2, :],
                   ACT.Silu).then_inc(s.silu_done, 1)


def gate_up_product(dve, s, ps, f, b):
    dve.wait_ge(s.silu_done, f + 1)
    dve.wait_ge(s.up_done, f + 1)
    h = whole_h_tile(s, f)
    dve.tensor_tensor(h, h, ps[:, 4 * b + 2:4 * b + 4, :].rearrange("p a c -> p (a c)"),
                      ALU.mult).then_inc(s.h_done, 1)


def gate_up_scalar(act, s, ps):
    FT = s.h.shape[1]
    gate_up_high(act, s, 1, 1, True)
    gate_up_silu(act, s, ps, 0, 0)
    with act.Fori(1, FT - 1, 2) as f:
        for q in range(2):
            gate_up_high(act, s, f + (q + 1), q, False)
            gate_up_silu(act, s, ps, f + q, 1 - q)


def gate_up_vector(dve, s, ps):
    FT = s.h.shape[1]
    gate_up_low(dve, s, 1, 1)
    gate_up_product(dve, s, ps, 0, 0)
    with dve.Fori(1, FT - 1, 2) as f:
        for q in range(2):
            gate_up_low(dve, s, f + (q + 1), q)
            gate_up_product(dve, s, ps, f + q, 1 - q)


def three_passes(pe, out, a, b, start, stop):
    for q, (i, j) in enumerate(((0, 0), (0, 1), (1, 0))):
        mm = pe.matmul(out, a[i], b[j], start=start and q == 0, stop=stop and q == 2)
    return mm


def gate_up_products(pe, s, ps, xn, b, m, th):
    K, w = s.part[0][0].shape[2], s.part[b][m]
    for k in range(K):
        mm = three_passes(pe, ps[:, 4 * b + 2 * m + th, :], [w[:, i, k, :] for i in range(2)],
                          [x[:, k, th * BANK:(th + 1) * BANK] for x in xn], k == 0, k == K - 1)
    return mm


def gate_up_tensor(pe, s, ps, xn):
    def tile(f, b, first):
        for m, (done, free) in enumerate(((s.gate_done, s.silu_done), (s.up_done, s.h_done))):
            pe.wait_ge(s.w_low, 2 * f + m + 1)
            if not first:
                pe.wait_ge(free, f - 1)
            for th in range(2):
                mm = gate_up_products(pe, s, ps, xn, b, m, th)
            mm.then_inc(done, 1)

    tile(1, 1, True)
    with pe.Fori(2, s.h.shape[1], 2) as f:
        for q in range(2):
            tile(f + q, q, False)



GROUPS = [(0, 2), (2, 3), (5, 3)]
RING = 3


def down_sync(sp, s, w_down):
    FT = s.h.shape[1]

    def load(g, i, c):
        v = FT * g + c
        if not (isinstance(i, int) and v < RING):
            sp.wait_ge(s.d_low, 3 * i + (v - RING + 1))
        sp.dma_start(s.draw[v % RING][:, :], w_down[bass.ds((3 * i + c) * P, P), :])\
          .then_inc(s.draw_loaded[v % RING], 16)

    for g in range(len(GROUPS)):
        for c in range(4):
            load(g, 0, c)
        with sp.Fori(1, FT // 3) as i:
            for c in range(1, 4):
                load(g, i, c)


def h_tile(s, g, i, c):
    t0, n = GROUPS[g]
    f = 3 * i + c
    if isinstance(f, int):
        return s.h[:, f, t0 * P:(t0 + n) * P]
    return s.h[:, bass.ds(f, 1), t0 * P:(t0 + n) * P].rearrange("p a s -> p (a s)")


def down_high(act, s, g, i, c):
    v, n = s.h.shape[1] * g + c, GROUPS[g][1]
    if v >= RING or not isinstance(i, int):
        act.wait_ge(s.unit_done, 3 * i + (v - RING + 1))
    act.activation(s.hpart[v % RING][:, 0, 0:n * P], h_tile(s, g, i, c), ACT.Copy).then_inc(s.hp_high, 1)
    act.wait_ge(s.draw_loaded[v % RING], 16 * i + 16 * (v // RING + 1))
    high = s.dpart[v % RING][0]
    act.activation(high, s.draw[v % RING][:, :].rearrange("p (a c) -> p a c", c=high.shape[2]),
                   ACT.Copy).then_inc(s.d_high, 1)


def down_low(dve, s, g, i, c):
    v, n = s.h.shape[1] * g + c, GROUPS[g][1]
    hp, (high, low) = s.hpart[v % RING], s.dpart[v % RING]
    dve.wait_ge(s.hp_high, 3 * i + v + 1)
    part_low(dve, hp[:, 1, 0:n * P], h_tile(s, g, i, c), hp[:, 0, 0:n * P]).then_inc(s.hp_low, 1)
    dve.wait_ge(s.d_high, 3 * i + v + 1)
    part_low(dve, low, s.draw[v % RING][:, :].rearrange("p (a c) -> p a c", c=high.shape[2]),
             high).then_inc(s.d_low, 1)


def products(pe, s, ps, g, i, c, k):
    v = s.h.shape[1] * g + c
    hp, dp = s.hpart[v % RING], s.dpart[v % RING]
    half = dp[0].shape[1] // 2
    for n in range(2):
        if c == 0 and g > 0 and k < GROUPS[g - 1][1]:
            pe.wait_ge((s.y_even, s.y_odd)[n], GROUPS[g - 1][0] + k + 1)
        elif c == 0 and g > 0 and k == 2 and n == 0:
            pe.wait_ge(s.silu_done, s.h.shape[1])
        mm = three_passes(pe, ps[:, 2 * k + n, :].rearrange("p (a c) -> p a c", a=half),
                          [hp[:, a, k * P:(k + 1) * P] for a in range(2)],
                          [w[:, n * half:(n + 1) * half, :] for w in dp],
                          c == 0, isinstance(i, int) and 3 * i + c == s.h.shape[1] - 1)
    return mm


def down_products(pe, s, ps, g, i, c):
    v = s.h.shape[1] * g + c
    pe.wait_ge(s.hp_low, 3 * i + v + 1)
    pe.wait_ge(s.d_low, 3 * i + v + 1)
    last = isinstance(i, int) and 3 * i + c == s.h.shape[1] - 1
    for k in range(GROUPS[g][1]):
        mm = products(pe, s, ps, g, i, c, k)
        if last and k < GROUPS[g][1] - 1:
            mm.then_inc(s.tile_done, 1)
    mm.then_inc(s.unit_done, 1)


def down_last_units(pe, s, ps):
    g, FT = len(GROUPS) - 1, s.h.shape[1]
    n = GROUPS[g][1]
    for k in range(n):
        for f in range(FT - RING, FT):
            pe.wait_ge(s.hp_low, FT * g + f + 1)
            pe.wait_ge(s.d_low, FT * g + f + 1)
            mm = products(pe, s, ps, g, 0, f, k)
            if k == n - 1:
                mm.then_inc(s.unit_done, 1)
        if k < n - 1:
            mm.then_inc(s.tile_done, 1)


def wait_tile(eng, s, g, k):
    if k < GROUPS[g][1] - 1:
        eng.wait_ge(s.tile_done, sum(n - 1 for _, n in GROUPS[:g]) + k + 1)
    else:
        eng.wait_ge(s.unit_done, s.h.shape[1] * (g + 1))


def y_free(eng, s, nm, g):
    if g > 0:
        eng.wait_ge(s.stored, 16 * GROUPS[g][0])
        if nm:
            eng.wait_ge(nm.turned, 2 * GROUPS[g][0])


def leave_scalar(act, s, ps, g, k):
    wait_tile(act, s, g, k)
    act.activation(s.y[:, k, 0:BANK], ps[:, 2 * k, :], ACT.Copy).then_inc(s.y_even, 1)


def leave_vector(dve, s, ps, g, k):
    wait_tile(dve, s, g, k)
    dve.tensor_copy(s.y[:, k, BANK:2 * BANK], ps[:, 2 * k + 1, :]).then_inc(s.y_odd, 1)


def in_banks(ps):
    return ps[:, 6:8, :].rearrange("p b c -> p (b c)")


def y_square_scalar(act, s, g, k, nm, junk):
    t = GROUPS[g][0] + k
    if t == 0:
        act.wait_ge(s.h_done, s.h.shape[1])
    act.wait_ge(s.y_odd, t + 1)
    act.wait_ge(s.y_even, t + 1)
    if t > 0:
        act.wait_ge(s.y_summed, t)
    if nm and k == 0 and g > 0:
        act.wait_ge(nm.summed, t)
        act.wait_ge(nm.low, 2 * t)
    act.activation(junk, s.y[:, k, :], ACT.Square,
                   accum_out=s.ssq[:, t:t + 1]).then_inc(s.y_summed, 1)


def y_root(dve, s, a, b, D, factor):
    dve.wait_ge(s.y_summed, b)
    return (s.rstd[:, a:b], s.ssq[:, a:b], factor ** -2 / D, EPS * factor ** -2,
            [x[:, a:b] for x in s.scratch])


def y_roots(dve, s, a, b, D, factor):
    inverse_roots(dve, s.chain, y_root(dve, s, a, b, D, factor))


def residual_vector(dve, s, g, k, y=None):
    t = GROUPS[g][0] + k
    if t == 0:
        dve.wait_ge(s.gains_loaded, s.gains)
    s.chain.then(dve, dve.scalar_tensor_tensor(s.y[:, k, :], s.y[:, k, :] if y is None else y,
                                               s.rstd[:, t:t + 1], s.gain_post[:, :], ALU.mult, ALU.mult))
    dve.wait_ge(s.res_loaded[s.place[t]], 16 * (s.place[:t].count(s.place[t]) + 1))
    dve.tensor_tensor(s.y[:, k, :], s.y[:, k, :], s.res[s.place[t]][:, :], ALU.add)\
       .then_inc(s.y_final, 1)


def square_scalar(act, s, nm, g, k, summed, junk):
    t = GROUPS[g][0] + k
    act.wait_ge(s.y_final, t + 1)
    act.wait_ge(s.y_summed, max(summed, t + 1))
    if t > 0:
        act.wait_ge(nm.summed, t)
    act.activation(junk, s.y[:, k, :], ACT.Square,
                   accum_out=nm.ssq[:, t:t + 1]).then_inc(nm.summed, 1)


Y_SQUARE, Y_ROOTS, RESIDUAL, SQUARE, ROOTS, SCALE, TURN, PARTS = (
    (2, 3, 4), 5, (5, 7, 9), (6, 8, 10), 11, (11, 14, 17), (12, 15, 18), (14, 17, 20))


def scale_y(dve, s, nm, t, k):
    dve.wait_ge(s.stored, 16 * (t + 1))
    scale_tile(dve, nm, t, s.y[:, k, :])


def steps_scalar(act, s, ps, nm, xn, g, f):
    t0, n = GROUPS[g]
    for k in range(n):
        if f == Y_SQUARE[k]:
            y_square_scalar(act, s, g, k, nm, in_banks(ps))
        if nm and f == SQUARE[k]:
            square_scalar(act, s, nm, g, k, t0 + n, in_banks(ps))
        if nm and f == PARTS[k]:
            high_tile(act, nm, ps, xn, t0 + k)


def steps_vector(dve, s, ps, nm, xn, g, f, D, factor):
    t0, n = GROUPS[g]
    if f == Y_ROOTS:
        y_roots(dve, s, t0, t0 + n, D, factor)
    if nm and f == ROOTS:
        norm_roots(dve, nm, t0, t0 + n, D)
    for k in range(n):
        if f == RESIDUAL[k]:
            residual_vector(dve, s, g, k)
        if nm and f == PARTS[k]:
            low_tile(dve, nm, ps, xn, t0 + k)
        if nm and f == SCALE[k]:
            scale_y(dve, s, nm, t0 + k, k)


def steps_tensor(pe, s, ps, nm, ident, g, f):
    for k in range(GROUPS[g][1]):
        if nm and f == TURN[k]:
            turn_tile(pe, nm, ps, ident, GROUPS[g][0] + k, s.y.shape[2] // P)



def tail_scalar(act, s, ps, nm, xn):
    g = len(GROUPS) - 1
    t0, n = GROUPS[g]
    junk = s.draw[0][:, :]
    act.wait_ge(s.d_low, len(GROUPS) * s.h.shape[1])
    y_free(act, s, nm, g)
    for k in range(n):
        if k == n - 1:
            square_scalar(act, s, nm, g, 0, t0 + k, junk)
        wait_tile(act, s, g, k)
        for half, left in enumerate((s.y_even, s.y_odd)):
            act.activation(s.y[:, k, half * BANK:(half + 1) * BANK], ps[:, 2 * k + half, :], ACT.Copy)\
               .then_inc(left, 1)
        if k == n - 1:
            act.wait_ge(nm.summed, t0 + 1)
        y_square_scalar(act, s, g, k, nm, junk)
    for k in range(1, n):
        square_scalar(act, s, nm, g, k, t0 + n, junk)
    for k in range(n):
        high_tile(act, nm, ps, xn, t0 + k)


def tail_vector(dve, s, ps, nm, xn, D, factor):
    g = len(GROUPS) - 1
    t0, n = GROUPS[g]

    for k in range(n - 1):
        y_roots(dve, s, t0 + k, t0 + k + 1, D, factor)
        residual_vector(dve, s, g, k)
    inverse_roots(dve, s.chain, norm_root(dve, nm, t0, t0 + 1, D), y_root(dve, s, t0 + n - 1, t0 + n, D, factor))
    residual_vector(dve, s, g, n - 1)
    scale_tile(dve, nm, t0, s.y[:, 0, :])
    norm_roots(dve, nm, t0 + 1, t0 + n, D)
    for k in range(1, n):
        scale_tile(dve, nm, t0 + k, s.y[:, k, :])
    for k in range(n):
        low_tile(dve, nm, ps, xn, t0 + k)


def tail_tensor(pe, s, ps, nm, ident, u):
    for k, after in enumerate((5, 6, 6)):
        if u == after:
            turn_tile(pe, nm, ps, ident, GROUPS[-1][0] + k, s.y.shape[2] // P)



EARLY_UNITS = {19: (0, 1), 20: (2, 3, 4), 21: (5, 6, 7)}


def down_scalar(act, s, ps, nm, xn, early=None):
    FT = s.h.shape[1]
    act.wait_ge(s.w_low, 2 * FT)
    act.wait_ge(s.up_done, FT - 1)
    down_high(act, s, 0, 0, 0)
    act.wait_ge(s.up_done, FT)
    down_high(act, s, 0, 0, 1)
    gate_up_silu(act, s, ps, FT - 1, 1)
    for c in range(2, 4):
        down_high(act, s, 0, 0, c)
    with act.Fori(1, FT // 3) as i:
        for c in range(1, 4):
            down_high(act, s, 0, i, c)
    for g in range(1, len(GROUPS)):
        for f in range(2):
            down_high(act, s, g, 0, f)
        y_free(act, s, nm, g - 1)
        for k in range(GROUPS[g - 1][1]):
            leave_scalar(act, s, ps, g - 1, k)
        for f in range(2, FT):
            down_high(act, s, g, 0, f)
            steps_scalar(act, s, ps, nm, xn, g - 1, f)
            if early and g == len(GROUPS) - 1:
                for u in EARLY_UNITS.get(f, ()):
                    early(u)
    if nm is None:
        last_scalar(act, s, ps)


def down_vector(dve, s, ps, nm, xn, D, factor, early=None):
    FT = s.h.shape[1]
    for c in range(4):
        down_low(dve, s, 0, 0, c)
        if c == 1:
            gate_up_product(dve, s, ps, FT - 1, 1)
    with dve.Fori(1, FT // 3) as i:
        for c in range(1, 4):
            down_low(dve, s, 0, i, c)
    for g in range(1, len(GROUPS)):
        for f in range(2):
            down_low(dve, s, g, 0, f)
        y_free(dve, s, nm, g - 1)
        for k in range(GROUPS[g - 1][1]):
            leave_vector(dve, s, ps, g - 1, k)
        for f in range(2, FT):
            down_low(dve, s, g, 0, f)
            steps_vector(dve, s, ps, nm, xn, g - 1, f, D, factor)
            if early and g == len(GROUPS) - 1:
                for u in EARLY_UNITS.get(f, ()):
                    early(u)
    if nm is None:
        last_vector(dve, s, ps, D, factor)


def down_tensor(pe, s, ps, nm, ident):
    FT = s.h.shape[1]
    pe.wait_ge(s.h_done, FT - 1)
    for c in range(4):
        down_products(pe, s, ps, 0, 0, c)
    with pe.Fori(1, FT // 3 - 1) as i:
        for c in range(1, 4):
            down_products(pe, s, ps, 0, i, c)
    for c in range(1, 4):
        down_products(pe, s, ps, 0, FT // 3 - 1, c)
    for g in range(1, len(GROUPS)):
        for c in range(4):
            down_products(pe, s, ps, g, 0, c)
        first = (TURN[0] - 1) // 3 if nm else FT // 3 - 1
        with pe.Fori(1, first) as i:
            for c in range(1, 4):
                down_products(pe, s, ps, g, i, c)
        last = g == len(GROUPS) - 1
        for f in range(3 * first + 1, FT - RING if last else FT):
            down_products(pe, s, ps, g, 0, f)
            steps_tensor(pe, s, ps, nm, ident, g - 1, f)
        if last:
            down_last_units(pe, s, ps)


def last_scalar(act, s, ps):
    g = len(GROUPS) - 1
    t0, n = GROUPS[g]
    for k in range(n):
        wait_tile(act, s, g, k)
        act.wait_ge(s.y_summed, t0 + k)
        act.activation(ps[:, 6:8, :], ps[:, 2 * k:2 * k + 2, :], ACT.Square,
                       accum_out=s.ssq[:, t0 + k:t0 + k + 1]).then_inc(s.y_summed, 1)


def last_vector(dve, s, ps, D, factor):
    g = len(GROUPS) - 1
    t0, n = GROUPS[g]
    dve.wait_ge(s.stored, 16 * t0)
    for k in range(n):
        t = t0 + k
        wait_tile(dve, s, g, k)
        dve.wait_ge(s.y_summed, t + 1)
        s.chain.then(dve, dve.tensor_tensor(s.y[:, k, :], ps[:, 2 * k:2 * k + 2, :].rearrange("p b c -> p (b c)"),
                                            s.gain_post[:, :], ALU.mult))
        y_roots(dve, s, t, t + 1, D, factor)
        dve.wait_ge(s.res_loaded[s.place[t]], 16 * (s.place[:t].count(s.place[t]) + 1))
        for half in range(2):
            at = slice(half * BANK, (half + 1) * BANK)
            dve.scalar_tensor_tensor(s.y[:, k, at], s.y[:, k, at], s.rstd[:, t:t + 1], s.res[s.place[t]][:, at],
                                     ALU.mult, ALU.add).then_inc(s.y_final, 1)


def last_stores(act, s, out):
    t0, n = GROUPS[-1]
    for k in range(n):
        for half in range(2):
            act.wait_ge(s.y_final, t0 + 2 * k + half + 1)
            at = slice(half * BANK, (half + 1) * BANK)
            act.dma_start(out[(t0 + k) * P:(t0 + k + 1) * P, at], s.y[:, k, at]).then_inc(s.last_stored, 16)


def down_pool(pool, s, res, out):
    tiles = out.shape[0] // P
    t0 = GROUPS[-1][0]
    finals = lambda t: 2 * t - t0 if s.last_stored and t > t0 else t
    loaded = 0
    for t in range(tiles):
        while loaded < tiles and all(j < t for j in range(loaded) if s.place[j] == s.place[loaded]):
            place = s.place[loaded]
            if t > 0 and place in s.place[:loaded]:
                pool.wait_ge(s.y_final, finals(t))
            if not s.last_stored and place > 0:
                if t < t0:
                    break
                pool.wait_ge(s.d_low, len(GROUPS) * s.h.shape[1])
            pool.dma_start(s.res[place][:, :], res[loaded * P:(loaded + 1) * P, :])\
                .then_inc(s.res_loaded[place], 16)
            loaded += 1
        if not s.last_stored or t < t0:
            pool.wait_ge(s.y_final, t + 1)
            k = t - max(g[0] for g in GROUPS if g[0] <= t)
            pool.dma_start(out[t * P:(t + 1) * P, :], s.y[:, k, :]).then_inc(s.stored, 16)



HEADS_M, HEADS_A, HEADS_KV, DH_A = 4, 8, 2, 64
CONV = 4
ROPE_HALF = 8
THETA = 500000.0
NV, NO, NQ = 129, 512, 512
TOK = HEADS_M * NV + NO + NQ
OG, AQ = HEADS_M * NV, HEADS_M * NV + NO
BIG = 3.0e38
QK_SCALE = 0.25 * P ** -0.5


class Mixer:

    def __init__(self, mem, S, D):
        at = lambda n, shape, dt, kb: mem.at(f"mix_{n}", shape, dt, int(kb * KB))
        s = lambda n: mem.sem(f"mix_{n}")
        T, K = S // P, D // P
        self.T, self.K = T, K
        self.tok = at("tok", [P, T, TOK], F32, 64)
        self.ak = at("ak", [P, T, 4, DH_A], F32, 132.25)
        self.av = at("av", [P, T, 4, DH_A], F32, 140.25)
        self.qk = at("qk", [P, 2 * HEADS_M, S], F32, 173)
        self.traw = [at(f"token_raw{b}", [P, BANK], F32, 112.25 + 2 * b) for b in range(3)]
        self.tpart = [at(f"token_part{b}", [P, 2, BANK], FR, 118.25 + 4 * b) for b in range(3)]
        self.tfirst = [at(f"token_first{k}", [P, 2, WIDTH[0]], FR, 64 + -(-4 * (TOK * k + OG) // 32) / 32)
                       for k in range(K)]
        self.traw_loaded = [s(f"token_loaded{b}") for b in range(3)]
        self.t_high, self.t_low, self.t_unit = s("token_high"), s("token_low"), s("token_unit_done")
        self.t_tile = s("token_tile_done")
        self.left = [s("bank_left_by_act"), s("bank_left_by_dve")]
        self.tanh_o, self.og_done = s("tanh_o"), s("og_done")
        self.gain_norm = at("gain_norm", [P, HEADS_M * P], F32, 130.25)
        self.pos_i = at("pos_i", [P, T], I32, 164.25)
        self.pos = at("pos", [P, T], F32, 164.375)
        self.freq = at("freq", [P, ROPE_HALF], F32, 164.5)
        self.ang = at("ang", [P, T, ROPE_HALF], F32, 164.75)
        self.turns = at("turns", [P, T, ROPE_HALF], F32, 165)
        self.cos = at("cos", [P, T, ROPE_HALF], F32, 165.25)
        self.sin = at("sin", [P, T, ROPE_HALF], F32, 165.5)
        self.rt = [at(f"rope{i}", [P, T, 8, ROPE_HALF], F32, 156.25 + 2 * i) for i in range(4)]
        self.pos_loaded, self.angles, self.sines = s("pos_loaded"), s("angles"), s("sines")
        self.roped = s("roped")
        self.qbd = at("q_blocks", [P, 4, 2, P], F32, 148.25)
        self.kt = [at(f"kt{b}", [P, 2, 3, DH_A], F32, 152.25 + 1.5 * b) for b in range(2)]
        self.vsh = at("v_shifted", [P, 4, DH_A], F32, 155.25)
        self.pr = [at(f"probs{e}", [P, 4, P], F32, 156.25 + 2 * e) for e in range(2)]
        self.pt = [at(f"probs_turned{e}", [P, 4, P], F32, 160.25 + 2 * e) for e in range(2)]
        small = 207.25
        names = ("mx", "neg", "es", "rs", "rinv", "sd")
        stats = at("softmax_stats", [P, 12, 4], F32, small)
        self.st = [{n: stats[:, 6 * e + i, :] for i, n in enumerate(names)} for e in range(2)]
        self.sink = at("sink", [P, 4], F32, small + .1875)
        self.conv_w = at("conv_w", [P, CONV, 8], F32, small + .375)
        self.conv_b = at("conv_b", [P, 8], F32, small + .34375)
        self.consts_loaded = s("constants_loaded")
        self.zeroed = s("zeroed")
        self.q_turned, self.k_turned = s("q_turned"), s("k_turned")
        self.qbd_ready, self.kt_ready = s("q_blocks_ready"), s("kt_ready")
        self.logits, self.stats, self.exps = s("logits"), s("softmax_shift"), s("exps")
        self.probs, self.pt_turned, self.pt_ready = s("probs"), s("probs_turned"), s("probs_turned_ready")
        self.vsh_ready, self.pv, self.ha_done = s("v_shifted_ready"), s("pv"), s("attention_out")
        self.qraw = [at(f"qk_raw{b}", [P, K, P], F32, kb) for b, kb in enumerate((201, 112.25))]
        self.qpart = [at(f"qk_part{b}", [P, 2, K, P], FR, kb) for b, kb in enumerate((193, 124.25, 116.25))]
        self.xp = at("conv_in", [P, 3 + S], F32, 164.25)
        self.tanh_half = at("tanh_half", [P, BANK], F32, 168.875)
        self.q_loaded = [s(f"qk_loaded{b}") for b in range(2)]
        self.q_high, self.q_low = s("qk_high"), s("qk_low")
        self.q_half, self.xp_ready = s("qk_half_done"), s("conv_in_ready")
        self.conv_done, self.tanh_qk, self.qk_done = s("conv_done"), s("tanh_qk"), s("qk_done")
        R = HEADS_M * T
        self.R = R
        self.gt = at("gates_token_major", [P, 2, HEADS_M, T], F32, 168.5)
        self.gbias = at("gate_bias", [P, 2, HEADS_M], F32, 168.75)
        g = [at(n, [R, P], F32, 168.8125 + .5 * i) for i, n in
             enumerate(("g_li", "g_f", "g_lf", "g_cum", "g_b", "g_cmax"))]
        self.g_li, self.g_f, self.g_lf, self.g_cum, self.g_b, self.g_cmax = g
        self.gout = at("g_out", [R, 2, P], F32, 171.8125)
        self.gsmall = at("g_small", [R, 8], F32, 172.875)
        self.gate_in, self.g_pe, self.g_sb, self.g_act = s("gate_in"), s("gate_pe"), s("gate_dve"), s("gate_act")
        self.g_stored = s("gate_rows_stored")
        self.col = at("gate_columns", [P, 3, R], F32, 206)
        self.dec = at("decay", [P, R], F32, 206.375)
        self.wo = [at(f"out_{n}", [P, K, D], FR, 32 * i) for i, n in enumerate(("high", "low"))]
        self.wraw = at("out_raw", [P, K, D], F32, 32)
        self.bc = [at(f"gate_rows{b}", [P, 2, HEADS_M, P], F32, 116.25 - 4 * b) for b in range(2)]
        self.dm = at("decay_matrix", [P, HEADS_M, P], F32, 120.25)
        self.sc = at("scores", [P, HEADS_M, P], F32, 122.25)
        self.kw = at("k_weighted", [P, HEADS_M, P], F32, 124.25)
        self.qw = at("q_weighted", [P, HEADS_M, P], F32, 126.25)
        self.hm = at("hm", [P, HEADS_M, P], F32, 128.25)
        self.junk = at("junk", [P, D], BF, 166.5)
        self.late_junk = at("late_junk", [P, D], BF, 128.25)
        self.C = [at(f"state{b}", [P, HEADS_M, NV], F32, 130.25 + 2.125 * b) for b in range(2)]
        self.hs = [at(f"out_in{b}", [P, 2, K, P], FR, 134.5 + 8 * b) for b in range(2)]
        self.res = at("residual", [P, D], F32, 168.75)
        self.last_res = at("last_residual", [P, D], F32, 116.25)
        self.gain_post, self.gain_next = (self.tok[:, t:t + 2, AQ:AQ + NQ] for t in (0, 2))
        names = ("ad", "r", "rs", "vr", "half", "value")
        stats = at("norm_stats", [P, 7, 5], F32, small)
        self.sm = {n: stats[:, i, :] for i, n in enumerate(names)}
        self.sm["guess"] = stats[:, 6, :].bitcast(I32)
        self.bn = at("bn", [P, 4, 6], F32, small + .15625)
        self.mv = at("mean_var", [P, 4, 2], F32, small + .25)
        self.w_loaded = [s(f"out_loaded{b}") for b in range(4)]
        self.w_high, self.w_low = s("out_high"), s("out_low")
        self.bc_loaded = [s(f"gate_rows_loaded{b}") for b in range(2)]
        self.s_done, self.k_done = s("scores_done"), s("k_turned_m")
        self.dm_shift, self.dm_done, self.wg_done = s("decay_shift"), s("decay_done"), s("wg_done")
        self.sc_done, self.kw_done, self.qw_done = s("scores_weighted"), s("kw_done"), s("qw_done")
        self.n_done, self.c_done, self.state = s("num_done"), s("kv_done"), s("state_done")
        self.hm_norm, self.hm_done = s("hm_norm"), s("hm_done")
        self.hm_turned, self.hs_high, self.hs_low = s("hm_turned"), s("out_in_high"), s("out_in_low")
        self.att_high, self.att_low, self.att_used = s("att_in_high"), s("att_in_low"), s("att_in_used")
        self.y_part = [s("y_half_done"), s("y_done")]
        self.y_half, self.y_done = self.y_part
        self.y_left = [s(f"y_left{n}") for n in range(2)]
        self.y_summed, self.y_scaled = s("y_summed"), s("y_scaled")
        self.res_loaded = [s("residual_loaded"), s("last_residual_loaded")]
        self.h_done, self.stored = s("h_done"), s("stored")
        self.gains_loaded = s("gains_loaded")
        self.chain = mem.chain


M_W = HEADS_M * P
GATES, A_Q = 4 * M_W, 4 * M_W + 2 * HEADS_M
A_K = A_Q + HEADS_A * DH_A
CHUNKS = [
    [(0, GATES, 2 * HEADS_M), (2 * HEADS_M, A_K, 2 * HEADS_KV * DH_A)],
    [(0, A_Q, HEADS_A * DH_A)],
    [(0, 2 * M_W, M_W)],
    [(0, 3 * M_W, M_W)],
]
WIDTH = [sum(w for _, _, w in c) for c in CHUNKS]


EARLY = GROUPS[-1][0]


def token_unit(m, u):
    return u // m.K, u % m.K


def token_parts(m, u):
    chunk, k = token_unit(m, u)
    return m.tfirst[k] if chunk == 0 else m.tpart[u % RING][:, :, 0:WIDTH[chunk]]


def tokens_sync(sp, m, w_in):
    for u in range(m.K * len(CHUNKS)):
        chunk, k = token_unit(m, u)
        if u >= RING:
            sp.wait_ge(m.t_low, u - RING + 1)
        for a, c, w in CHUNKS[chunk]:
            sp.dma_start(m.traw[u % RING][:, a:a + w], w_in[k * P:(k + 1) * P, c:c + w])\
              .then_inc(m.traw_loaded[u % RING], 16)


def token_loads(m, u):
    return 16 * sum(len(CHUNKS[token_unit(m, v)[0]]) for v in range(u % RING, u + 1, RING))


def units_through(m, chunk):
    return m.K * (chunk + 2)


def token_high(act, m, u):
    act.wait_ge(m.traw_loaded[u % RING], token_loads(m, u))
    if u >= m.K + RING:
        act.wait_ge(m.t_unit, m.K + u - RING + 1)
    parts = token_parts(m, u)
    act.activation(parts[:, 0, :], m.traw[u % RING][:, 0:parts.shape[2]], ACT.Copy).then_inc(m.t_high, 1)


def token_low(dve, m, u):
    dve.wait_ge(m.t_high, u + 1)
    parts = token_parts(m, u)
    part_low(dve, parts[:, 1, :], m.traw[u % RING][:, 0:parts.shape[2]], parts[:, 0, :]).then_inc(m.t_low, 1)


def tokens_tensor(pe, m, ps, xn, ff, nm, ident):
    def unit(u, tiles, units):
        chunk, k = token_unit(m, u)
        pe.wait_ge(m.t_low, u + 1)
        parts = token_parts(m, u)
        if units % m.K == 0 and chunk == 0:
            pe.wait_ge(nm.low, 2 * tiles[-1] + 2)
        for t in tiles:
            if k == 0 and chunk > 0:
                pe.wait_ge(m.left[t % 2], m.T // 2 * (chunk - 1) + t // 2 + 1)
            elif k == 0 and t < 2 * GROUPS[-1][1]:
                pe.wait_ge((ff.y_even, ff.y_odd)[t % 2], EARLY + t // 2 + 1)
            mm = three_passes(pe, ps[:, t, 0:parts.shape[2]], [x[:, k, t * P:(t + 1) * P] for x in xn],
                              [parts[:, i, :] for i in range(2)], k == 0, k == m.K - 1)
            if k == m.K - 1 and t != tiles[-1]:
                mm.then_inc(m.t_tile, 1)
        mm.then_inc(m.t_unit, 1)

    for u in range(m.K):
        unit(u, range(EARLY), u)
        tail_tensor(pe, ff, ps, nm, ident, u)
    for u in range(m.K):
        unit(u, range(EARLY, m.T), m.K + u)
    for u in range(m.K, m.K * len(CHUNKS)):
        unit(u, range(m.T), m.K + u)


def wait_bank(eng, m, chunk, t):
    if chunk == 0:
        tiles, before = (range(EARLY), 0) if t < EARLY else (range(EARLY, m.T), EARLY - 1)
        units = m.K if t < EARLY else 2 * m.K
    else:
        tiles, before, units = range(m.T), m.T - 2 + (m.T - 1) * (chunk - 1), units_through(m, chunk)
    if t == tiles[-1]:
        eng.wait_ge(m.t_unit, units)
    else:
        eng.wait_ge(m.t_tile, before + tiles.index(t) + 1)


def tokens_leave(eng, copy, m, ps, chunk, which, tiles):
    for t in tiles[(which - tiles[0]) % 2::2]:
        wait_bank(eng, m, chunk, t)
        bank = ps[:, t, :]
        if chunk == 0:
            copy(m.gt[:, :, :, t], bank[:, 0:8].rearrange("p (g h) -> p g h", g=2))
            for j, to in enumerate((m.ak, m.av)):
                src = bank[:, 8 + P * j:8 + P * (j + 1)].rearrange("p (k f) -> p k f", k=2)
                for d in range(2):
                    ins = copy(to[:, t, d::2, :], src)
        elif chunk == 1:
            ins = copy(m.tok[:, t, AQ:AQ + NQ], bank)
        elif chunk == 2:
            ins = copy(m.tok[:, t, 0:HEADS_M * NV].rearrange("p (h e) -> p h e", e=NV)[:, :, 0:P],
                       bank.rearrange("p (h e) -> p h e", e=P))
        ins.then_inc(m.left[which], 1)


def tokens_scalar(act, m, ps, xn, ff, nm):
    copy = lambda out, in_: act.activation(out, in_, ACT.Copy)
    tail_scalar(act, ff, ps, nm, xn)
    for u in range(m.K, m.K * len(CHUNKS)):
        chunk, k = token_unit(m, u)
        if u == m.K:
            act.wait_ge(ff.unit_done, len(GROUPS) * ff.h.shape[1])
            tokens_leave(act, copy, m, ps, 0, 0, range(EARLY))
        token_high(act, m, u)
        if k == 1:
            tokens_leave(act, copy, m, ps, chunk - 1, 0, range(EARLY if chunk == 1 else 0, m.T))
        if chunk == 2 and k == 5:
            act.wait_ge(m.angles, 1)
            act.activation(m.sin[:, :, :], m.sin[:, :, :], ACT.Sin).then_inc(m.sines, 1)
            act.activation(m.cos[:, :, :], m.cos[:, :, :], ACT.Sin).then_inc(m.sines, 1)
    qk_high(act, m, 0)
    for t in range(m.T):
        wait_bank(act, m, len(CHUNKS) - 1, t)
        act.activation(m.tok[:, t, OG:OG + NO], ps[:, t, :], ACT.Tanh, scale=0.5).then_inc(m.tanh_o, 1)


def angles_vector(dve, m):
    then = m.chain.then
    for i in range(ROPE_HALF):
        dve.memset(m.freq[:, i:i + 1], float(np.float32(np.float32(THETA) ** np.float32(-i / ROPE_HALF))))\
           .then_inc(m.chain.sem, 1)
        m.chain.count += 1
    dve.wait_ge(m.chain.sem, m.chain.count)
    dve.wait_ge(m.pos_loaded, 16)
    then(dve, dve.tensor_copy(m.pos[:, :], m.pos_i[:, :]))
    wide = [P, m.T, ROPE_HALF]
    then(dve, dve.tensor_tensor(m.ang[:, :, :], m.pos[:, :].unsqueeze(2).to_broadcast(wide),
                                m.freq[:, :].unsqueeze(1).to_broadcast(wide), ALU.mult))
    ROUND = 1.5 * 2.0 ** 23
    turn = 2 * np.pi
    c1 = 6.28125
    c2 = float(np.float32(np.round((turn - c1) * 2 ** 21) / 2 ** 21))
    c3 = float(np.float32(turn - c1 - c2))
    for out, shift in ((m.sin, 0.0), (m.cos, 0.25)):
        n, o, a = m.turns[:, :, :], out[:, :, :], m.ang[:, :, :]
        then(dve, dve.tensor_scalar(n, a, 1 / turn, shift, ALU.mult, ALU.add))
        then(dve, dve.tensor_scalar(n, n, ROUND, ROUND, ALU.add, ALU.subtract))
        for i, c in enumerate((c1, c2, c3)):
            then(dve, dve.scalar_tensor_tensor(o, n, -c, a if i == 0 else o, ALU.mult, ALU.add))
        if shift:
            then(dve, dve.tensor_scalar(o, o, turn / 4, None, ALU.add))
        last = dve.tensor_scalar(o, o, 3.1415925, -3.1415925, ALU.min, ALU.max)
        if shift:
            last.then_inc(m.angles, 1)
        else:
            then(dve, last)


def rope_vector(dve, m):
    dve.wait_ge(m.sines, 2)
    then = m.chain.then
    q = m.tok[:, :, AQ:AQ + NQ].rearrange("p t (h f) -> p t h f", f=DH_A)
    for x, H in ((q, HEADS_A), (m.ak[:, :, :, :], 4)):
        wide = [P, m.T, H, ROPE_HALF]
        cos = m.cos[:, :, :].unsqueeze(2).to_broadcast(wide)
        sin = m.sin[:, :, :].unsqueeze(2).to_broadcast(wide)
        x1, x2 = x[:, :, :, 0:ROPE_HALF], x[:, :, :, ROPE_HALF:2 * ROPE_HALF]
        a, b, c, d = (r[:, :, 0:H, :] for r in m.rt)
        for o, u, v in ((a, x1, cos), (b, x2, sin), (c, x2, cos), (d, x1, sin)):
            then(dve, dve.tensor_tensor(o, u, v, ALU.mult))
        dve.tensor_tensor(x1, a, b, ALU.subtract).then_inc(m.roped, 1)
        dve.tensor_tensor(x2, c, d, ALU.add).then_inc(m.roped, 1)
        dve.wait_ge(m.roped, 2 if H == HEADS_A else 4)


def tokens_vector(dve, m, ps, xn, ff, nm, D):
    then = m.chain.then
    tail_vector(dve, ff, ps, nm, xn, D, 0.5)
    for u in range(m.K, m.K * len(CHUNKS)):
        chunk, k = token_unit(m, u)
        if u == m.K:
            tokens_leave(dve, dve.tensor_copy, m, ps, 0, 1, range(EARLY))
        token_low(dve, m, u)
        if k == 1:
            tokens_leave(dve, dve.tensor_copy, m, ps, chunk - 1, 1, range(EARLY if chunk == 1 else 0, m.T))
        if chunk == 1 and k == 4:
            angles_vector(dve, m)
        if chunk == 2 and k == 4:
            dve.wait_ge(m.left[0], m.T)
            rope_vector(dve, m)
        if chunk == 3 and k == 4:
            dve.wait_ge(m.consts_loaded, m.consts)
            then(dve, dve.tensor_scalar(m.gain_norm[:, :], m.gain_norm[:, :], 0.5, None, ALU.mult))
            dve.wait_ge(m.left[0], m.T // 2)
            dve.wait_ge(m.left[1], m.T // 2)
            dve.tensor_tensor(m.gt[:, :, :, :], m.gt[:, :, :, :],
                              m.gbias[:, :, :].unsqueeze(3).to_broadcast([P, 2, HEADS_M, m.T]),
                              ALU.add).then_inc(m.gate_in, 1)
    qk_low(dve, m, 0)
    for t in range(m.T):
        dve.wait_ge(m.tanh_o, t + 1)
        og = m.tok[:, t, OG:OG + NO]
        dve.scalar_tensor_tensor(og, og, 1.0, m.gain_norm[:, :], ALU.add, ALU.mult).then_inc(m.og_done, 1)



B_Q, B_K, B_L, B_P, B_V = 2, 3, (4, 5), 6, 7


def qk_raw(m, i):
    return m.qraw[min(i, 1)]


def qk_parts(m, i):
    return m.qpart[0 if i == 0 else 1 + (i - 1) % 2]


def qk_sync(sp, m, w_in):
    w = w_in[:, 0:2 * M_W].rearrange("(k p) f -> p k f", p=P)
    for i in range(2 * HEADS_M):
        if i == 1:
            sp.wait_ge(m.t_low, m.K * len(CHUNKS))
        elif i > 1:
            sp.wait_ge(m.q_low, i)
        sp.dma_start(qk_raw(m, i)[:, :, :], w[:, :, i * P:(i + 1) * P]).then_inc(m.q_loaded[min(i, 1)], 16)


def qk_high(act, m, i):
    act.wait_ge(m.q_loaded[min(i, 1)], 16 * max(i, 1))
    if i == 1:
        act.wait_ge(m.t_unit, units_through(m, len(CHUNKS) - 1))
        act.wait_ge(m.og_done, m.T)
    if i >= 3:
        act.wait_ge(m.q_half, 2 * (i - 1))
    act.activation(qk_parts(m, i)[:, 0, :, :], qk_raw(m, i)[:, :, :], ACT.Copy).then_inc(m.q_high, 1)


def qk_low(dve, m, i):
    dve.wait_ge(m.q_high, i + 1)
    p = qk_parts(m, i)
    part_low(dve, p[:, 1, :, :], qk_raw(m, i)[:, :, :], p[:, 0, :, :]).then_inc(m.q_low, 1)


def qk_half(pe, m, ps, xn, i, th):
    pe.wait_ge(m.q_low, i + 1)
    if i == 0:
        pe.wait_ge(m.tanh_o, th + 1)
    else:
        pe.wait_ge(m.xp_ready, 2 * (i - 1) + th + 1)
    w = qk_parts(m, i)
    for k in range(m.K):
        mm = three_passes(pe, ps[:, th, :], [w[:, a, k, :] for a in range(2)],
                          [x[:, k, th * BANK:(th + 1) * BANK] for x in xn], k == 0, k == m.K - 1)
    mm.then_inc(m.q_half, 1)


def conv_in_scalar(act, m, ps, i, th):
    act.wait_ge(m.q_half, 2 * i + th + 1)
    if i > 0:
        act.wait_ge(m.qk_done, i)
    else:
        act.wait_ge(m.roped, 4)
        act.wait_ge(m.sines, 2)
    act.activation(m.xp[:, 3 + th * BANK:3 + (th + 1) * BANK], ps[:, th, :], ACT.Copy)\
       .then_inc(m.xp_ready, 1)


def qk_columns(m, i, th):
    S = m.qk.shape[2]
    if i < 2 * HEADS_M - 1:
        return slice(0, S), i + 1
    return slice(th * BANK, (th + 1) * BANK), i + 1 + th


def conv_vector(dve, m, i, th=1):
    then = m.chain.then
    at, _ = qk_columns(m, i, th)
    dve.wait_ge(m.xp_ready, 2 * i + th + 1)
    out = m.qk[:, i, at]
    then(dve, dve.tensor_scalar(out, m.xp[:, 3 + at.start:3 + at.stop], m.conv_w[:, 3, i:i + 1],
                                m.conv_b[:, i:i + 1], ALU.mult, ALU.add))
    for j in (2, 1, 0):
        ins = dve.scalar_tensor_tensor(out, m.xp[:, j + at.start:j + at.stop], m.conv_w[:, j, i:i + 1], out,
                                       ALU.mult, ALU.add)
        if j:
            then(dve, ins)
    ins.then_inc(m.conv_done, 1)


def tanh_of(m, i, th):
    at, _ = qk_columns(m, i, th)
    return m.tanh_half[:, :] if at.stop == BANK else m.xp[:, 3 + at.start:3 + at.stop]


def tanh_scalar(act, m, i, th=1):
    at, count = qk_columns(m, i, th)
    act.wait_ge(m.conv_done, count)
    act.activation(tanh_of(m, i, th), m.qk[:, i, at], ACT.Tanh, scale=0.5).then_inc(m.tanh_qk, 1)


def silu_vector(dve, m, i, th=1):
    at, count = qk_columns(m, i, th)
    dve.wait_ge(m.tanh_qk, count)
    dve.scalar_tensor_tensor(m.qk[:, i, at], tanh_of(m, i, th), 1.0, m.qk[:, i, at], ALU.add, ALU.mult)\
       .then_inc(m.qk_done, 1)


def attend_turn_tensor(pe, m, ps, ident, i):
    if i == 0:
        pe.wait_ge(m.roped, 4)
        pe.wait_ge(m.tanh_o, m.T)
    else:
        pe.wait_ge(m.qbd_ready, 2 * i)
        pe.wait_ge(m.kt_ready, i)
        step = min(i, len(GATE_ACT)) - 1
        pe.wait_ge(m.g_act, GATE_ACT[step])
        pe.wait_ge(m.g_sb, GATE_READ[step])
    for j in range(4):
        mm = pe.transpose(ps[:, B_Q, j * P:(j + 1) * P], m.tok[:, i, AQ + j * P:AQ + (j + 1) * P], ident[:, :])
    mm.then_inc(m.q_turned, 1)
    for j in range(2):
        mm = pe.transpose(ps[:, B_K, j * P:(j + 1) * P],
                          m.ak[:, i, 2 * j:2 * j + 2, :].rearrange("p d f -> p (d f)"), ident[:, :])
    mm.then_inc(m.k_turned, 1)


def attend_q_scalar(act, m, ps, i):
    act.wait_ge(m.q_turned, i + 1)
    if i == 0:
        act.wait_ge(m.zeroed, m.zeros)
    else:
        act.wait_ge(m.logits, 2 * i)
    for e in range(2):
        h = slice(64 * e, 64 * e + 64)
        act.activation(m.qbd[h, :, :, h], ps[h, B_Q, :].rearrange("p (j c q) -> p j c q", j=4, c=2),
                       ACT.Copy).then_inc(m.qbd_ready, 1)


def attend_k_vector(dve, m, ps, i):
    dve.wait_ge(m.k_turned, i + 1)
    if i == 0:
        dve.wait_ge(m.zeroed, m.zeros)
    if i >= 1:
        dve.wait_ge(m.logits, 2 * i)
    src = ps[:, B_K, 0:2 * P].rearrange("p (k c s) -> p k c s", k=2, c=2)
    dve.tensor_copy(m.kt[i % 2][:, :, 0:2, :], src)
    dve.tensor_copy(m.kt[1 - i % 2][:, :, 2, :], src[:, :, 1, :]).then_inc(m.kt_ready, 1)


def attend_logits_tensor(pe, m, ps, i, e):
    if e == 0:
        pe.wait_ge(m.qbd_ready, 2 * i + 2)
        pe.wait_ge(m.kt_ready, i + 1)
    if i > 0:
        pe.wait_ge(m.exps, 2 * (i - 1) + e + 1)
    for j in range(4):
        kt = m.kt[i % 2][:, j // 2, :, :]
        keys = kt[:, 0:2, :] if e else (kt[:, 0::2, :] if i else kt[:, 0:1, :])
        n = keys.shape[1] * DH_A
        mm = pe.matmul(ps[:, B_L[e], j * P:j * P + n], m.qbd[:, j, e, :], keys, start=True, stop=True)
    mm.then_inc(m.logits, 1)


def keys_of(i, e):
    return P if i or e else DH_A


def attend_max_vector(dve, m, ps, i, e):
    then, st, n = m.chain.then, m.st[e], keys_of(i, e)
    dve.wait_ge(m.logits, 2 * i + e + 1)
    if i > 0:
        dve.wait_ge(m.exps, 2 * (i - 1) + e + 1)
    lg = ps[:, B_L[e], :].rearrange("p (j s) -> p j s", j=4)[:, :, 0:n]
    then(dve, dve.tensor_reduce(st["mx"][:, :], lg, AX, ALU.max))
    then(dve, dve.scalar_tensor_tensor(st["mx"][:, :], st["mx"][:, :], DH_A ** -0.5, m.sink[:, :],
                                       ALU.mult, ALU.max))
    dve.tensor_scalar(st["neg"][:, :], st["mx"][:, :], -1.0, None, ALU.mult)
    dve.tensor_tensor(st["sd"][:, :], m.sink[:, :], st["mx"][:, :], ALU.subtract).then_inc(m.stats, 1)


def attend_exp_scalar(act, m, ps, i, e):
    st, n = m.st[e], keys_of(i, e)
    act.wait_ge(m.stats, 2 * i + e + 1)
    if i > 0:
        act.wait_ge(m.pt_turned, 2 * (i - 1) + e + 1)
        act.wait_ge(m.probs, 2 * (i - 1) + e + 1)
    else:
        act.wait_ge(m.zeroed, m.zeros)
        act.wait_ge(m.roped, 4)
    for j in range(4):
        act.activation(m.pr[e][:, j, 0:n], ps[:, B_L[e], j * P:j * P + n], ACT.Exp,
                       bias=st["neg"][:, j:j + 1], scale=DH_A ** -0.5, accum_out=st["rs"][:, j:j + 1])
    act.activation(st["es"][:, :], st["sd"][:, :], ACT.Exp).then_inc(m.exps, 1)


def attend_divide_vector(dve, m, i, e):
    then, st, n = m.chain.then, m.st[e], keys_of(i, e)
    dve.wait_ge(m.exps, 2 * i + e + 1)
    then(dve, dve.tensor_tensor(st["rinv"][:, :], st["rs"][:, :], st["es"][:, :], ALU.add))
    then(dve, dve.reciprocal(st["rinv"][:, :], st["rinv"][:, :]))
    if n < P:
        dve.memset(m.pr[e][:, :, n:P], 0.0)
    pr = m.pr[e][:, :, 0:n]
    dve.tensor_tensor(pr, pr, st["rinv"][:, :].unsqueeze(2).to_broadcast([P, 4, n]), ALU.mult)\
       .then_inc(m.probs, 1)


def attend_probs_tensor(pe, m, ps, ident, i, e):
    pe.wait_ge(m.probs, 2 * i + e + 1)
    if i or e:
        pe.wait_ge(m.pt_ready, 2 * i + e)
    for j in range(4):
        mm = pe.transpose(ps[:, B_P, j * P:(j + 1) * P], m.pr[e][:, j, :], ident[:, :])
    mm.then_inc(m.pt_turned, 1)


def attend_probs_scalar(act, m, ps, i, e):
    act.wait_ge(m.pt_turned, 2 * i + e + 1)
    if i:
        act.wait_ge(m.pv, 2 * (i - 1) + e + 1)
    act.activation(m.pt[e][:, :, :], ps[:, B_P, :].rearrange("p (j q) -> p j q", j=4), ACT.Copy)\
       .then_inc(m.pt_ready, 1)


def attend_values_tensor(pe, m, ps, i, e):
    pe.wait_ge(m.pt_ready, 2 * i + e + 1)
    if not e:
        pe.wait_ge(m.vsh_ready, 2 * i + 2)
    if i or e:
        pe.wait_ge(m.ha_done, 2 * (2 * i + e))
    for kv in range(2):
        v = m.av[:, i, 2 * kv:2 * kv + 2, :] if e else m.vsh[:, 2 * kv:2 * kv + 2, :]
        mm = pe.matmul(ps[:, B_V, 2 * kv * P:2 * (kv + 1) * P], v.rearrange("p d f -> p (d f)"),
                       m.pt[e][:, 2 * kv:2 * kv + 2, :], start=True, stop=True)
    mm.then_inc(m.pv, 1)


def attend_out_scalar(act, m, ps, i, e):
    act.wait_ge(m.pv, 2 * i + e + 1)
    ha = m.tok[:, i, AQ:AQ + NQ].rearrange("p (j q) -> p j q", j=4)
    bank = ps[:, B_V, :].rearrange("p (j q) -> p j q", j=4)
    for d in range(2):
        h = slice(64 * d, 64 * d + 64)
        act.activation(ha[h, :, 64 * e:64 * e + 64], bank[h, :, h], ACT.Copy).then_inc(m.ha_done, 1)


def shifted_values_pool(pool, m, i):
    if i == 0:
        pool.wait_ge(m.left[0], m.T // 2)
        pool.wait_ge(m.left[1], m.T // 2)
        pool.wait_ge(m.zeroed, m.zeros)
    else:
        pool.wait_ge(m.pv, 2 * i - 1)
        pool.wait_ge(m.vsh_ready, 2 * i)
    pool.tensor_copy(m.vsh[0:64, :, :], m.av[0:64, i, :, :]).then_inc(m.vsh_ready, 1)
    pool.wait_ge(m.vsh_ready, 2 * i + 1)
    if i == 0:
        pool.memset(m.vsh[64:128, :, :], 0.0).then_inc(m.vsh_ready, 1)
    else:
        pool.tensor_copy(m.vsh[64:128, :, :], m.av[64:128, i - 1, :, :]).then_inc(m.vsh_ready, 1)



GATE_DVE = (4, 9, 13, 14)
GATE_ACT = (2, 2, 3, 4)
GATE_READ = (2, 5, 10, 10)


def gate_tensor(pe, m, ps, ident, ones, step):
    R = m.R
    bank = ps[:, B_K, :]
    pe.wait_ge(m.kt_ready, step + 1)
    if step == 0:
        pe.wait_ge(m.gate_in, 1)
        for g in range(2):
            mm = pe.transpose(bank[0:R, g * P:(g + 1) * P], m.gt[:, g, :, :].rearrange("p h t -> p (h t)"),
                              ident[:, :])
    elif step == 1:
        pe.wait_ge(m.g_sb, 4)
        for g in range(2):
            mm = pe.matmul(bank[0:1, g * R:(g + 1) * R], m.gsmall[:, g:g + 1], ident[0:R, 0:R],
                           start=True, stop=True)
    elif step == 2:
        pe.wait_ge(m.g_sb, 9)
        pe.matmul(bank[0:R, 0:1], m.g_lf[0:1, 64:96], ident[0:1, 0:1], start=True, stop=True)
        pe.matmul(bank[0:R, 1:2], m.g_lf[0:1, 96:128], ident[0:1, 0:1], start=True, stop=True)
        mm = pe.matmul(bank[:, 64:64 + R], ones[0:1, :], m.g_f[0:1, 0:R], start=True, stop=True)
    else:
        pe.wait_ge(m.g_sb, 13)
        for j, x in enumerate((m.g_b, m.g_li, m.g_f)):
            mm = pe.transpose(bank[:, j * R:(j + 1) * R], x[:, :], ident[0:R, 0:R])
    mm.then_inc(m.g_pe, 1)


def gate_vector(dve, m, ps, step):
    R, T, then = m.R, m.T, m.chain.then
    bank = ps[:, B_K, :]
    last = lambda ins: ins.then_inc(m.g_sb, 1)
    if step == 0:
        dve.wait_ge(m.g_pe, 1)
        last(dve.tensor_copy(m.g_li[:, :], bank[0:R, 0:P]))
        then(dve, dve.tensor_copy(m.g_f[:, :], bank[0:R, P:2 * P]))
        last(dve.scalar_tensor_tensor(m.g_lf[:, :], m.g_f[:, :], -1.0, m.g_f[:, :], ALU.mult, ALU.max))
        then(dve, dve.memset(m.gout[:, 0, :], 1.0))
        dve.wait_ge(m.g_act, 2)
        then(dve, dve.scalar_tensor_tensor(m.g_lf[:, :], m.g_f[:, :], 0.0, m.g_lf[:, :], ALU.min, ALU.subtract))
        then(dve, dve.tensor_tensor_scan(m.g_cum[:, :], m.gout[:, 0, :], m.g_lf[:, :], 0.0, ALU.mult, ALU.add))
        then(dve, dve.tensor_tensor(m.g_b[:, :], m.g_li[:, :], m.g_cum[:, :], ALU.subtract))
        then(dve, dve.tensor_tensor_scan(m.g_cmax[:, :], m.g_b[:, :], m.g_b[:, :], -BIG, ALU.max, ALU.max))
        last(dve.tensor_copy(m.gsmall[:, 0:1], m.g_cum[:, P - 1:P]))
        last(dve.tensor_tensor(m.gsmall[:, 1:2], m.g_cum[:, P - 1:P], m.g_cmax[:, P - 1:P], ALU.add))
    elif step == 1:
        dve.wait_ge(m.g_pe, 2)
        row = m.g_lf[0:1, :]
        then(dve, dve.tensor_copy(row[:, 0:2 * R], bank[0:1, 0:2 * R]))
        then(dve, dve.memset(row[:, 64:96], 0.0))
        for h in range(HEADS_M):
            a = slice(h * T, (h + 1) * T)
            last(dve.tensor_tensor_scan(row[:, 96 + h * T:96 + (h + 1) * T], row[:, h * T:(h + 1) * T],
                                        row[:, R + h * T:R + (h + 1) * T], 0.0, ALU.add, ALU.max))
        dve.wait_ge(m.g_sb, 8)
        rows = lambda a: row[:, a:a + R].rearrange("p (h t) -> p h t", h=HEADS_M)
        then(dve, dve.tensor_copy(rows(64)[:, :, 1:T], rows(96)[:, :, 0:T - 1]))
        then(dve, dve.tensor_tensor(m.g_f[0:1, 0:R], row[:, 0:R], row[:, 64:96], ALU.add))
        last(dve.tensor_tensor(m.g_f[0:1, 0:R], m.g_f[0:1, 0:R], row[:, 96:128], ALU.subtract))
    elif step == 2:
        dve.wait_ge(m.g_pe, 3)
        then(dve, dve.tensor_copy(m.gsmall[:, 2:4], bank[0:R, 0:2]))
        before, after = m.gsmall[:, 2:3], m.gsmall[:, 3:4]
        then(dve, dve.tensor_scalar(m.gout[:, 0, :], m.g_cmax[:, :], before, -1.0, ALU.max, ALU.mult))
        last(dve.tensor_scalar(m.gout[:, 1, :], m.gout[:, 0, :], before, None, ALU.add))
        last(dve.tensor_tensor(m.g_f[:, :], m.gout[:, 0, :], m.g_cum[:, :], ALU.subtract))
        then(dve, dve.tensor_tensor(m.gsmall[:, 4:5], m.gsmall[:, 0:1], after, ALU.subtract))
        last(dve.tensor_scalar(m.g_li[:, :], m.g_b[:, :], m.gsmall[:, 4:5], None, ALU.add))
        last(dve.memset(m.gsmall[:, 5:6], 0.0))
    else:
        dve.wait_ge(m.g_act, 4)
        last(dve.tensor_scalar(m.col[:, 1, :], m.col[:, 1, :], QK_SCALE, None, ALU.mult))


def gate_scalar(act, m, ps, step):
    R, bank = m.R, ps[:, B_K, :]
    if step == 0:
        act.wait_ge(m.g_sb, 2)
        act.activation(m.g_lf[:, :], m.g_lf[:, :], ACT.Exp, scale=-1.0).then_inc(m.g_act, 1)
        act.wait_ge(m.g_act, 1)
        act.activation(m.g_lf[:, :], m.g_lf[:, :], ACT.Ln, bias=1.0).then_inc(m.g_act, 1)
    elif step == 2:
        act.wait_ge(m.g_sb, GATE_READ[2])
        act.activation(m.dec[:, :], bank[:, 64:64 + R], ACT.Exp).then_inc(m.g_act, 1)
    elif step == 3:
        act.wait_ge(m.g_pe, 4)
        act.activation(m.col[:, 0, :], bank[:, 0:R], ACT.Copy)
        act.activation(m.col[:, 1:3, :], bank[:, R:3 * R].rearrange("p (a r) -> p a r", a=2), ACT.Exp)\
           .then_inc(m.g_act, 1)


def heads_tensor(pe, m, ps, xn, ident, ones):
    qk_half(pe, m, ps, xn, 0, 0)
    for i in range(m.T):
        attend_turn_tensor(pe, m, ps, ident, i)
        if i:
            attend_values_tensor(pe, m, ps, i - 1, 0)
            attend_probs_tensor(pe, m, ps, ident, i - 1, 1)
            qk_half(pe, m, ps, xn, i, 0)
        attend_logits_tensor(pe, m, ps, i, 0)
        attend_logits_tensor(pe, m, ps, i, 1)
        if i < 4:
            gate_tensor(pe, m, ps, ident, ones, i)
        if i:
            attend_values_tensor(pe, m, ps, i - 1, 1)
        qk_half(pe, m, ps, xn, i, 1)
        if i == m.T - 1:
            chunk_scores_tensor(pe, m, ps, ident, 0)
        attend_probs_tensor(pe, m, ps, ident, i, 0)
    chunk_products_tensor(pe, m, ps, 0)
    attend_values_tensor(pe, m, ps, m.T - 1, 0)
    attend_probs_tensor(pe, m, ps, ident, m.T - 1, 1)
    attend_values_tensor(pe, m, ps, m.T - 1, 1)


def heads_scalar(act, m, ps):
    T = m.T
    for i in range(T):
        if i:
            conv_in_scalar(act, m, ps, i - 1, 1)
            attend_probs_scalar(act, m, ps, i - 1, 0)
        attend_q_scalar(act, m, ps, i)
        if i:
            attend_out_scalar(act, m, ps, i - 1, 0)
            attend_probs_scalar(act, m, ps, i - 1, 1)
        if i + 1 < T:
            qk_high(act, m, i + 1)
        if i:
            tanh_scalar(act, m, i - 1)
        conv_in_scalar(act, m, ps, i, 0)
        attend_exp_scalar(act, m, ps, i, 0)
        if i < 4:
            gate_scalar(act, m, ps, i)
        attend_exp_scalar(act, m, ps, i, 1)
        if i:
            attend_out_scalar(act, m, ps, i - 1, 1)
    tanh_scalar(act, m, T - 1, 0)
    att_high_scalar(act, m, 0)
    conv_in_scalar(act, m, ps, T - 1, 1)
    chunk_exps_scalar(act, m, ps, 0)
    attend_probs_scalar(act, m, ps, T - 1, 0)
    chunk_keys_scalar(act, m, ps, 0)
    out_weights_scalar(act, m, 0)
    attend_out_scalar(act, m, ps, T - 1, 0)
    attend_probs_scalar(act, m, ps, T - 1, 1)
    attend_out_scalar(act, m, ps, T - 1, 1)


def heads_vector(dve, m, ps, causal):
    T = m.T
    for i in range(T):
        attend_k_vector(dve, m, ps, i)
        if i:
            conv_vector(dve, m, i - 1)
        if i + 1 < T:
            qk_low(dve, m, i + 1)
        if i:
            silu_vector(dve, m, i - 1)
        attend_max_vector(dve, m, ps, i, 0)
        attend_max_vector(dve, m, ps, i, 1)
        if i < 4:
            gate_vector(dve, m, ps, i)
        if i == T - 1:
            conv_vector(dve, m, i, 0)
        attend_divide_vector(dve, m, i, 0)
        attend_divide_vector(dve, m, i, 1)
    silu_vector(dve, m, T - 1, 0)
    chunk_decay_vector(dve, m, causal, 0)
    chunk_weight_vector(dve, m, ps, 0)
    att_low_vector(dve, m, 0)



B_S, B_T, B_N, B_C, B_Y = 0, 1, 2, 4, 6


def head_banks(ps, first):
    return ps[:, first:first + 2, 0:2 * NV].rearrange("p b (h e) -> p b h e", e=NV)


QUARTERS = (0, 2, 1, 3)


def out_quarter(q):
    j, n = 1 - q % 2, q // 2
    return slice(None), slice(4 * j, 4 * j + 4), slice(n * BANK, (n + 1) * BANK)


def out_weights_sync(sp, m, w_out, gate_rows):
    def rows(c):
        if c == 0:
            sp.wait_ge(m.g_stored, 16)
            sp.wait_ge(m.q_half, 2 * m.T - 2)
        if c == 1:
            sp.wait_ge(m.q_low, m.T)
        if c >= 2:
            sp.wait_ge(m.qw_done, c - 1)
            sp.wait_ge(m.dm_done, c - 1)
            sp.wait_ge(m.dm_shift, c - 1)
        src = gate_rows.rearrange("(h c) a l -> c a h l", h=HEADS_M)[c]
        for a in range(2):
            sp.dma_start(m.bc[c % 2][:, a, :, :], src[a].unsqueeze(0).to_broadcast([P, HEADS_M, P]))\
              .then_inc(m.bc_loaded[c % 2], 16)

    rows(0)
    rows(1)
    w = w_out.rearrange("(k p) f -> p k f", p=P)
    for q in QUARTERS:
        sp.wait_ge(m.q_half, 2 * m.T - 1 + q // 2)
        at = out_quarter(q)
        sp.dma_start(m.wraw[at], w[at]).then_inc(m.w_loaded[q], 16)
    for c in range(2, m.T):
        rows(c)


def out_weights_scalar(act, m, turn):
    q = QUARTERS[turn]
    at = out_quarter(q)
    act.wait_ge(m.w_loaded[q], 16)
    act.activation(m.wo[0][at], m.wraw[at], ACT.Copy).then_inc(m.w_high, 1)


def out_weights_pool(pool, m, turn):
    at = out_quarter(QUARTERS[turn])
    pool.wait_ge(m.w_high, turn + 1)
    if turn:
        pool.wait_ge(m.w_low, turn)
    else:
        pool.wait_ge(m.vsh_ready, 2 * m.T)
    part_low(pool, m.wo[1][at], m.wraw[at], m.wo[0][at]).then_inc(m.w_low, 1)


def tile(m, h, c):
    return m.qk[:, h, c * P:(c + 1) * P]


def chunk_scores_tensor(pe, m, ps, ident, c):
    if c == 0:
        pe.wait_ge(m.qk_done, 2 * HEADS_M)
        pe.wait_ge(m.xp_ready, 2 * m.T)
    else:
        pe.wait_ge(m.kw_done, c)
        if c >= m.T // 2:
            pe.wait_ge(m.qk_done, 2 * HEADS_M + 1)
    for h in range(HEADS_M):
        mm = pe.transpose(ps[:, B_T, h * P:(h + 1) * P], tile(m, HEADS_M + h, c), ident[:, :])
    mm.then_inc(m.k_done, 1)
    if c > 0:
        pe.wait_ge(m.sc_done, c)
    for h in range(HEADS_M):
        mm = pe.matmul(ps[:, B_S, h * P:(h + 1) * P], tile(m, HEADS_M + h, c), tile(m, h, c),
                       start=True, stop=True)
    mm.then_inc(m.s_done, 1)


def chunk_decay_vector(dve, m, causal, c):
    dve.wait_ge(m.bc_loaded[c % 2], 32 * (c // 2 + 1))
    if c == 0:
        dve.wait_ge(m.g_act, 4)
    else:
        dve.wait_ge(m.sc_done, c)
    for h in range(HEADS_M):
        r = h * m.T + c
        ins = dve.scalar_tensor_tensor(m.dm[:, h, :], m.bc[c % 2][:, 0, h, :], m.col[:, 0, r:r + 1],
                                       causal[:, :], ALU.add, ALU.min)
    ins.then_inc(m.dm_shift, 1)


def chunk_exps_scalar(act, m, ps, c):
    act.wait_ge(m.bc_loaded[c % 2], 32 * (c // 2 + 1))
    act.activation(m.bc[c % 2][:, 1, :, :], m.bc[c % 2][:, 1, :, :], ACT.Exp).then_inc(m.wg_done, 1)
    act.wait_ge(m.dm_shift, c + 1)
    act.activation(m.dm[:, :, :], m.dm[:, :, :], ACT.Exp).then_inc(m.dm_done, 1)


def chunk_keys_scalar(act, m, ps, c):
    act.wait_ge(m.k_done, c + 1)
    if c == 0:
        act.wait_ge(m.g_sb, 14)
    else:
        act.wait_ge(m.c_done, c)
    for h in range(HEADS_M):
        r = h * m.T + c
        ins = act.activation(m.kw[:, h, :], ps[:, B_T, h * P:(h + 1) * P], ACT.Copy, scale=m.col[:, 1, r:r + 1])
    ins.then_inc(m.kw_done, 1)


def chunk_weight_vector(dve, m, ps, c):
    dve.wait_ge(m.s_done, c + 1)
    dve.wait_ge(m.dm_done, c + 1)
    if c > 0:
        dve.wait_ge(m.n_done, c)
    dve.scalar_tensor_tensor(m.sc[:, :, :], ps[:, B_S, :].rearrange("p (h l) -> p h l", h=HEADS_M), QK_SCALE,
                             m.dm[:, :, :], ALU.mult, ALU.mult).then_inc(m.sc_done, 1)
    dve.wait_ge(m.wg_done, c + 1)
    dve.tensor_tensor(m.qw[:, :, :], m.qk[:, 0:HEADS_M, c * P:(c + 1) * P], m.bc[c % 2][:, 1, :, :], ALU.mult)\
       .then_inc(m.qw_done, 1)


def chunk_products_tensor(pe, m, ps, c):
    v = lambda h: m.tok[:, c, h * NV:(h + 1) * NV]
    pe.wait_ge(m.sc_done, c + 1)
    pe.wait_ge(m.qw_done, c + 1)
    if c == 0:
        pe.wait_ge(m.left[0], 3 * m.T // 2)
        pe.wait_ge(m.left[1], 3 * m.T // 2)
        pe.wait_ge(m.zeroed, m.zeros)
        pe.wait_ge(m.exps, 2 * m.T)
    else:
        pe.wait_ge(m.state, c)
        pe.wait_ge(m.hm_norm, c)
    N, C = head_banks(ps, B_N), head_banks(ps, B_C)
    for h in range(HEADS_M):
        out = N[:, h // 2, h % 2, :]
        mm = pe.matmul(out, m.sc[:, h, :], v(h), start=True, stop=(c == 0))
        if c > 0:
            mm = pe.matmul(out, m.qw[:, h, :], m.C[(c - 1) % 2][:, h, :], start=False, stop=True)
    mm.then_inc(m.n_done, 1)
    if c == m.T - 1:
        return
    pe.wait_ge(m.kw_done, c + 1)
    if c > 0:
        pe.wait_ge(m.hs_low, c)
    for h in range(HEADS_M):
        mm = pe.matmul(C[:, h // 2, h % 2, :], m.kw[:, h, :], v(h), start=True, stop=True)
    mm.then_inc(m.c_done, 1)


def chunk_state_vector(dve, m, ps, c):
    dve.wait_ge(m.c_done, c + 1)
    C = head_banks(ps, B_C)
    if c == 0:
        dve.wait_ge(m.g_act, 3)
        ins = dve.tensor_copy(m.C[0][:, :, :].rearrange("p (b h) e -> p b h e", b=2), C)
    else:
        for h in range(HEADS_M):
            r = h * m.T + c
            ins = dve.scalar_tensor_tensor(m.C[c % 2][:, h, :], m.C[(c - 1) % 2][:, h, :], m.dec[:, r:r + 1],
                                           C[:, h // 2, h % 2, :], ALU.mult, ALU.add)
    ins.then_inc(m.state, 1)


def chunk_root(m, a, b):
    return (m.sm["rs"][:, a:b], m.sm["vr"][:, a:b], 1.0, EPS,
            [m.sm[x][:, a:b] for x in ("guess", "half", "value")])


def chunk_stats_vector(dve, m, ps, c, others):
    then = m.chain.then
    N = head_banks(ps, B_N)
    dve.wait_ge(m.n_done, c + 1)
    sm = {n: x[:, 0:HEADS_M] for n, x in m.sm.items()}
    pair = lambda x: x.rearrange("p (b h) -> p b h", b=2)
    if c > 0:
        dve.wait_ge(m.hm_norm, c)
    for h in range(HEADS_M):
        dve.bn_stats(m.bn[:, h, :], N[:, h // 2, h % 2, 0:P])
    then(dve, dve.tensor_scalar(pair(sm["ad"]), N[:, :, :, P], -1.0, None, ALU.mult))
    for h in range(HEADS_M):
        dve.bn_aggr(m.mv[:, h, :], m.bn[:, h, :])
    then(dve, dve.tensor_tensor(pair(sm["ad"]), pair(sm["ad"]), N[:, :, :, P], ALU.max))
    emt = m.col[:, 2, :].rearrange("p (h t) -> p h t", h=HEADS_M)[:, :, c]
    then(dve, dve.tensor_tensor(sm["ad"][:, :], sm["ad"][:, :], emt, ALU.max))
    then(dve, dve.reciprocal(sm["r"][:, :], sm["ad"][:, :]))
    if c > 0:
        dve.wait_ge(m.hm_turned, c)
    for h in range(HEADS_M):
        at = OG + h * P
        ins = dve.scalar_tensor_tensor(m.hm[:, h, :], N[:, h // 2, h % 2, 0:P], m.mv[:, h, 0:1],
                                       m.tok[:, c, at:at + P], ALU.subtract, ALU.mult)
    ins.then_inc(m.hm_norm, 1)
    then(dve, dve.tensor_tensor(sm["vr"][:, :], m.mv[:, :, 1], sm["r"][:, :], ALU.mult))
    then(dve, dve.tensor_tensor(sm["vr"][:, :], sm["vr"][:, :], sm["r"][:, :], ALU.mult))
    n = HEADS_M + (c >= 2)
    if c >= 2:
        dve.wait_ge(m.y_summed, c - 1)
    inverse_roots(dve, m.chain, chunk_root(m, 0, n), *others)
    then(dve, dve.tensor_tensor(sm["rs"], sm["rs"], sm["r"], ALU.mult))
    dve.wait_ge(m.hm_norm, c + 1)
    dve.tensor_tensor(m.hm[:, :, :], m.hm[:, :, :], sm["rs"].unsqueeze(2).to_broadcast([P, HEADS_M, P]),
                      ALU.mult).then_inc(m.hm_done, 1)


def chunk_turn_tensor(pe, m, ps, ident, c):
    pe.wait_ge(m.hm_done, c + 1)
    pe.wait_ge(m.state, min(c + 1, m.T - 1))
    if c:
        pe.wait_ge(m.hs_low, c)
    for h in range(HEADS_M):
        mm = pe.transpose(ps[:, B_C, h * P:(h + 1) * P], m.hm[:, h, :], ident[:, :])
    mm.then_inc(m.hm_turned, 1)


def attention_in(m, c):
    return m.tok[:, c, AQ:AQ + NQ].rearrange("p (j q) -> p j q", j=4)


def mlstm_in(m, ps):
    return ps[:, B_C, :].rearrange("p (h l) -> p h l", h=HEADS_M)


def att_high_scalar(act, m, c):
    if c >= 2:
        act.wait_ge(m.att_used, c - 1)
    act.activation(m.hs[c % 2][:, 0, 4:8, :], attention_in(m, c), ACT.Copy).then_inc(m.att_high, 1)


def att_low_vector(dve, m, c):
    dve.wait_ge(m.att_high, c + 1)
    part_low(dve, m.hs[c % 2][:, 1, 4:8, :], attention_in(m, c), m.hs[c % 2][:, 0, 4:8, :])\
       .then_inc(m.att_low, 1)


def out_high_scalar(act, m, ps, c):
    if c >= 2:
        act.wait_ge(m.y_done, c - 1)
    act.wait_ge(m.hm_turned, c + 1)
    act.activation(m.hs[c % 2][:, 0, 0:4, :], mlstm_in(m, ps), ACT.Copy).then_inc(m.hs_high, 1)


def out_low_vector(dve, m, ps, c):
    dve.wait_ge(m.hs_high, c + 1)
    part_low(dve, m.hs[c % 2][:, 1, 0:4, :], mlstm_in(m, ps), m.hs[c % 2][:, 0, 0:4, :])\
       .then_inc(m.hs_low, 1)


def out_part(pe, m, ps, c, n, ks):
    hs = m.hs[c % 2]
    for k in ks:
        mm = three_passes(pe, ps[:, B_Y + n, :], [hs[:, a, k, :] for a in range(2)],
                          [w[:, k, n * BANK:(n + 1) * BANK] for w in m.wo], k == 4, k == 3)
    return mm


def out_attention_tensor(pe, m, ps, c, n):
    pe.wait_ge(m.att_low, c + 1)
    pe.wait_ge(m.w_low, n + 1)
    if c > 0:
        pe.wait_ge(m.y_left[n], c)
    else:
        pe.wait_ge(m.pt_ready, 2 * m.T)
        pe.wait_ge(m.ha_done, 4 * m.T)
    mm = out_part(pe, m, ps, c, n, range(4, 8))
    if n == 1:
        mm.then_inc(m.att_used, 1)


def out_mlstm_tensor(pe, m, ps, c, n):
    pe.wait_ge(m.hs_low, c + 1)
    pe.wait_ge(m.w_low, n + 3)
    out_part(pe, m, ps, c, n, range(4)).then_inc(m.y_part[n], 1)


def out_leave_scalar(act, m, ps, c, n):
    act.wait_ge(m.y_part[n], c + 1)
    act.wait_ge(m.hm_done, c + 1)
    act.activation(m.tok[:, c, n * BANK:(n + 1) * BANK], ps[:, B_Y + n, :], ACT.Copy).then_inc(m.y_left[n], 1)


def out_sum_scalar(act, m, c):
    D = m.wo[0].shape[2]
    for n in range(2):
        act.wait_ge(m.y_left[n], c + 1)
    if c > 0:
        act.wait_ge(m.y_summed, c)
    if 0 < c < m.T - 1:
        act.wait_ge(m.hm_done, c + 2)
    elif c:
        act.wait_ge(m.y_scaled, c)
    junk = m.late_junk if c == m.T - 1 else m.junk
    act.activation(junk[:, :], m.tok[:, c, 0:D], ACT.Square, scale=D ** -0.5,
                   accum_out=m.sm["vr"][:, 4:5]).then_inc(m.y_summed, 1)


def out_scale_vector(dve, m, c, *others):
    if c >= m.T - 2:
        dve.wait_ge(m.y_summed, c + 1)
        inverse_roots(dve, m.chain, chunk_root(m, 4, 5), *others)
    if c == 0:
        dve.wait_ge(m.gains_loaded, 16)
    y = m.tok[:, c, 0:m.wo[0].shape[2]].rearrange("p (b c) -> p b c", c=BANK)
    dve.scalar_tensor_tensor(y, y, m.sm["rs"][:, 4:5], m.gain_post, ALU.mult, ALU.mult)\
       .then_inc(m.y_scaled, 1)


def out_residual_pool(pool, m, c, res, out, D):
    to, loaded = m.res, m.res_loaded[0]
    if c == m.T - 1:
        to, loaded = m.last_res, m.res_loaded[1]
        pool.wait_ge(m.qw_done, c)
        pool.wait_ge(m.dm_shift, c)
    pool.dma_start(to[:, :], res[c * P:(c + 1) * P, :]).then_inc(loaded, 16)
    h = m.tok[:, c, 0:D]
    if c < m.T - 1:
        pool.wait_ge(m.y_scaled, c + 1)
        pool.wait_ge(loaded, 16 * (c + 1))
        if c == 0:
            pool.wait_ge(m.w_low, len(QUARTERS))
        pool.tensor_tensor(h, h, to[:, :], ALU.add).then_inc(m.h_done, 1)
    pool.wait_ge(m.h_done, c + 1)
    pool.dma_start(out[c * P:(c + 1) * P, :], h).then_inc(m.stored, 16)


def last_residual_vector(dve, m, D):
    dve.wait_ge(m.y_scaled, m.T)
    dve.wait_ge(m.res_loaded[1], 16)
    dve.wait_ge(m.h_done, m.T - 1)
    h = m.tok[:, m.T - 1, 0:D]
    dve.tensor_tensor(h, h, m.last_res[:, :], ALU.add).then_inc(m.h_done, 1)


def chunks_tensor(pe, m, ps, ident):
    for c in range(m.T):
        if c:
            chunk_products_tensor(pe, m, ps, c)
        if c + 1 < m.T:
            chunk_scores_tensor(pe, m, ps, ident, c + 1)
        if c:
            out_mlstm_tensor(pe, m, ps, c - 1, 0)
            out_mlstm_tensor(pe, m, ps, c - 1, 1)
        out_attention_tensor(pe, m, ps, c, 0)
        if c:
            chunk_turn_tensor(pe, m, ps, ident, c)
        out_attention_tensor(pe, m, ps, c, 1)
        if c == 0:
            chunk_turn_tensor(pe, m, ps, ident, c)
    out_mlstm_tensor(pe, m, ps, m.T - 1, 0)


def chunks_scalar(act, m, ps, nm, tiles, ready):
    out_weights_scalar(act, m, 1)
    for c in range(m.T):
        if c == 0:
            out_weights_scalar(act, m, 2)
        if c + 1 < m.T:
            chunk_exps_scalar(act, m, ps, c + 1)
            chunk_keys_scalar(act, m, ps, c + 1)
            att_high_scalar(act, m, c + 1)
        if c == 0:
            out_weights_scalar(act, m, 3)
        else:
            out_leave_scalar(act, m, ps, c - 1, 0)
            out_leave_scalar(act, m, ps, c - 1, 1)
        out_high_scalar(act, m, ps, c)
        if c == 0:
            tanh_scalar(act, m, 2 * HEADS_M - 1, 1)
        if c:
            if c >= 4:
                act.wait_ge(nm.summed, c - 3)
            out_sum_scalar(act, m, c - 1)
        if 3 <= c < m.T - 1:
            square_tiles(act, nm, tiles, ready, [c - 3], m.junk[:, :])


def chunks_vector(dve, m, ps, causal, nm, tiles, D, stored):
    for c in range(m.T):
        if c + 1 < m.T:
            chunk_decay_vector(dve, m, causal, c + 1)
        if c == 1:
            silu_vector(dve, m, 2 * HEADS_M - 1, 1)
        chunk_stats_vector(dve, m, ps, c, [norm_root(dve, nm, c - 4, c - 3, D)] if c >= 4 else [])
        if c + 1 < m.T:
            chunk_state_vector(dve, m, ps, c)
            chunk_weight_vector(dve, m, ps, c + 1)
            att_low_vector(dve, m, c + 1)
        if c == 0:
            conv_vector(dve, m, 2 * HEADS_M - 1, 1)
        out_low_vector(dve, m, ps, c)
        if c >= 2:
            out_scale_vector(dve, m, c - 2)
        if 4 <= c < m.T - 1:
            stored(dve, c - 4)
            scale_tile(dve, nm, c - 4, tiles[c - 4])
    out_scale_vector(dve, m, m.T - 2, norm_root(dve, nm, m.T - 4, m.T - 3, D))



def bass_hymba_layer(nc, x, positions, ff1_pre_w, ff1_w_gate, ff1_w_up, ff1_w_down, ff1_post_w,
                     mix_pre_w, w_in, conv_w, conv_b, b_igate, b_fgate, mlstm_norm_w, sinks, w_out,
                     mix_post_w, ff2_pre_w, ff2_w_gate, ff2_w_up, ff2_w_down, ff2_post_w, out):
    _, S, D = x.shape
    F = ff1_w_gate.shape[2]
    T, K = S // P, D // P
    x, out = x[0], out[0]
    row = lambda w: w.to_broadcast([P, w.shape[1]])
    by_rows = lambda w: w[0].rearrange("(k p) f -> p k f", p=P)

    with ExitStack() as ctx:
        mem = Memory(nc, ctx)
        ps = ctx.enter_context(nc.psum_tensor("ps", [P, 8, BANK], F32))
        h1 = nc.dram_tensor("after_ff1", [S, D], F32, kind="Internal").ap()
        h2 = nc.dram_tensor("after_mixer", [S, D], F32, kind="Internal").ap()
        gate_rows = nc.dram_tensor("gate_rows", [HEADS_M * T, 2, P], F32, kind="Internal").ap()

        ident = mem.at("ident", [P, P], F32, 205 * KB)
        causal = mem.at("causal", [P, P], F32, 205 * KB + 512)
        xn = [mem.at("xn_high", [P, K, S], FR, 0), mem.at("xn_low", [P, K, S], FR, 32 * KB)]
        small = 206 * KB + 512
        root = [mem.at("root_guess", [P, T], I32, small), mem.at("root_half", [P, T], F32, small + 32),
                mem.at("root_value", [P, T], F32, small + 64)]
        sums = [[mem.at(f"ssq{i}", [P, T], F32, small + 96 + 64 * i),
                 mem.at(f"rstd{i}", [P, T], F32, small + 128 + 64 * i)] + [root] for i in range(6)]

        xt = mem.at("x_tiles", [P, T, D], F32, 64 * KB)
        xs1 = [mem.at(f"norm1_xs{i}", [P, D], F32, (96 + 4 * i) * KB) for i in range(2)]
        gain1 = mem.at("norm1_gain", [P, D], F32, 104 * KB)
        junk1 = mem.at("norm1_junk", [P, D], F32, 108 * KB)
        n1 = Norm(mem, "norm1", sums[0], [xs[:, :] for xs in xs1] * (T // 2), junk1[:, :], gain1[:, :].unsqueeze(1), [4, 5, 6, 7] * (T // 2))
        x_loaded = [mem.sem(f"x_loaded{b}") for b in range(T // 2)]
        gain1_loaded = mem.sem("norm1_gain_loaded")
        set_up = mem.sem("constants_set")

        f1 = FeedForward(mem, "ff1", D, F, S, xn, True)
        f1.ssq, f1.rstd, f1.scratch = sums[1]
        f1.gains = 32
        nm = Norm(mem, "norm_mix", sums[2], [f1.y[:, k, :] for _, n in GROUPS[:-1] for k in range(n)] +
                  [x[:, :] for x in f1.res], None,
                  f1.gain_pre[:, :].unsqueeze(1), [6, 7] * T)

        m = Mixer(mem, S, D)
        m.zeros, m.consts = 2, 16 * (CONV + 1 + 2 + 3)

        h_tiles = [m.tok[:, t, 0:D] for t in range(T)]
        n2 = Norm(mem, "norm2", sums[4], h_tiles[:-1] + [m.last_res[:, :]], m.late_junk[:, :], m.gain_next,
                  [4, 5, 2, 3] * (T // 4) + [4, 5, 6, 7] * (T // 4))
        f2 = FeedForward(mem, "ff2", D, F, S, xn, False)
        f2.ssq, f2.rstd, f2.scratch = sums[5]
        f2.gains = 16

        x_tiles = [xt[:, t, :] for t in range(T)]
        block = ctx.enter_context(nc.Block())

        @block.sync
        def _(sp):
            w1, w2 = ([by_rows(g), by_rows(u)] for g, u in ((ff1_w_gate, ff1_w_up), (ff2_w_gate, ff2_w_up)))
            for half in range(2):
                for t in range(T // 2 * half, T // 2 * (half + 1)):
                    if half:
                        sp.wait_ge(n1.summed, t - T // 2 + 1)
                    sp.dma_start(xt[:, t, :], x[t * P:(t + 1) * P, :]).then_inc(x_loaded[t % (T // 2)], 16)
                gate_up_sync(sp, f1, w1, half == 0)
            down_sync(sp, f1, ff1_w_down[0])
            sp.wait_ge(f1.unit_done, (len(GROUPS) - 1) * (F // P) + 14)
            tokens_sync(sp, m, w_in[0])
            qk_sync(sp, m, w_in[0])
            out_weights_sync(sp, m, w_out[0], gate_rows)
            sp.wait_ge(m.pt_ready, 2 * T)
            sp.wait_ge(m.pv, 2 * T)
            gate_up_sync(sp, f2, w2, True)
            gate_up_sync(sp, f2, w2, False)
            down_sync(sp, f2, ff2_w_down[0])

        @block.gpsimd
        def _(pool):
            pool.dma_start(gain1[:, :], row(ff1_pre_w)).then_inc(gain1_loaded, 16)
            pool.memset(ident[:, :], 0.0).then_inc(set_up, 1)
            pool.memset(causal[:, :], 0.0).then_inc(set_up, 1)
            pool.wait_ge(set_up, 2)
            pool.affine_select(out=ident[:, :], in_=ident[:, :], compare_op=ALU.not_equal, fill=1.0,
                               base=0, pattern=[[-1, P]], channel_multiplier=1).then_inc(set_up, 1)
            pool.affine_select(out=causal[:, :], in_=causal[:, :], compare_op=ALU.is_ge, fill=-BIG,
                               base=0, pattern=[[1, P]], channel_multiplier=-1).then_inc(set_up, 1)
            with nc.allow_non_contiguous_dma(reason="a few KB of per-feature constants"):
                for j in range(CONV):
                    pool.dma_start(m.conv_w[:, j, :], conv_w[0, j].rearrange("(f p) -> p f", p=P))\
                        .then_inc(m.consts_loaded, 16)
                pool.dma_start(m.conv_b[:, :], conv_b[0].rearrange("(f p) -> p f", p=P))\
                    .then_inc(m.consts_loaded, 16)
                for e in range(2):
                    pool.dma_start(m.sink[64 * e:64 * e + 64, :],
                                   sinks.rearrange("a (j e) -> a e j", e=2)[:, e, :].to_broadcast([64, 4]))\
                        .then_inc(m.consts_loaded, 16)
            pool.wait_ge(f1.h_done, F // P)
            pool.dma_start(f1.gain_post[:, :], row(ff1_post_w)).then_inc(f1.gains_loaded, 16)
            pool.dma_start(f1.gain_pre[:, :], row(mix_pre_w)).then_inc(f1.gains_loaded, 16)
            down_pool(pool, f1, x, h1)

            pool.wait_ge(f1.unit_done, len(GROUPS) * (F // P))
            pool.dma_start(m.gain_norm[:, :], row(mlstm_norm_w.rearrange("a h d -> a (h d)")))\
                .then_inc(m.consts_loaded, 16)
            with nc.allow_non_contiguous_dma(reason="positions and gate biases"):
                pool.dma_start(m.pos_i[:, :], positions[0].rearrange("(t p) -> p t", p=P))\
                    .then_inc(m.pos_loaded, 16)
                for g, b in enumerate((b_igate, b_fgate)):
                    pool.dma_start(m.gbias[:, g, :], row(b)).then_inc(m.consts_loaded, 16)
            pool.memset(m.tok[:, :, 0:HEADS_M * NV].rearrange("p t (h e) -> p t h e", e=NV)[:, :, :, P], 1.0)\
                .then_inc(m.zeroed, 1)
            pool.memset(m.qbd[:, :, :, :], 0.0).then_inc(m.zeroed, 1)
            for i in range(T):
                shifted_values_pool(pool, m, i)
            pool.wait_ge(m.g_sb, GATE_DVE[-1])
            pool.dma_start(gate_rows, m.gout[:, :, :]).then_inc(m.g_stored, 16)
            for turn in range(len(QUARTERS)):
                out_weights_pool(pool, m, turn)
            gains = lambda w: row(w).rearrange("p (a c) -> p a c", a=2)
            pool.wait_ge(m.att_low, 2)
            pool.dma_start(m.gain_post, gains(mix_post_w)).then_inc(m.gains_loaded, 16)
            pool.wait_ge(m.g_act, GATE_ACT[-1])
            pool.wait_ge(f1.stored, 16 * T)
            for c in range(T):
                if c == 1:
                    pool.wait_ge(m.att_low, 4)
                    pool.dma_start(m.gain_next, gains(ff2_pre_w)).then_inc(m.gains_loaded, 16)
                out_residual_pool(pool, m, c, h1, h2, D)

            pool.wait_ge(m.stored, 16 * T)
            pool.wait_ge(f2.h_done, F // P)
            pool.dma_start(f2.gain_post[:, :], row(ff2_post_w)).then_inc(f2.gains_loaded, 16)
            down_pool(pool, f2, h2, out)
            pool.wait_ge(f2.stored, 16 * GROUPS[-1][0])

        @block.scalar
        def _(act):
            start_scalar(act, n1, ps, xn, x_tiles,
                         lambda e, t: e.wait_ge(x_loaded[t % (T // 2)], 16 * (t // (T // 2) + 1)), f1)
            act.wait_ge(n1.xs_ready, T)
            gate_up_scalar(act, f1, ps)
            down_scalar(act, f1, ps, nm, xn, lambda u: token_high(act, m, u))
            tokens_scalar(act, m, ps, xn, f1, nm)
            heads_scalar(act, m, ps)
            h_ready = lambda e, t: (e.wait_ge(m.h_done, t + 1), e.wait_ge(m.y_summed, min(t + 3, T)))
            chunks_scalar(act, m, ps, n2, h_tiles, h_ready)

            def last_projection():
                for n in range(2):
                    out_leave_scalar(act, m, ps, T - 1, n)
                act.wait_ge(n2.summed, T - 3)
                out_sum_scalar(act, m, T - 1)

            resume_scalar(act, n2, ps, xn, h_tiles, h_ready, f2, T, lambda e: e.wait_ge(m.h_done, T - 1),
                          last_projection)
            act.wait_ge(m.stored, 16 * T)
            gate_up_scalar(act, f2, ps)
            down_scalar(act, f2, ps, None, xn)
            last_stores(act, f2, out)
            act.wait_ge(f2.last_stored, 32 * GROUPS[-1][1])

        @block.vector
        def _(dve):
            start_vector(dve, n1, ps, xn, x_tiles, lambda e: e.wait_ge(gain1_loaded, 16), D, f1)
            gate_up_vector(dve, f1, ps)
            down_vector(dve, f1, ps, nm, xn, D, 0.5, lambda u: token_low(dve, m, u))
            tokens_vector(dve, m, ps, xn, f1, nm, D)
            dve.wait_ge(f1.stored, 16 * T)
            m.chain.then(dve, dve.memset(m.xp[:, 0:3], 0.0))
            dve.wait_ge(set_up, 4)
            heads_vector(dve, m, ps, causal)
            stored = lambda e, t: (e.wait_ge(m.stored, 16 * (t + 1)), e.wait_ge(m.gains_loaded, 32))
            chunks_vector(dve, m, ps, causal, n2, h_tiles, D, stored)
            resume_vector(dve, n2, ps, xn, h_tiles, D, f2, T, stored,
                          lambda root: (out_scale_vector(dve, m, T - 1, root), last_residual_vector(dve, m, D)))
            gate_up_vector(dve, f2, ps)
            down_vector(dve, f2, ps, None, xn, D, 0.5)

        @block.tensor
        def _(pe):
            pe.wait_ge(set_up, 4)
            start_tensor(pe, n1, ps, ident, f1, xn, T, K)
            gate_up_tensor(pe, f1, ps, xn)
            down_tensor(pe, f1, ps, nm, ident)
            tokens_tensor(pe, m, ps, xn, f1, nm, ident)
            heads_tensor(pe, m, ps, xn, ident, m.gout[:, 0, :])
            chunks_tensor(pe, m, ps, ident)
            for t in range(2):
                turn_tile(pe, n2, ps, ident, t, K)
            out_mlstm_tensor(pe, m, ps, T - 1, 1)
            start_tensor(pe, n2, ps, ident, f2, xn, T, K, 2)
            gate_up_tensor(pe, f2, ps, xn)
            down_tensor(pe, f2, ps, None, ident)


_INS = ['x', 'positions', 'ff1_pre_w', 'ff1_w_gate', 'ff1_w_up', 'ff1_w_down', 'ff1_post_w', 'mix_pre_w',
        'w_in', 'conv_w', 'conv_b', 'b_igate', 'b_fgate', 'mlstm_norm_w', 'sinks', 'w_out', 'mix_post_w',
        'ff2_pre_w', 'ff2_w_gate', 'ff2_w_up', 'ff2_w_down', 'ff2_post_w']


def kernel(**inputs):
    import numpy as _np
    import concourse.bacc as _bacc
    from concourse import mybir as _mybir
    from concourse.bass_utils import run_bass_kernel_spmd as _run

    nc = _bacc.Bacc("TRN2", target_bir_lowering=False, num_devices=1)
    arrays, args = {}, []
    for name in _INS:
        a = _np.ascontiguousarray(inputs[name])
        arrays[f"in_{name}_dram"] = a
        args.append(nc.dram_tensor(f"in_{name}_dram", a.shape, _mybir.dt.from_np(a.dtype), kind="ExternalInput").ap())
    out = nc.dram_tensor("out_dram", inputs["x"].shape, _mybir.dt.float32, kind="ExternalOutput").ap()
    bass_hymba_layer(nc, *args, out)
    r = _run(nc, [arrays], core_ids=[0])
    return r.results[0]["out_dram"]
```
